# Optimizing a Trainium2 kernel written in Bass

```python
import jax
import jax.numpy as jnp
from jax import lax
import numpy as np
import jax, jax.numpy as jnp

D_MODEL = 1024
BATCH = 1
SEQ = 512
DEPTH = 2

HEAD_DIM = 64
RET_HEADS = 4
DSA_HEADS = 4
DIL_HEADS = 8
RET_W = RET_HEADS * HEAD_DIM
DSA_W = DSA_HEADS * HEAD_DIM
DIL_W = DIL_HEADS * HEAD_DIM
D_MIX = RET_W + DSA_W + DIL_W
RET_CHUNK = 128
RET_ROPE_BASE = 10000.0
KV_LATENT = 128
IDX_HEADS = 8
IDX_DIM = 64
TOPK_MAX = 256
QUERY_BLOCK = 128
DIL_PATTERNS = ((128, 1), (512, 4), (2048, 16))
D_FF = 4 * D_MODEL
NORM_EPS = 1e-6
RET_COLS = 4 * RET_W
DSA_SIZES = (DSA_W, KV_LATENT, IDX_HEADS * IDX_DIM, IDX_DIM, IDX_HEADS)
DSA_COLS = sum(DSA_SIZES)
DIL_COLS = 3 * DIL_W
N_IN = RET_COLS + DSA_COLS + DIL_COLS


def _offsets(sizes):
    return [int(o) for o in np.cumsum(sizes)[:-1]]

def rms_norm(x, w):
    xf = x.astype(jnp.float32)
    y = xf * lax.rsqrt(jnp.mean(xf * xf, axis=-1, keepdims=True) + NORM_EPS)
    return (y * w.astype(jnp.float32)).astype(x.dtype)

def rotary(x, pos):
    half = x.shape[-1] // 2
    inv = RET_ROPE_BASE ** (-jnp.arange(half, dtype=jnp.float32) / half)
    ang = pos.astype(jnp.float32)[:, None] * inv[None, :]
    cos = jnp.cos(ang)[None, :, None, :]
    sin = jnp.sin(ang)[None, :, None, :]
    xf = x.astype(jnp.float32)
    x1, x2 = xf[..., :half], xf[..., half:]
    return jnp.concatenate([x1 * cos - x2 * sin, x2 * cos + x1 * sin], axis=-1)

def retention_chunkwise(q, k, v):
    B, S, H, d = q.shape
    C = RET_CHUNK
    N = S // C
    log_g = jnp.log(1.0 - 2.0 ** (-5.0 - jnp.arange(H, dtype=jnp.float32)))

    def chunks(t):
        return t.reshape(B, N, C, H, d).transpose(0, 3, 1, 2, 4)

    qc, kc, vc = chunks(q), chunks(k * (d ** -0.5)), chunks(v)
    i = jnp.arange(C, dtype=jnp.float32)
    diff = i[:, None] - i[None, :]
    decay = jnp.exp(jnp.maximum(diff, 0.0)[None] * log_g[:, None, None]) * (diff >= 0)[None]
    inner = jnp.einsum('bhncd,bhnmd->bhncm', qc, kc) * decay[None, :, None]
    inner = jnp.einsum('bhncm,bhnme->bhnce', inner, vc)
    zeta = jnp.exp((C - 1.0 - i)[None, :] * log_g[:, None])
    xi = jnp.exp((i + 1.0)[None, :] * log_g[:, None])
    kv = jnp.einsum('bhnmd,bhnme->nbhde', kc * zeta[None, :, None, :, None], vc)
    g_chunk = jnp.exp(C * log_g)[None, :, None, None]

    def step(state, kv_n):
        return g_chunk * state + kv_n, state

    _, state_prev = lax.scan(step, jnp.zeros((B, H, d, d), jnp.float32), kv)
    cross = jnp.einsum('bhncd,nbhde->bhnce', qc, state_prev) * xi[None, :, None, :, None]
    o = inner + cross
    return o.transpose(0, 2, 3, 1, 4).reshape(B, S, H, d)

def retention_mixer(cols, norm_w, pos):
    B, S, _ = cols.shape
    q, k, v, g = jnp.split(cols, 4, axis=-1)
    shp = (B, S, RET_HEADS, HEAD_DIM)
    o = retention_chunkwise(rotary(q.reshape(shp), pos), rotary(k.reshape(shp), pos),
                            v.reshape(shp).astype(jnp.float32))
    mu = jnp.mean(o, axis=-1, keepdims=True)
    var = jnp.mean(jnp.square(o - mu), axis=-1, keepdims=True)
    o = (o - mu) * lax.rsqrt(var + NORM_EPS) * norm_w.astype(jnp.float32)
    o = o.reshape(B, S, RET_W)
    return (jax.nn.silu(g.astype(jnp.float32)) * o).astype(cols.dtype)

def dsa_mixer(cols, kv_norm_w, w_uk, w_uv):
    B, S, _ = cols.shape
    q, c_kv, q_idx, k_idx, w_idx = jnp.split(cols, _offsets(DSA_SIZES), axis=-1)
    q = q.reshape(B, S, DSA_HEADS, HEAD_DIM)
    c_kv = rms_norm(c_kv, kv_norm_w)
    k = (c_kv @ w_uk).reshape(B, S, DSA_HEADS, HEAD_DIM)
    v = (c_kv @ w_uv).reshape(B, S, DSA_HEADS, HEAD_DIM)
    q_idx = q_idx.reshape(B, S, IDX_HEADS, IDX_DIM)
    w_idx = w_idx * (IDX_HEADS ** -0.5 * IDX_DIM ** -0.5)
    n_sel = min(TOPK_MAX, S // 4)
    nblk = S // QUERY_BLOCK
    key_pos = jnp.arange(S)

    def to_blocks(t):
        return jnp.moveaxis(t.reshape((B, nblk, QUERY_BLOCK) + t.shape[2:]), 1, 0)

    def block(args):
        qb, qib, wb, start = args
        qpos = start + jnp.arange(QUERY_BLOCK)
        logits = jnp.einsum('bqhd,bsd->bqhs', qib, k_idx)
        score = jnp.einsum('bqhs,bqh->bqs', jax.nn.relu(logits), wb).astype(jnp.float32)
        causal = key_pos[None, :] <= qpos[:, None]
        score = jnp.where(causal[None], score, -jnp.inf)
        _, idx = lax.top_k(score, n_sel)
        k_sel = jax.vmap(lambda kb, ib: kb[ib])(k, idx)
        v_sel = jax.vmap(lambda vb, ib: vb[ib])(v, idx)
        s = jnp.einsum('bqhd,bqnhd->bhqn', qb, k_sel).astype(jnp.float32) * (HEAD_DIM ** -0.5)
        valid = (idx <= qpos[None, :, None])[:, None]
        p = jax.nn.softmax(jnp.where(valid, s, -jnp.inf), axis=-1).astype(v.dtype)
        return jnp.einsum('bhqn,bqnhd->bqhd', p, v_sel)

    starts = jnp.arange(nblk) * QUERY_BLOCK
    o = lax.map(block, (to_blocks(q), to_blocks(q_idx), to_blocks(w_idx), starts))
    return jnp.moveaxis(o, 0, 1).reshape(B, S, DSA_W).astype(cols.dtype)

def dilated_branch(q, k, v, window, dilation):
    B, S, H, d = q.shape
    steps = window // dilation
    n = S // dilation
    lb = min(steps, n)
    nb = -(-n // lb)
    pad = nb * lb - n

    def to_sub(t):
        t = t.reshape(B, n, dilation, H, d).transpose(0, 2, 3, 1, 4)
        t = jnp.pad(t, ((0, 0), (0, 0), (0, 0), (0, pad), (0, 0)))
        return t.reshape(B, dilation, H, nb, lb, d)

    def with_prev(t):
        prev = jnp.pad(t, ((0, 0), (0, 0), (0, 0), (1, 0), (0, 0), (0, 0)))[:, :, :, :-1]
        return jnp.concatenate([prev, t], axis=4)

    qs = to_sub(q)
    kk = with_prev(to_sub(k))
    vv = with_prev(to_sub(v)).astype(jnp.float32)
    qi = jnp.arange(lb)[:, None]
    kj = jnp.arange(2 * lb)[None, :]
    dist = lb + qi - kj
    key_idx = jnp.arange(nb)[:, None, None] * lb - lb + kj[None]
    mask = (dist >= 0) & (dist <= steps) & (key_idx >= 0)
    s = jnp.einsum('brhnqd,brhnkd->brhnqk', qs, kk).astype(jnp.float32) * (d ** -0.5)
    s = jnp.where(mask, s, -jnp.inf)
    m = jnp.max(s, axis=-1, keepdims=True)
    p = jnp.exp(s - m)
    den = jnp.sum(p, axis=-1, keepdims=True)
    o = jnp.einsum('brhnqk,brhnkd->brhnqd', p, vv) / den
    lse = (m + jnp.log(den))[..., 0]
    o = o.reshape(B, dilation, H, nb * lb, d)[:, :, :, :n].transpose(0, 3, 1, 2, 4).reshape(B, S, H, d)
    lse = lse.reshape(B, dilation, H, nb * lb)[:, :, :, :n].transpose(0, 3, 1, 2).reshape(B, S, H)
    return o, lse

def dilated_mixer(cols):
    B, S, _ = cols.shape
    q, k, v = jnp.split(cols, 3, axis=-1)
    shp = (B, S, DIL_HEADS, HEAD_DIM)
    q, k, v = q.reshape(shp), k.reshape(shp), v.reshape(shp)
    outs = []
    lses = []
    for window, dilation in DIL_PATTERNS:
        o, lse = dilated_branch(q, k, v, window, dilation)
        outs.append(o)
        lses.append(lse)
    alpha = jax.nn.softmax(jnp.stack(lses, axis=0), axis=0)
    o = jnp.sum(alpha[..., None] * jnp.stack(outs, axis=0), axis=0)
    return o.reshape(B, S, DIL_W).astype(cols.dtype)

def hybrid_layer(x, attn_norm_w, w_in, ret_norm_w, kv_norm_w, w_uk, w_uv, w_out, mlp_norm_w, w_up, w_down, pos):
    h = rms_norm(x, attn_norm_w)
    proj = h @ w_in
    ret_cols, dsa_cols, dil_cols = jnp.split(proj, _offsets((RET_COLS, DSA_COLS, DIL_COLS)), axis=-1)
    mixed = jnp.concatenate([retention_mixer(ret_cols, ret_norm_w, pos),
                             dsa_mixer(dsa_cols, kv_norm_w, w_uk, w_uv),
                             dilated_mixer(dil_cols)], axis=-1)
    x = x + mixed @ w_out
    h = rms_norm(x, mlp_norm_w)
    return x + jnp.square(jax.nn.relu(h @ w_up)) @ w_down

def first_inputs(seed: int = 0) -> dict:
    key = jax.random.key(seed)
    ks = jax.random.split(key, 12)
    f32 = jnp.float32

    def nrm(k, shape, scale):
        return jax.random.normal(k, shape, f32) * scale

    return {
        'x': nrm(ks[0], (BATCH, SEQ, D_MODEL), 1.0),
        'attn_norm_w': 1.0 + nrm(ks[1], (DEPTH, D_MODEL), 0.02),
        'w_in': nrm(ks[2], (DEPTH, D_MODEL, N_IN), D_MODEL ** -0.5),
        'ret_norm_w': 1.0 + nrm(ks[3], (DEPTH, RET_HEADS, HEAD_DIM), 0.02),
        'dsa_kv_norm_w': 1.0 + nrm(ks[4], (DEPTH, KV_LATENT), 0.02),
        'dsa_w_uk': nrm(ks[5], (DEPTH, KV_LATENT, DSA_W), KV_LATENT ** -0.5),
        'dsa_w_uv': nrm(ks[6], (DEPTH, KV_LATENT, DSA_W), KV_LATENT ** -0.5),
        'w_out': nrm(ks[7], (DEPTH, D_MIX, D_MODEL), D_MIX ** -0.5),
        'mlp_norm_w': 1.0 + nrm(ks[8], (DEPTH, D_MODEL), 0.02),
        'w_up': nrm(ks[9], (DEPTH, D_MODEL, D_FF), D_MODEL ** -0.5),
        'w_down': nrm(ks[10], (DEPTH, D_FF, D_MODEL), D_FF ** -0.5),
        'final_norm_w': 1.0 + nrm(ks[11], (D_MODEL,), 0.02),
    }

def first_block(x, attn_norm_w, w_in, ret_norm_w, dsa_kv_norm_w, dsa_w_uk, dsa_w_uv, w_out, mlp_norm_w, w_up, w_down, final_norm_w):
    pos = jnp.arange(x.shape[1])
    for layer in range(DEPTH):
        x = hybrid_layer(x, attn_norm_w[layer], w_in[layer], ret_norm_w[layer], dsa_kv_norm_w[layer],
                         dsa_w_uk[layer], dsa_w_uv[layer], w_out[layer], mlp_norm_w[layer],
                         w_up[layer], w_down[layer], pos)
    return rms_norm(x, final_norm_w)


CHUNK = 64
Q_BLOCK = 128
FOX_HEADS = 8
FOX_HEAD_DIM = 64
FOX_WIDTH = FOX_HEADS * FOX_HEAD_DIM
POOL_WINDOWS = (2, 4, 8, 16)
POOL_GROUPS = len(POOL_WINDOWS)
POOL_WIDTH = D_MODEL - FOX_WIDTH
POOL_GROUP_DIM = POOL_WIDTH // POOL_GROUPS
EVEN_IN_WIDTH = 3 * FOX_WIDTH + FOX_HEADS + POOL_WIDTH
LRU_WIDTH = D_MODEL
LRU_HEADS = 4
LRU_HEAD_DIM = LRU_WIDTH // LRU_HEADS
CONV_WIDTH = 4
LRU_C = 8.0
D_FF_2 = -(-8 * D_MODEL // (3 * 256)) * 256
RMS_EPS = 1e-6


def rmsnorm(x, g):
    xf = x.astype(jnp.float32)
    y = xf * lax.rsqrt(jnp.mean(xf * xf, axis=-1, keepdims=True) + RMS_EPS)
    return (y * g.astype(jnp.float32)).astype(x.dtype)

def swiglu(h, w_gate, w_up, w_down):
    return (jax.nn.silu(h @ w_gate) * (h @ w_up)) @ w_down

def forgetting_attention(q, k, v, log_f):
    B, S, H, Dh = q.shape
    n_blk = S // Q_BLOCK
    scale = Dh ** -0.5
    c = jnp.cumsum(log_f, axis=1).transpose(0, 2, 1)
    q_blocks = q.reshape(B, n_blk, Q_BLOCK, H, Dh).transpose(1, 0, 3, 2, 4)
    c_blocks = c.reshape(B, H, n_blk, Q_BLOCK).transpose(2, 0, 1, 3)
    k_pos = jnp.arange(S, dtype=jnp.int32)

    def one_block(args):
        qb, cb, i = args
        s = jnp.einsum('bhqd,bshd->bhqs', qb, k, preferred_element_type=jnp.float32)
        s = s * scale + cb[..., None] - c[:, :, None, :]
        q_pos = i * Q_BLOCK + jnp.arange(Q_BLOCK, dtype=jnp.int32)
        mask = k_pos[None, :] <= q_pos[:, None]
        s = jnp.where(mask, s, -jnp.inf)
        p = jax.nn.softmax(s, axis=-1)
        return jnp.einsum('bhqs,bshd->bqhd', p.astype(v.dtype), v)

    out = lax.map(one_block, (q_blocks, c_blocks, jnp.arange(n_blk, dtype=jnp.int32)))
    return out.transpose(1, 0, 2, 3, 4).reshape(B, S, H * Dh)

def multiscale_pool(u, pool_w, pool_scale):
    B, S, _ = u.shape
    uf = u.astype(jnp.float32).reshape(B, S, POOL_GROUPS, POOL_GROUP_DIM)
    cs = jnp.cumsum(uf, axis=1)
    t1 = jnp.arange(1, S + 1, dtype=jnp.float32)
    pooled = []
    for g, w in enumerate(POOL_WINDOWS):
        cg = cs[:, :, g]
        lagged = jnp.pad(cg, ((0, 0), (w, 0), (0, 0)))[:, :S]
        mean = (cg - lagged) / jnp.minimum(t1, float(w))[None, :, None]
        pooled.append(mean - uf[:, :, g])
    pooled = jnp.stack(pooled, axis=2)
    mixed = jnp.einsum('bsgd,gde->bsge', pooled, pool_w.astype(jnp.float32))
    return (mixed.reshape(B, S, POOL_WIDTH) * pool_scale.astype(jnp.float32)).astype(u.dtype)

def even_mixer(h, w_in, b_f, pool_w, pool_scale, w_out):
    B, S, _ = h.shape
    proj = h @ w_in
    q, k, v, f_logit, u = jnp.split(
        proj, [FOX_WIDTH, 2 * FOX_WIDTH, 3 * FOX_WIDTH, 3 * FOX_WIDTH + FOX_HEADS], axis=-1)
    q = q.reshape(B, S, FOX_HEADS, FOX_HEAD_DIM)
    k = k.reshape(B, S, FOX_HEADS, FOX_HEAD_DIM)
    v = v.reshape(B, S, FOX_HEADS, FOX_HEAD_DIM)
    log_f = jax.nn.log_sigmoid(f_logit.astype(jnp.float32) + b_f.astype(jnp.float32))
    attn = forgetting_attention(q, k, v, log_f)
    pool = multiscale_pool(u, pool_w, pool_scale)
    return jnp.concatenate([attn, pool.astype(attn.dtype)], axis=-1) @ w_out

def causal_depthwise_conv(x, conv_w, conv_b):
    C = x.shape[-1]
    y = lax.conv_general_dilated(
        x, conv_w[:, None, :], window_strides=(1,), padding=[(CONV_WIDTH - 1, 0)],
        dimension_numbers=('NWC', 'WIO', 'NWC'), feature_group_count=C)
    return y + conv_b

def rg_lru(x, w_a, b_a, w_x, b_x, lam):
    B, S, W = x.shape
    xf = x.astype(jnp.float32)
    xh = xf.reshape(B, S, LRU_HEADS, LRU_HEAD_DIM)
    r = jax.nn.sigmoid(jnp.einsum('bshd,hde->bshe', xh, w_a.astype(jnp.float32)).reshape(B, S, W)
                       + b_a.astype(jnp.float32))
    i = jax.nn.sigmoid(jnp.einsum('bshd,hde->bshe', xh, w_x.astype(jnp.float32)).reshape(B, S, W)
                       + b_x.astype(jnp.float32))
    log_a = -LRU_C * r * jax.nn.softplus(-lam.astype(jnp.float32))
    a = jnp.exp(log_a)
    b = jnp.sqrt(-jnp.expm1(2.0 * log_a)) * (i * xf)

    def combine(c1, c2):
        a1, b1 = c1
        a2, b2 = c2
        return a1 * a2, a2 * b1 + b2

    _, hs = lax.associative_scan(combine, (a, b), axis=1)
    return hs.astype(x.dtype)

def odd_mixer(h, w_in, conv_w, conv_b, w_a, b_a, w_x, b_x, lam, w_out):
    proj = h @ w_in
    gate, xr = jnp.split(proj, 2, axis=-1)
    xr = causal_depthwise_conv(xr, conv_w, conv_b)
    y = rg_lru(xr, w_a, b_a, w_x, b_x, lam)
    return (jax.nn.gelu(gate) * y) @ w_out

def second_inputs(seed: int = 0) -> dict:
    key = jax.random.key(seed)
    ks = jax.random.split(key, 32)
    f32 = jnp.float32
    ne = (DEPTH + 1) // 2
    no = DEPTH // 2

    def nrm(k, shape, scale):
        return jax.random.normal(k, shape, f32) * scale

    def gain(k, shape):
        return 1.0 + 0.05 * jax.random.normal(k, shape, f32)

    u = jax.random.uniform(ks[24], (no, LRU_WIDTH), f32, minval=0.9, maxval=0.999)
    s = u ** (1.0 / LRU_C)
    lam = jnp.log(s) - jnp.log1p(-s)
    return {
        "x": jax.random.normal(ks[0], (BATCH, SEQ, D_MODEL), f32),
        "mix_pre_g": gain(ks[1], (DEPTH, D_MODEL)),
        "mix_post_g": gain(ks[2], (DEPTH, D_MODEL)),
        "ffn_pre_g": gain(ks[3], (DEPTH, D_MODEL)),
        "ffn_post_g": gain(ks[4], (DEPTH, D_MODEL)),
        "ffn_w_gate": nrm(ks[5], (DEPTH, D_MODEL, D_FF_2), D_MODEL ** -0.5),
        "ffn_w_up": nrm(ks[6], (DEPTH, D_MODEL, D_FF_2), D_MODEL ** -0.5),
        "ffn_w_down": nrm(ks[7], (DEPTH, D_FF_2, D_MODEL), D_FF_2 ** -0.5),
        "ev_w_in": nrm(ks[8], (ne, D_MODEL, EVEN_IN_WIDTH), D_MODEL ** -0.5),
        "ev_b_f": jax.random.uniform(ks[9], (ne, FOX_HEADS), f32, minval=1.0, maxval=6.0),
        "ev_pool_w": nrm(ks[10], (ne, POOL_GROUPS, POOL_GROUP_DIM, POOL_GROUP_DIM), POOL_GROUP_DIM ** -0.5),
        "ev_pool_scale": 1.0 + 0.1 * jax.random.normal(ks[11], (ne, POOL_WIDTH), f32),
        "ev_w_out": nrm(ks[12], (ne, D_MODEL, D_MODEL), D_MODEL ** -0.5),
        "od_w_in": nrm(ks[13], (no, D_MODEL, 2 * LRU_WIDTH), D_MODEL ** -0.5),
        "od_conv_w": nrm(ks[14], (no, CONV_WIDTH, LRU_WIDTH), CONV_WIDTH ** -0.5),
        "od_conv_b": nrm(ks[15], (no, LRU_WIDTH), 0.01),
        "od_w_a": nrm(ks[16], (no, LRU_HEADS, LRU_HEAD_DIM, LRU_HEAD_DIM), LRU_HEAD_DIM ** -0.5),
        "od_b_a": nrm(ks[17], (no, LRU_WIDTH), 0.01),
        "od_w_x": nrm(ks[18], (no, LRU_HEADS, LRU_HEAD_DIM, LRU_HEAD_DIM), LRU_HEAD_DIM ** -0.5),
        "od_b_x": nrm(ks[19], (no, LRU_WIDTH), 0.01),
        "od_lam": lam,
        "od_w_out": nrm(ks[20], (no, LRU_WIDTH, D_MODEL), LRU_WIDTH ** -0.5),
    }

def second_block(x, mix_pre_g, mix_post_g, ffn_pre_g, ffn_post_g, ffn_w_gate, ffn_w_up, ffn_w_down,
              ev_w_in, ev_b_f, ev_pool_w, ev_pool_scale, ev_w_out,
              od_w_in, od_conv_w, od_conv_b, od_w_a, od_b_a, od_w_x, od_b_x, od_lam, od_w_out):
    for layer in range(DEPTH):
        h = rmsnorm(x, mix_pre_g[layer])
        if layer % 2 == 0:
            e = layer // 2
            m = even_mixer(h, ev_w_in[e], ev_b_f[e], ev_pool_w[e], ev_pool_scale[e], ev_w_out[e])
        else:
            o = layer // 2
            m = odd_mixer(h, od_w_in[o], od_conv_w[o], od_conv_b[o], od_w_a[o], od_b_a[o],
                          od_w_x[o], od_b_x[o], od_lam[o], od_w_out[o])
        x = x + rmsnorm(m, mix_post_g[layer])
        h = rmsnorm(x, ffn_pre_g[layer])
        x = x + rmsnorm(swiglu(h, ffn_w_gate[layer], ffn_w_up[layer], ffn_w_down[layer]), ffn_post_g[layer])
    return x


def setup_inputs(seed=0):
    out = dict(first_inputs(seed))
    for name, value in second_inputs(seed + 1).items():
        if name != "x":
            out[name + "_2"] = value
    return out


def reference(
    x, attn_norm_w, w_in, ret_norm_w, dsa_kv_norm_w, dsa_w_uk, dsa_w_uv, w_out, mlp_norm_w,
    w_up, w_down, final_norm_w, mix_pre_g_2, mix_post_g_2, ffn_pre_g_2, ffn_post_g_2,
    ffn_w_gate_2, ffn_w_up_2, ffn_w_down_2, ev_w_in_2, ev_b_f_2, ev_pool_w_2, ev_pool_scale_2,
    ev_w_out_2, od_w_in_2, od_conv_w_2, od_conv_b_2, od_w_a_2, od_b_a_2, od_w_x_2, od_b_x_2,
    od_lam_2, od_w_out_2,
):
    x = first_block(
        x, attn_norm_w, w_in, ret_norm_w, dsa_kv_norm_w, dsa_w_uk, dsa_w_uv, w_out, mlp_norm_w,
        w_up, w_down, final_norm_w,
    )
    return second_block(
        x, mix_pre_g_2, mix_post_g_2, ffn_pre_g_2, ffn_post_g_2, ffn_w_gate_2, ffn_w_up_2,
        ffn_w_down_2, ev_w_in_2, ev_b_f_2, ev_pool_w_2, ev_pool_scale_2, ev_w_out_2, od_w_in_2,
        od_conv_w_2, od_conv_b_2, od_w_a_2, od_b_a_2, od_w_x_2, od_b_x_2, od_lam_2, od_w_out_2,
    )


_drawn_inputs = setup_inputs


def setup_inputs(seed=0):
    import zlib

    import numpy as np

    out = dict(_drawn_inputs(seed))
    spreads = {}
    factors = {'ret_norm_w': 5.451,
     'dsa_kv_norm_w': 8.0,
     'od_conv_b_2': 3.669,
     'od_b_a_2': 56.383,
     'od_b_x_2': 23.049}
    for name, (base, spread) in spreads.items():
        noise = np.random.default_rng([zlib.crc32(name.encode()), seed]).standard_normal(out[name].shape)
        drawn = base * np.exp(spread * noise) if base else spread * noise
        out[name] = jnp.asarray(drawn.astype(out[name].dtype))
    for name, factor in factors.items():
        out[name] = (out[name] * factor).astype(out[name].dtype)
    return out
```

```python
from contextlib import ExitStack

import numpy as np
import concourse.bass as bass
from concourse import mybir

F32 = mybir.dt.float32
F32R = mybir.dt.float32r
ALU = mybir.AluOpType
ACT = mybir.ActivationFunctionType

P = 128
S = 512
TB = S // P
D = 1024
DB = D // P
HD = 64
DEPTH = 2
DEPTH2 = 2
RET_H, DSA_H, DIL_H, FOX_H, IDX_H = 4, 4, 8, 8, 8
TOPK = min(256, S // 4)
D_FF = 4096
D_FF2 = 2816
POOL_W = (2, 4, 8, 16)
EPS = 1e-6
LRU_C = 8.0
SCALE = HD ** -0.5
NEG = -1e30
TAKEN = -3e38
C_RET, C_DSA = 0, 1024
C_DSAQ, C_CKV, C_QIDX, C_KIDX, C_WIDX = 1024, 1280, 1408, 1920, 1984
C_DIL = 1992
N_IN = 3528
KT = 4
RING = 2
BANKS = 8
HALF = 4

T_IDENT, T_ONES, T_MEAN, T_ROT, T_LOGC, T_CAUSAL, T_POOL = 0, 128, 256, 384, 512, 1024, 1536
T_SHARED = 1600
T_COS, T_SIN, T_DECAY = 0, 512, 1024
T_RET = 1024 + RET_H * S


def shape_tables():
    f = np.float32
    q = np.arange(P)[:, None]
    t = np.zeros((P, T_SHARED), f)
    t[:, T_IDENT:T_IDENT + P] = np.eye(P)
    t[:, T_ONES:T_ONES + P] = 1.0
    half = (np.arange(P)[:, None] // HD) == (np.arange(P)[None] // HD)
    t[:, T_MEAN:T_MEAN + P] = half / HD
    for m in range(P):
        if m % HD < HD // 2:
            t[m + HD // 2, T_ROT + m] = -1.0
        else:
            t[m - HD // 2, T_ROT + m] = 1.0
    dist = q - (np.arange(S)[None] - (S - P))
    count = ((dist >= 0) & (dist <= 128)).astype(int)
    for dil, in ((4,), (16,)):
        count = count + ((dist >= 0) & (dist % dil == 0)).astype(int)
    t[:, T_LOGC:T_LOGC + S] = np.where(count > 0, np.log(np.maximum(count, 1)) / SCALE, NEG)
    t[:, T_CAUSAL:T_CAUSAL + S] = np.where(dist >= 0, 0.0, NEG)
    for g, w in enumerate(POOL_W):
        t[:, T_POOL + 16 * g:T_POOL + 16 * g + 16] = 1.0 / np.minimum(np.arange(16) + 1, w)
    r = np.zeros((P, T_RET), f)
    inv = (f(10000.0) ** (-np.arange(HD // 2, dtype=f) / f(HD // 2))).astype(f)
    ang = np.arange(S, dtype=f)[None] * inv[np.arange(P) % (HD // 2)][:, None]
    r[:, T_COS:T_COS + S] = np.cos(ang.astype(np.float64))
    r[:, T_SIN:T_SIN + S] = np.sin(ang.astype(np.float64))
    diff = np.arange(S)[None] - q
    for h in range(RET_H):
        lg = np.log(1.0 - 2.0 ** (-5.0 - h))
        r[:, T_DECAY + h * S:T_DECAY + (h + 1) * S] = np.where(diff >= 0, np.exp(diff * lg), 0.0) * SCALE
    sel = np.zeros((FOX_H, FOX_H * P), f)
    for h in range(FOX_H):
        sel[h, h * P:(h + 1) * P] = 1.0
    return t, r, sel


class Signal:

    def __init__(self, sem):
        self.sem = sem
        self.n = 0

    def by(self, ins, k=1):
        ins.then_inc(self.sem, k)
        self.n += k
        return ins


def build(nc, a, out):
    ctx = ExitStack()
    with ctx:
        at = [16512]

        def place(name, shape, dt=F32, where=None):
            size = int(np.prod(shape[1:])) * 4
            off = where
            if where is None:
                off = at[0]
                at[0] += -(-size // 32) * 32
                assert at[0] <= 229368, (name, at[0])
            t = nc.alloc_sbuf_tensor_at(name, shape, dt, offset=off)
            t_off[name] = off
            return t

        t_off = {}
        x = place("x", [P, DB, S])
        h_hi, h_lo = place("h_hi", [P, DB, S], F32R), place("h_lo", [P, DB, S], F32R)
        hid_hi, hid_lo = place("hid_hi", [P, DB, S], F32R), place("hid_lo", [P, DB, S], F32R)
        raw = [place(f"raw{i}", [P, KT, 512]) for i in range(RING)]
        w_hi = [place(f"w_hi{i}", [P, KT, 512], F32R) for i in range(RING)]
        w_lo = [place(f"w_lo{i}", [P, KT, 512], F32R) for i in range(RING)]
        tab = place("tab", [P, T_SHARED])
        gains = place("gains", [P, 4, DB])
        sq = [place(f"sq{i}", [P, S]) for i in range(2)]
        rstd = place("rstd", [P, S])
        tmp = [place(f"tmp{i}", [P, S]) for i in range(2)]
        stat = place("stat", [P, 4 * P])
        region = at[0]
        ident = tab[:, T_IDENT:T_IDENT + P]
        ones = tab[:, T_ONES:T_ONES + P]
        mean_m = tab[:, T_MEAN:T_MEAN + P]
        rot_m = tab[:, T_ROT:T_ROT + P]
        p_t = [place(f"p{i}", [P, S], where=t_off[f"sq{i}"]) for i in range(2)]
        pT = [place(f"pT{i}", [P, TB, P], where=t_off[f"tmp{i}"]) for i in range(2)]
        on = place("on", [P, 8, HD], where=t_off["rstd"])
        sx, sn, sd, sr = (stat[:, 0:64], stat[:, 64:128], stat[:, 128:192], stat[:, 192:256])
        xin = place("xin", [P, TB, D], where=t_off["hid_hi"])

        ps = ctx.enter_context(nc.psum_tensor("ps", [P, BANKS, 512], F32))

        names = (
            "loaded0 loaded1 hi_split lo_split slot_used bank_ready bank_free consts small "
            "sq_ready sq_used ln_done rstd_ready normed h_hi_done h_lo_done "
            "dve_link act_link relu_ready hid_hi_done hid_lo_done v_ready "
            "idx_ready idx_relu idx_used kv_up kv_out ckv_in ckv_n ret_rot ret_rotd ret_s ret_p ret_o "
            "gn_in gn_mean gn_c gn_sq gn_var gn_rstd gn_out mix_hi mix_lo g_silu "
            "s_ready s_masked nmax p_ready pT_ready pT_copied pv_done o_norm oT_ready "
            "x_T x_copied stored f_in f_c f_done pool_in pool_mm pool_out bias_ready "
            "conv_done lru_mm lru_r lru_t lru_a lru_b gelu_done y_done m_done xup").split()
        sems = {n: ctx.enter_context(nc.semaphore(n)) for n in names}
        sg = {}

        def fresh():
            for n in names:
                sg[n] = Signal(sems[n])

        class Slot:
            def __init__(self, pieces, rows):
                self.pieces, self.rows = pieces, rows
                self.width = sum(n for _, _, n in pieces)

        class Stream:

            def __init__(self):
                self.slots, self.groups = [], []
                self.need = [0, 0]
                self.landed = []

            def group(self, w, cols, tiles, r0=0):
                first = len(self.slots)
                done = 0
                for n in tiles:
                    pieces, c = [], 0
                    for (col, wid) in cols:
                        src = w[r0 + P * done:r0 + P * (done + n), col:col + wid]
                        pieces.append((src.rearrange("(k p) c -> p k c", p=P), c, wid))
                        c += wid
                    s = Slot(pieces, n)
                    r = len(self.slots) % RING
                    self.need[r] += 16 * len(pieces)
                    self.landed.append(self.need[r])
                    self.slots.append(s)
                    done += n
                self.groups.append((first, list(tiles)))

            def group_pairs(self, parts, tiles):
                first = len(self.slots)
                done = 0
                for n in tiles:
                    pieces, c = [], 0
                    for w, col, wid in parts:
                        src = w[P * done:P * (done + n), col:col + wid]
                        pieces.append((src.rearrange("(k p) c -> p k c", p=P), c, wid))
                        c += wid
                    self.need[len(self.slots) % RING] += 16 * len(pieces)
                    self.landed.append(self.need[len(self.slots) % RING])
                    self.slots.append(Slot(pieces, n))
                    done += n
                self.groups.append((first, list(tiles)))

            def used(self, s):
                for g, (first, tiles) in enumerate(self.groups):
                    if first <= s < first + len(tiles):
                        if s == first + len(tiles) - 1:
                            return "bank_ready", HALF * (g + 1)
                        before = sum(len(t) - 1 for _, t in self.groups[:g])
                        return "slot_used", before + s - first + 1

        def load_slot(sp, s, pieces, wait):
            if wait is not None:
                sp.wait_ge(sems["lo_split"], wait)
            for src, c, wid in pieces:
                sp.dma_start(raw[s % RING][:, 0:src.shape[1], c:c + wid], src).then_inc(
                    sems[f"loaded{s % RING}"], 16)

        def split_hi(act, s, rows, width, landed, used):
            act.wait_ge(sems[f"loaded{s % RING}"], landed)
            if used is not None:
                act.wait_ge(sems[used[0]], used[1])
            act.activation(w_hi[s % RING][:, 0:rows, 0:width], raw[s % RING][:, 0:rows, 0:width],
                           ACT.Copy).then_inc(sems["hi_split"], 1)

        def split_lo(pool, s, rows, width, count):
            pool.wait_ge(sems["hi_split"], count)
            pool.tensor_tensor(w_lo[s % RING][:, 0:rows, 0:width], raw[s % RING][:, 0:rows, 0:width],
                               w_hi[s % RING][:, 0:rows, 0:width].bitcast(F32),
                               ALU.subtract).then_inc(sems["lo_split"], 1)

        def stream_sp(sp, st):
            for s, slot in enumerate(st.slots):
                load_slot(sp, s, slot.pieces, s - RING + 1 if s >= RING else None)

        def stream_hi(act, st, s):
            if s < len(st.slots):
                slot = st.slots[s]
                split_hi(act, s, slot.rows, slot.width, st.landed[s], st.used(s - RING) if s >= RING else None)

        def stream_lo(pool, st):
            for s, slot in enumerate(st.slots):
                split_lo(pool, s, slot.rows, slot.width, s + 1)

        def group(pe, g, s0, tiles, blocks, act_hi, act_lo, half, k0=0):
            pe.wait_ge(sems["bank_free"], HALF * (g + 1))
            k_at = k0
            total = sum(tiles)
            nb = len({b[0] for b in blocks})
            for i, nk in enumerate(tiles):
                s = s0 + i
                r = (i + s0_ring(s0)) % RING
                pe.wait_ge(sems["lo_split"], s + 1)
                last_slot = i == len(tiles) - 1
                for m, (bank, c, n, tok, off) in enumerate(blocks):
                    for k in range(nk):
                        kk = k_at + k
                        first, last = kk == k0, kk == k0 + total - 1
                        whi, wlo = w_hi[r][:, k, c:c + n], w_lo[r][:, k, c:c + n]
                        if tok is None:
                            o = ps[0:n, half * HALF + bank, :]
                            pairs = ((whi, act_hi[:, kk, :]), (whi, act_lo[:, kk, :]), (wlo, act_hi[:, kk, :]))
                        else:
                            t0 = tok * P
                            o = ps[:, half * HALF + bank, off:off + n]
                            ahi, alo = act_hi[:, kk, t0:t0 + P], act_lo[:, kk, t0:t0 + P]
                            pairs = ((ahi, whi), (ahi, wlo), (alo, whi))
                        for j, (lh, rh) in enumerate(pairs):
                            mm = pe.matmul(o, lh, rh, start=first and j == 0 and off == 0, stop=last and j == 2,
                                           skip_group_check=True)
                    if last_slot and m == len(blocks) - 1:
                        mm.then_inc(sems["bank_ready"], HALF - nb + 1)
                    elif last_slot and blocks[m + 1][0] != bank:
                        mm.then_inc(sems["bank_ready"], 1)
                    elif not last_slot and m == len(blocks) - 1:
                        mm.then_inc(sems["slot_used"], 1)
                k_at += nk

        ring_of = [0]

        def s0_ring(s0):
            return s0 % RING if isinstance(s0, int) else ring_of[0]

        FEAT = [(b, b * P, P, None, 0) for b in range(4)]

        def stats_act(act, src, n, scale, blocks=DB, ready=None):
            for k in range(blocks):
                i = DB * n + k
                if ready is not None:
                    act.wait_ge(sems[ready[0]], ready[1] + k)
                if k >= 2:
                    act.wait_ge(sems["sq_used"], i - 1)
                sg["sq_ready"].by(act.activation(sq[k % 2][:], src(k), ACT.Square),
                                  DB - k if k == blocks - 1 else 1)
            act.wait_ge(sems["sq_used"], DB * (n + 1))
            sg["ln_done"].by(act.activation(rstd[:], ps[:, stats_bank[n], :], ACT.Ln, scale=scale, bias=eps_c))
            act.wait_ge(sems["ln_done"], sg["ln_done"].n)
            sg["rstd_ready"].by(act.activation(rstd[:], rstd[:], ACT.Exp, scale=-0.5))

        stats_bank = {}

        def stats_pe(pe, n, bank, blocks=DB):
            stats_bank[n] = bank
            for k in range(blocks):
                pe.wait_ge(sems["sq_ready"], DB * n + k + 1)
                pe.matmul(ps[:, bank, :], ones, sq[k % 2][:], start=k == 0, stop=k == blocks - 1,
                          skip_group_check=True).then_inc(sems["sq_used"], DB - k if k == blocks - 1 else 1)

        def norm_split_dve(dve, gain, n, m):
            dve.wait_ge(sems["rstd_ready"], n + 1)
            for k in range(DB):
                i = DB * m + k
                if k >= 2:
                    dve.wait_ge(sems["h_lo_done"], i - 1)
                sg["normed"].by(dve.scalar_tensor_tensor(out=tmp[k % 2][:], in0=x[:, k, :], scalar=gain(k),
                                                         in1=rstd[:], op0=ALU.mult, op1=ALU.mult))
                dve.wait_ge(sems["h_hi_done"], i + 1)
                sg["h_lo_done"].by(dve.tensor_tensor(h_lo[:, k, :], tmp[k % 2][:], h_hi[:, k, :].bitcast(F32),
                                                     ALU.subtract))

        def norm_split_act(act, m):
            for k in range(DB):
                act.wait_ge(sems["normed"], DB * m + k + 1)
                sg["h_hi_done"].by(act.activation(h_hi[:, k, :], tmp[k % 2][:], ACT.Copy))

        def norm_post_dve(dve, src, gain, n, m):
            dve.wait_ge(sems["rstd_ready"], n + 1)
            for k in range(DB):
                if k >= 2:
                    dve.wait_ge(sems["xup"], DB * m + k - 1)
                link(dve, dve.scalar_tensor_tensor(out=tmp[k % 2][:], in0=src(k), scalar=gain(k),
                                                   in1=rstd[:], op0=ALU.mult, op1=ALU.mult))
                sg["xup"].by(dve.tensor_tensor(x[:, k, :], x[:, k, :], tmp[k % 2][:], ALU.add))

        def link(dve, ins):
            sg["dve_link"].by(ins)
            dve.wait_ge(sems["dve_link"], sg["dve_link"].n)

        def alink(act, ins):
            sg["act_link"].by(ins)
            act.wait_ge(sems["act_link"], sg["act_link"].n)

        class Attention:

            def __init__(self, heads, q, k, v, bias, mix0, u0, b0, decay=None):
                self.H, self.q, self.k, self.v, self.bias = heads, q, k, v, bias
                self.mix0, self.u0, self.b0, self.decay = mix0, u0, b0, decay
                self.units = [(qb, h) for qb in range(TB) for h in range(heads)]

            def scores(self, pe, i):
                qb, h = self.units[i]
                u = self.u0 + i
                n = (qb + 1) * P
                if i >= 2:
                    pe.wait_ge(sems["s_masked"], u - 1)
                p0 = HD * (h % 2)
                o = ps[:, i % 2, 0:n]
                mm = pe.matmul(o, self.q[p0:p0 + HD, h // 2, qb * P:(qb + 1) * P],
                               self.k[p0:p0 + HD, h // 2, 0:n], start=True, stop=self.decay is None)
                if self.decay is not None:
                    sel, negc = self.decay
                    mm = pe.matmul(o, sel[:, h * P:(h + 1) * P], negc[:, 0:n], start=False, stop=True)
                mm.then_inc(sems["s_ready"], 1)

            def turn(self, pe, i):
                qb, h = self.units[i]
                u = self.u0 + i
                pe.wait_ge(sems["p_ready"], u + 1)
                if i >= 2:
                    pe.wait_ge(sems["pT_copied"], u - 1)
                for kb in range(qb + 1):
                    mm = pe.transpose(ps[:, 2 + i % 2, kb * P:(kb + 1) * P], p_t[i % 2][:, kb * P:(kb + 1) * P], ident)
                mm.then_inc(sems["pT_ready"], 1)

            def values(self, pe, i):
                qb, h = self.units[i]
                u = self.u0 + i
                pe.wait_ge(sems["pT_copied"], u + 1)
                if h == 0 and qb >= 2:
                    pe.wait_ge(sems["o_norm"], self.b0 + qb - 1)
                for kb in range(qb + 1):
                    mm = pe.matmul(ps[:, 4 + qb % 2, h * HD:(h + 1) * HD], pT[i % 2][:, kb, :],
                                   self.v[:, kb, h * HD:(h + 1) * HD], start=kb == 0, stop=kb == qb,
                                   skip_group_check=True)
                mm.then_inc(sems["pv_done"], 1)

            def back(self, pe, qb):
                pe.wait_ge(sems["o_norm"], self.b0 + qb + 1)
                if qb >= 1:
                    pe.wait_ge(sems["mix_lo"], self.l0 + qb)
                for j in range(self.H // 2):
                    mm = pe.transpose(ps[:, 6, j * P:(j + 1) * P],
                                      on[:, 2 * j:2 * j + 2, :].rearrange("p a b -> p (a b)"), ident)
                mm.then_inc(sems["oT_ready"], 1)

            def tensor(self, pe, l0):
                self.l0 = l0
                n = len(self.units)
                for i in range(n + 5):
                    if i < n:
                        self.scores(pe, i)
                    if 1 <= i <= n:
                        self.turn(pe, i - 1)
                    if 2 <= i <= n + 1:
                        self.values(pe, i - 2)
                    if i >= 4 and (i - 3) % self.H == 0 and i - 4 < n:
                        self.back(pe, (i - 4) // self.H)

            def vector(self, dve, l0):
                n = len(self.units)
                for i in range(n + 5):
                    if i < n:
                        qb, h = self.units[i]
                        u = self.u0 + i
                        w = (qb + 1) * P
                        dve.wait_ge(sems["s_ready"], u + 1)
                        if i >= 2:
                            dve.wait_ge(sems["pT_ready"], u - 1)
                        sg["s_masked"].by(dve.tensor_tensor_reduce(
                            out=p_t[i % 2][:, 0:w], in0=ps[:, i % 2, 0:w], in1=self.bias(qb), scale=1.0,
                            scalar=TAKEN, op0=ALU.add, op1=ALU.max, accum_out=sx[:, i:i + 1]))
                        dve.wait_ge(sems["s_masked"], u + 1)
                        sg["nmax"].by(dve.tensor_scalar(sn[:, i:i + 1], sx[:, i:i + 1], -SCALE, None, ALU.mult))
                    if i >= 3 and (i - 2) % self.H == 0 and i - 3 < n:
                        qb = (i - 3) // self.H
                        dve.wait_ge(sems["pv_done"], self.u0 + (qb + 1) * self.H)
                        if qb >= 1:
                            dve.wait_ge(sems["oT_ready"], self.b0 + qb)
                        a0, a1 = qb * self.H, (qb + 1) * self.H
                        link(dve, dve.reciprocal(sr[:, a0:a1], sd[:, a0:a1]))
                        sg["o_norm"].by(dve.tensor_tensor(
                            on[:, 0:self.H, :],
                            ps[:, 4 + qb % 2, 0:self.H * HD].rearrange("p (h d) -> p h d", d=HD),
                            sr[:, a0:a1].unsqueeze(2).to_broadcast([P, self.H, HD]), ALU.mult))
                    if i >= 5 and (i - 4) % self.H == 0 and i - 5 < n:
                        qb = (i - 5) // self.H
                        dve.wait_ge(sems["mix_hi"], l0 + qb + 1)
                        hb = self.H // 2
                        sl = (slice(None), slice(self.mix0, self.mix0 + hb), slice(qb * P, (qb + 1) * P))
                        sg["mix_lo"].by(dve.tensor_tensor(
                            hid_lo[sl], ps[:, 6, 0:hb * P].rearrange("p (a b) -> p a b", b=P),
                            hid_hi[sl].bitcast(F32), ALU.subtract))

            def scalar(self, act, l0):
                n = len(self.units)
                for i in range(n + 5):
                    if i < n:
                        qb, h = self.units[i]
                        u = self.u0 + i
                        w = (qb + 1) * P
                        act.wait_ge(sems["nmax"], u + 1)
                        sg["p_ready"].by(act.activation(p_t[i % 2][:, 0:w], p_t[i % 2][:, 0:w], ACT.Exp,
                                                        bias=sn[:, i:i + 1], scale=SCALE, accum_out=sd[:, i:i + 1]))
                    if 1 <= i <= n:
                        j = i - 1
                        qb, h = self.units[j]
                        u = self.u0 + j
                        act.wait_ge(sems["pT_ready"], u + 1)
                        if j >= 2:
                            act.wait_ge(sems["pv_done"], u - 1)
                        sg["pT_copied"].by(act.activation(
                            pT[j % 2][:, 0:qb + 1, :].rearrange("p a b -> p (a b)"),
                            ps[:, 2 + j % 2, 0:(qb + 1) * P], ACT.Copy))
                    if i >= 5 and (i - 4) % self.H == 0 and i - 5 < n:
                        qb = (i - 5) // self.H
                        hb = self.H // 2
                        act.wait_ge(sems["oT_ready"], self.b0 + qb + 1)
                        sg["mix_hi"].by(act.activation(
                            hid_hi[:, self.mix0:self.mix0 + hb, qb * P:(qb + 1) * P],
                            ps[:, 6, 0:hb * P].rearrange("p (a b) -> p a b", b=P), ACT.Copy))

        def causal(qb):
            return tab[:, T_CAUSAL + S - P - qb * P:T_CAUSAL + S]

        def logc(qb):
            return tab[:, T_LOGC + S - P - qb * P:T_LOGC + S]

        def clear():
            nc.all_engine_barrier()
            for n in names:
                nc.sync.sem_clear(sems[n])
            nc.all_engine_barrier()

        def gain_view(v):
            return v.rearrange("(k p) -> p k", p=P)

        eps_c = tab_eps = place("eps", [P, 1])[:, 0:1]
        region = at[0]

        fresh()
        with nc.Block() as block:
            @block.sync
            def _(sp):
                sp.dma_start(xin[:], a["x"][0].rearrange("(t p) d -> p t d", p=P)).then_inc(sems["small"], 16)
                sp.dma_start(tab[:], a["tab"]).then_inc(sems["consts"], 16)

            @block.tensor
            def _(pe):
                pe.wait_ge(sems["small"], 16)
                pe.wait_ge(sems["consts"], 16)
                for k in range(DB):
                    for t in range(TB):
                        mm = pe.transpose(ps[:, k, t * P:(t + 1) * P], xin[:, t, k * P:(k + 1) * P], ident)
                    mm.then_inc(sems["x_T"], 1)

            @block.vector
            def _(dve):
                dve.memset(eps_c, EPS).then_inc(sems["x_copied"], 1)
                for k in range(DB):
                    dve.wait_ge(sems["x_T"], k + 1)
                    dve.tensor_copy(x[:, k, :], ps[:, k, :]).then_inc(sems["x_copied"], 1)
        clear()

        def first_layer(L):
            fresh()
            at[0] = region
            rtab = place("rtab", [P, T_RET])
            dsaq = place("dsaq", [P, 2, S])
            gate = place("gate", [P, 2, S])
            dil_q, dil_k = place("dil_q", [P, 4, S]), place("dil_k", [P, 4, S])
            dil_v = place("dil_v", [P, TB, 512])
            dsa_k, dsa_v = place("dsa_k", [P, 2, S]), place("dsa_v", [P, TB, 256])
            sc = [None] + [place(f"sc{q}", [P, (q + 1) * P]) for q in range(1, TB)]
            w_uk, w_uv = place("w_uk", [P, 256]), place("w_uv", [P, 256])
            widx = place("widx", [P, TB, IDX_H])
            top8 = place("top8", [P, 8])
            q_idx = place("q_idx", [P, 4, S], where=t_off["hid_hi"] + 4 * 2048)
            retqk = place("retqk", [P, 4, S], where=t_off["hid_lo"] + 4 * 2048)
            retv = place("retv", [P, TB, 256], where=t_off["hid_hi"] + 2 * 2048)
            ckv = place("ckv", [P, S], where=t_off["hid_lo"] + 2 * 2048)
            kk = place("kk", [P, S], where=t_off["hid_lo"] + 3 * 2048)
            rl = p_t
            st_b = [place(f"ret_st{i}", [P, S], where=t_off[f"tmp{i}"]) for i in range(2)]

            w_in = a["w_in"][L]
            st = Stream()
            kv = [KT, KT]
            st.group(w_in, [(C_CKV, P), (C_KIDX, HD), (C_KIDX, HD), (C_WIDX, IDX_H)], kv)
            st.group(w_in, [(C_QIDX, 512)], kv)
            st.group(w_in, [(C_DSAQ, 256), (C_RET + 768, 256)], kv)
            st.group(w_in, [(C_RET, 512)], kv)
            st.group(w_in, [(C_RET + 512, 256)], kv)
            st.group(w_in, [(C_DIL, 512)], kv)
            st.group(w_in, [(C_DIL + 512, 512)], kv)
            st.group(w_in, [(C_DIL + 1024, 512)], kv)
            G_MIX = len(st.groups)
            st.group(a["w_out"][L], [(0, 512)], kv)
            st.group(a["w_out"][L], [(512, 512)], kv)
            G0, S0 = len(st.groups), len(st.slots)
            U0 = sum(len(t) - 1 for _, t in st.groups)
            CH = D_FF // D
            land0 = list(st.need)
            TOK = lambda n: [(t, 0, n, t, 0) for t in range(TB)]
            dil = Attention(DIL_H, dil_q, dil_k, dil_v, logc, 4, 0, 0)
            dsa = Attention(DSA_H, dsaq, dsa_k, dsa_v,
                            lambda q: causal(q) if q == 0 else sc[q][:], 2, TB * DIL_H, TB)
            MIX = [2, 2 + TB]
            units = [(qb, h) for qb in range(1, TB) for h in range(IDX_H)]

            with nc.Block() as block:
                @block.sync
                def _(sp):
                    for i, n in enumerate(("attn_norm_w", "mlp_norm_w")):
                        sp.dma_start(gains[:, i, :], gain_view(a[n][L]), allow_slow_non_contiguous=True).then_inc(sems["small"], 16)
                    sp.dma_start(gains[:, 2, 0:2], a["ret_norm_w"][L].rearrange("(b h) d -> (h d) b", h=2), allow_slow_non_contiguous=True).then_inc(sems["small"], 16)
                    sp.dma_start(gains[:, 2, 2:3], a["dsa_kv_norm_w"][L].rearrange("(p o) -> p o", o=1), allow_slow_non_contiguous=True).then_inc(sems["small"], 16)
                    load_slot(sp, 0, st.slots[0].pieces, None)
                    load_slot(sp, 1, st.slots[1].pieces, None)
                    sp.dma_start(w_uk[:], a["dsa_w_uk"][L]).then_inc(sems["consts"], 16)
                    sp.dma_start(w_uv[:], a["dsa_w_uv"][L]).then_inc(sems["consts"], 16)
                    sp.dma_start(rtab[:], a["rtab"]).then_inc(sems["consts"], 16)
                    for s in range(2, len(st.slots)):
                        load_slot(sp, s, st.slots[s].pieces, s - RING + 1)
                    with sp.Fori(0, CH) as c:
                        for j in range(8):
                            col = 512 * (j % 4 // 2)
                            if j < 4:
                                src = a["w_up"][L, 512 * (j % 2):512 * (j % 2) + 512, bass.ds(D * c + col, 512)]
                            else:
                                src = a["w_down"][L, bass.ds(D * c + 512 * (j % 2), 512), col:col + 512]
                            load_slot(sp, j, [(src.rearrange("(k p) c -> p k c", p=P), 0, 512)],
                                      8 * c + S0 + j - RING + 1)

                @block.gpsimd
                def _(pool):
                    stream_lo(pool, st)
                    with pool.Fori(0, CH) as c:
                        for j in range(8):
                            split_lo(pool, j, KT, 512, 8 * c + S0 + j + 1)

                @block.tensor
                def _(pe):
                    def grp(g, blocks, hi=h_hi, lo=h_lo):
                        first, tiles = st.groups[g]
                        group(pe, g, first, tiles, blocks, hi, lo, g % 2)

                    pe.sem_inc(sems["bank_free"], BANKS)
                    stats_pe(pe, 0, 0)
                    pe.wait_ge(sems["h_lo_done"], DB)
                    grp(0, [(0, 0, P, None, 0), (1, P, P, None, 0)]
                        + [(2, 2 * P, IDX_H, t, t * IDX_H) for t in range(TB)])
                    grp(1, FEAT)
                    pe.wait_ge(sems["bank_free"], BANKS + 2 * HALF)
                    stats_pe(pe, 1, 7, 1)
                    for i, (qb, h) in enumerate(units):
                        if i >= 3:
                            pe.wait_ge(sems["idx_relu"], i - 2)
                        p0 = HD * (h % 2)
                        pe.matmul(ps[:, 4 + i % 3, 0:(qb + 1) * P], q_idx[p0:p0 + HD, h // 2, qb * P:(qb + 1) * P],
                                  kk[p0:p0 + HD, 0:(qb + 1) * P], start=True, stop=True).then_inc(sems["idx_ready"], 1)
                    pe.wait_ge(sems["idx_relu"], len(units))
                    pe.wait_ge(sems["ckv_n"], 1)
                    pe.wait_ge(sems["consts"], 16 * 3)
                    for j in range(2):
                        pe.matmul(ps[:, 4 + j, :], w_uk[:, j * P:(j + 1) * P], ckv[:], start=True,
                                  stop=True).then_inc(sems["kv_up"], 1)
                    for t in range(TB):
                        pe.matmul(ps[:, 6 + t // 2, 256 * (t % 2):256 * (t % 2) + 256], ckv[:, t * P:(t + 1) * P],
                                  w_uv[:], start=True, stop=True, skip_group_check=True).then_inc(sems["kv_up"], 1)
                    grp(2, FEAT)
                    pe.wait_ge(sems["kv_out"], 4)
                    grp(3, FEAT)
                    grp(4, TOK(256))
                    grp(5, FEAT)
                    grp(6, FEAT)
                    grp(7, TOK(512))
                    pe.wait_ge(sems["bank_free"], BANKS + HALF * G_MIX)
                    for j in range(4):
                        pe.matmul(ps[:, j, :], rot_m, retqk[:, j, :], start=True, stop=True).then_inc(sems["ret_rot"], 1)
                    pe.wait_ge(sems["ret_rotd"], 4)
                    ru = [(h, kb) for h in range(RET_H) for kb in range(TB)]
                    for i in range(len(ru) + 1):
                        if i < len(ru):
                            h, kb = ru[i]
                            p0, w = HD * (h % 2), S - kb * P
                            if i >= 2:
                                pe.wait_ge(sems["ret_p"], i - 1)
                            pe.matmul(ps[:, 4 + i % 2, 0:w], retqk[p0:p0 + HD, 2 + h // 2, kb * P:(kb + 1) * P],
                                      retqk[p0:p0 + HD, h // 2, kb * P:S], start=True, stop=True).then_inc(sems["ret_s"], 1)
                        if i >= 1:
                            h, kb = ru[i - 1]
                            p0, w = HD * (h % 2), S - kb * P
                            pe.wait_ge(sems["ret_p"], i)
                            pe.matmul(ps[p0:p0 + HD, 6 + h // 2, kb * P:S], retv[:, kb, h * HD:(h + 1) * HD],
                                      st_b[(i - 1) % 2][:, 0:w], start=kb == 0, stop=kb == TB - 1,
                                      skip_group_check=True).then_inc(sems["ret_o"], 1)
                    for j in range(2):
                        pe.wait_ge(sems["gn_in"], j + 1)
                        pe.matmul(ps[:, j, :], mean_m, p_t[j][:], start=True, stop=True).then_inc(sems["gn_mean"], 1)
                    for j in range(2):
                        pe.wait_ge(sems["gn_sq"], j + 1)
                        pe.matmul(ps[:, 2 + j, :], mean_m, st_b[j][:], start=True, stop=True).then_inc(sems["gn_var"], 1)
                    pe.wait_ge(sems["mix_lo"], 2)
                    dil.tensor(pe, MIX[0])
                    pe.wait_ge(sems["mix_lo"], MIX[0] + TB)
                    pe.wait_ge(sems["bias_ready"], 3)
                    dsa.tensor(pe, MIX[1])
                    pe.wait_ge(sems["mix_lo"], MIX[1] + TB)
                    grp(8, FEAT, hid_hi, hid_lo)
                    grp(9, FEAT, hid_hi, hid_lo)
                    pe.wait_ge(sems["bank_free"], BANKS + HALF * (G0 - 1))
                    stats_pe(pe, 2, HALF * (G0 % 2))
                    pe.wait_ge(sems["h_lo_done"], 2 * DB)
                    with pe.Fori(0, CH) as c:
                        for j in range(4):
                            ring_of[0] = 0
                            g = 4 * c + (G0 + j)
                            if j >= 2:
                                pe.wait_ge(sems["hid_lo_done"], 8 * c + 8)
                            group(pe, g, 8 * c + (S0 + 2 * j), kv, FEAT, *((h_hi, h_lo) if j < 2 else (hid_hi, hid_lo)),
                                  (G0 + j) % 2)

                @block.scalar
                def _(act):
                    stream_hi(act, st, 0)
                    stream_hi(act, st, 1)
                    stats_bank[0] = 0
                    stats_act(act, lambda k: x[:, k, :], 0, 1.0 / D)
                    norm_split_act(act, 0)
                    stream_hi(act, st, 2)
                    stream_hi(act, st, 3)
                    stream_hi(act, st, 4)
                    act.wait_ge(sems["ckv_in"], 1)
                    stats_bank[1] = 7
                    stats_act(act, lambda k: ckv[:], 1, 1.0 / P, 1)
                    for i, (qb, h) in enumerate(units):
                        act.wait_ge(sems["idx_ready"], i + 1)
                        if i >= 2:
                            act.wait_ge(sems["idx_used"], i - 1)
                        else:
                            act.wait_ge(sems["ckv_n"], 1)
                        sg["idx_relu"].by(act.activation(rl[i % 2][:, 0:(qb + 1) * P],
                                                         ps[:, 4 + i % 3, 0:(qb + 1) * P], ACT.Relu))
                    for s in range(5, 10):
                        stream_hi(act, st, s)
                    act.wait_ge(sems["bank_free"], BANKS + HALF * 3)
                    alink(act, act.activation(gate[:], gate[:], ACT.Silu))
                    for s in range(10, 18):
                        stream_hi(act, st, s)
                    for j in range(2):
                        act.wait_ge(sems["gn_c"], j + 1)
                        sg["gn_sq"].by(act.activation(st_b[j][:], p_t[j][:], ACT.Square))
                    for j in range(2):
                        act.wait_ge(sems["gn_var"], j + 1)
                        alink(act, act.activation(st_b[j][:], ps[:, 2 + j, :], ACT.Ln, bias=eps_c))
                        sg["gn_rstd"].by(act.activation(st_b[j][:], st_b[j][:], ACT.Exp, scale=-0.5))
                    for j in range(2):
                        act.wait_ge(sems["gn_out"], j + 1)
                        sg["mix_hi"].by(act.activation(hid_hi[:, j, :], p_t[j][:], ACT.Copy))
                    act.wait_ge(sems["mix_lo"], 2)
                    dil.scalar(act, MIX[0])
                    dsa.scalar(act, MIX[1])
                    stream_hi(act, st, 18)
                    stream_hi(act, st, 19)
                    base = S0

                    def hi(c, j):
                        if j % 2 == 0:
                            used = ("slot_used", 4 * c + (U0 + j // 2)) if not isinstance(c, int) else ("slot_used", 4 * c + U0 + j // 2)
                        else:
                            used = ("bank_ready", 16 * c + HALF * (G0 + j // 2))
                        split_hi(act, j, KT, 512, 64 * c + (land0[j % 2] + 16 * (j // 2 + 1)), used)

                    hi(0, 0)
                    hi(0, 1)
                    act.wait_ge(sems["bank_free"], BANKS + HALF * G0)
                    stats_bank[2] = HALF * (G0 % 2)
                    stats_act(act, lambda k: x[:, k, :], 2, 1.0 / D)
                    norm_split_act(act, 1)

                    def chunk(c, last):
                        for j in range(4):
                            hi_a = not (last and j == 3)
                            if hi_a:
                                hi(c, 2 * j + 2)
                            if j < 2:
                                for m in range(4):
                                    n_in = 4 * j + m
                                    n = 8 * c + n_in
                                    act.wait_ge(sems["bank_ready"], 16 * c + (HALF * (G0 + j) + m + 1))
                                    act.wait_ge(sems["bank_free"], 16 * c + (HALF * (G0 + j) + m + 7))
                                    if n_in >= 2:
                                        act.wait_ge(sems["hid_hi_done"], 8 * c + (n_in - 1))
                                    act.activation(tmp[m % 2][:], ps[:, HALF * ((G0 + j) % 2) + m, :],
                                                   ACT.Relu).then_inc(sems["relu_ready"], 1)
                                    act.wait_ge(sems["relu_ready"], n + 1)
                                    act.activation(hid_hi[:, 4 * j + m, :], tmp[m % 2][:],
                                                   ACT.Square).then_inc(sems["hid_hi_done"], 1)
                            if hi_a:
                                hi(c, 2 * j + 3)

                    with act.Fori(0, CH - 1) as c:
                        chunk(c, False)
                    chunk(CH - 1, True)

                @block.vector
                def _(dve):
                    dve.wait_ge(sems["small"], 16 * 4)
                    norm_split_dve(dve, lambda k: gains[:, 0, k:k + 1], 0, 0)

                    def evac(g, m, o, src=None):
                        dve.wait_ge(sems["bank_ready"], HALF * g + m + 1)
                        i = ps[:, HALF * (g % 2) + m, :] if src is None else src
                        sg["bank_free"].by(dve.tensor_copy(o, i))

                    dve.wait_ge(sems["bank_ready"], HALF)
                    sg["bank_free"].by(dve.tensor_copy(kk[:], ps[:, 1, :]))
                    sg["ckv_in"].by(dve.tensor_copy(ckv[:], ps[:, 0, :]))
                    dve.wait_ge(sems["ckv_in"], 1)
                    dve.wait_ge(sems["bank_ready"], HALF)
                    sg["bank_free"].by(dve.tensor_scalar(widx[:].rearrange("p a b -> p (a b)"), ps[:, 2, 0:TB * IDX_H],
                                                         IDX_H ** -0.5 * HD ** -0.5, None, ALU.mult), 3)
                    for m in range(4):
                        evac(1, m, q_idx[:, m, :])
                    dve.wait_ge(sems["rstd_ready"], 2)
                    sg["ckv_n"].by(dve.scalar_tensor_tensor(out=ckv[:], in0=ckv[:], scalar=gains[:, 2, 2:3],
                                                            in1=rstd[:], op0=ALU.mult, op1=ALU.mult))
                    for i, (qb, h) in enumerate(units):
                        w = (qb + 1) * P
                        dve.wait_ge(sems["idx_relu"], i + 1)
                        wt = widx[:, qb, h:h + 1]
                        if h == 0:
                            sg["idx_used"].by(dve.tensor_scalar(sc[qb][:], rl[i % 2][:, 0:w], wt, None, ALU.mult))
                        else:
                            dve.wait_ge(sems["idx_used"], i)
                            sg["idx_used"].by(dve.scalar_tensor_tensor(out=sc[qb][:], in0=rl[i % 2][:, 0:w], scalar=wt,
                                                                       in1=sc[qb][:], op0=ALU.mult, op1=ALU.add))
                    dve.wait_ge(sems["idx_used"], len(units))
                    for qb in range(1, TB):
                        link(dve, dve.tensor_tensor(sc[qb][:], sc[qb][:], causal(qb), ALU.add))
                    dve.wait_ge(sems["kv_up"], 2)
                    sg["kv_out"].by(dve.tensor_copy(dsa_k[:, 0, :], ps[:, 4, :]))
                    sg["kv_out"].by(dve.tensor_copy(dsa_k[:, 1, :], ps[:, 5, :]))
                    dve.wait_ge(sems["kv_up"], 6)
                    sg["kv_out"].by(dve.tensor_copy(dsa_v[:, 0:2, :].rearrange("p a b -> p (a b)"), ps[:, 6, :]))
                    sg["kv_out"].by(dve.tensor_copy(dsa_v[:, 2:4, :].rearrange("p a b -> p (a b)"), ps[:, 7, :]))
                    rounds = [(qb, r) for r in range(TOPK // 8) for qb in range(1, TB)]

                    def take(n):
                        for _ in range(min(n, len(rounds))):
                            qb, r = rounds.pop(0)
                            link(dve, dve.max(top8[:], sc[qb][:]))
                            link(dve, dve.match_replace(sc[qb][:], top8[:], sc[qb][:], TAKEN))

                    for g, outs in ((2, [dsaq[:, 0, :], dsaq[:, 1, :], gate[:, 0, :], gate[:, 1, :]]),
                                    (3, [retqk[:, m, :] for m in range(4)]),
                                    (4, None),
                                    (5, [dil_q[:, m, :] for m in range(4)]),
                                    (6, [dil_k[:, m, :] for m in range(4)]),
                                    (7, [dil_v[:, m, :] for m in range(4)])):
                        for m in range(4):
                            if g == 4:
                                evac(g, m, retv[:, m, :], ps[:, HALF * (g % 2) + m, 0:256])
                            else:
                                evac(g, m, outs[m])
                        if g < 7:
                            take(10)
                    take(len(rounds))
                    for qb in range(1, TB):
                        sg["bias_ready"].by(dve.tensor_scalar(sc[qb][:], sc[qb][:], -2e38, NEG, ALU.is_gt, ALU.mult))
                    dve.wait_ge(sems["consts"], 16 * 3)
                    for j in range(4):
                        dve.wait_ge(sems["ret_rot"], j + 1)
                        link(dve, dve.tensor_tensor(st_b[0][:], ps[:, j, :], rtab[:, T_SIN:T_SIN + S], ALU.mult))
                        link(dve, dve.tensor_tensor(st_b[1][:], retqk[:, j, :], rtab[:, T_COS:T_COS + S], ALU.mult))
                        sg["ret_rotd"].by(dve.tensor_tensor(retqk[:, j, :], st_b[0][:], st_b[1][:], ALU.add))
                        dve.wait_ge(sems["ret_rotd"], j + 1)
                    for i in range(RET_H * TB):
                        h, kb = divmod(i, TB)
                        w = S - kb * P
                        dve.wait_ge(sems["ret_s"], i + 1)
                        if i >= 2:
                            dve.wait_ge(sems["ret_o"], i - 1)
                        sg["ret_p"].by(dve.tensor_tensor(st_b[i % 2][:, 0:w], ps[:, 4 + i % 2, 0:w],
                                                         rtab[:, T_DECAY + h * S:T_DECAY + h * S + w], ALU.mult))
                    for j in range(2):
                        dve.wait_ge(sems["ret_o"], 2 * TB * (j + 1))
                        sg["gn_in"].by(dve.tensor_copy(p_t[j][:], ps[:, 6 + j, :]))
                    dve.wait_ge(sems["gn_in"], 2)
                    for j in range(2):
                        dve.wait_ge(sems["gn_mean"], j + 1)
                        sg["gn_c"].by(dve.tensor_tensor(p_t[j][:], p_t[j][:], ps[:, j, :], ALU.subtract))
                    for j in range(2):
                        dve.wait_ge(sems["gn_rstd"], j + 1)
                        link(dve, dve.scalar_tensor_tensor(out=p_t[j][:], in0=p_t[j][:], scalar=gains[:, 2, j:j + 1],
                                                           in1=st_b[j][:], op0=ALU.mult, op1=ALU.mult))
                        sg["gn_out"].by(dve.tensor_tensor(p_t[j][:], p_t[j][:], gate[:, j, :], ALU.mult))
                        dve.wait_ge(sems["gn_out"], j + 1)
                        dve.wait_ge(sems["mix_hi"], j + 1)
                        sg["mix_lo"].by(dve.tensor_tensor(hid_lo[:, j, :], p_t[j][:], hid_hi[:, j, :].bitcast(F32),
                                                          ALU.subtract))
                    dve.wait_ge(sems["mix_lo"], 2)
                    dil.vector(dve, MIX[0])
                    dve.wait_ge(sems["mix_lo"], MIX[0] + TB)
                    dsa.vector(dve, MIX[1])
                    for g in (8, 9):
                        for m in range(4):
                            dve.wait_ge(sems["bank_ready"], HALF * g + m + 1)
                            b = 4 * (g - 8) + m
                            sg["bank_free"].by(dve.tensor_tensor(x[:, b, :], x[:, b, :], ps[:, HALF * (g % 2) + m, :],
                                                                 ALU.add))
                    dve.wait_ge(sems["bank_free"], BANKS + HALF * G0)
                    norm_split_dve(dve, lambda k: gains[:, 1, k:k + 1], 2, 1)
                    dve.wait_ge(sems["h_lo_done"], 2 * DB)
                    with dve.Fori(0, CH) as c:
                        for j in range(4):
                            for m in range(4):
                                bank = HALF * ((G0 + j) % 2) + m
                                if j < 2:
                                    n = 4 * j + m
                                    dve.wait_ge(sems["relu_ready"], 8 * c + (n + 1))
                                    dve.scalar_tensor_tensor(out=sq[m % 2][:], in0=ps[:, bank, :], scalar=0.0,
                                                             in1=tmp[m % 2][:], op0=ALU.max,
                                                             op1=ALU.mult).then_inc(sems["bank_free"], 1)
                                    dve.wait_ge(sems["bank_free"], 16 * c + (BANKS + HALF * (G0 + j) + m + 1))
                                    dve.wait_ge(sems["hid_hi_done"], 8 * c + (n + 1))
                                    dve.tensor_tensor(hid_lo[:, n, :], sq[m % 2][:], hid_hi[:, n, :].bitcast(F32),
                                                      ALU.subtract).then_inc(sems["hid_lo_done"], 1)
                                    dve.wait_ge(sems["hid_lo_done"], 8 * c + (n + 1))
                                else:
                                    b = 4 * (j - 2) + m
                                    dve.wait_ge(sems["bank_ready"], 16 * c + (HALF * (G0 + j) + m + 1))
                                    dve.tensor_tensor(x[:, b, :], x[:, b, :], ps[:, bank, :],
                                                      ALU.add).then_inc(sems["bank_free"], 1)

        with nc.Fori(0, DEPTH) as L:
            first_layer(L)
            clear()

        acc = None

        def second_layer(layer):
            fresh()
            at[0] = region
            even = layer == 0
            acc = place(f"acc{layer}", [P, DB, S])
            gain_f = place(f"gain_f{layer}", [P, DB])
            st = Stream()
            kv = [KT, KT]
            if even:
                w_in = a["ev_w_in_2"][0]
                F = 512
                st.group(w_in, [(3 * F, P)], kv)
                st.group(w_in, [(3 * F + FOX_H, 512)], kv)
                st.group(w_in, [(0, 512)], kv)
                st.group(w_in, [(F, 512)], kv)
                st.group(w_in, [(2 * F, 512)], kv)
                w_out = a["ev_w_out_2"][0]
            else:
                w_in = a["od_w_in_2"][0]
                for c in (2, 3, 0, 1):
                    st.group(w_in, [(512 * c, 512)], kv)
                w_out = a["od_w_out_2"][0]
            GM = len(st.groups)
            st.group(w_out, [(0, 512)], kv)
            st.group(w_out, [(512, 512)], kv)
            wg, wu, wd = (a[n][layer] for n in ("ffn_w_gate_2", "ffn_w_up_2", "ffn_w_down_2"))
            CH = D_FF2 // 512
            R0 = CH * 512

            class Pair:
                pass

            def up_group(col, width):
                st.group_pairs(((wg, col, width), (wu, col, width)), kv)

            up_group(R0, D_FF2 - R0)
            st.group(wd, [(0, 512)], [(D_FF2 - R0) // P], r0=R0)
            st.group(wd, [(512, 512)], [(D_FF2 - R0) // P], r0=R0)
            G0, S0 = len(st.groups), len(st.slots)
            GU = GM + 2
            U0 = sum(len(t) - 1 for _, t in st.groups)
            land0 = list(st.need)
            SL, GC = 6, 4
            N0 = 1 if even else 0
            TOK = [(t, 0, 512, t, 0) for t in range(TB)]
            gb = lambda i: (lambda k: gains[:, i, k:k + 1])
            xb = lambda k: x[:, k, :]
            ab = lambda k: acc[:, k, :]

            if even:
                fq, fk = place("fq", [P, 4, S]), place("fk", [P, 4, S])
                fv = place("fv", [P, TB, 512])
                bf = place("bf", [FOX_H, 1])
                lf, lc = place("lf", [FOX_H, S]), place("lc", [FOX_H, S])
                sel = place("sel_t", [FOX_H, FOX_H * P], where=t_off["acc0"])
                pw = place("pw", [P, 4, P], where=t_off["acc0"] + 4096)
                psc = place("psc", [P, 4])
                pooled = place("pooled", [P, 4, S], where=t_off["acc0"] + 4096 + 2048)
                ub = [place(f"ub{i}", [P, 16 + S], where=t_off["fq"] + 2112 * i) for i in range(3)]
                t16 = place("t16", [P, 16])
                fox = Attention(FOX_H, fq, fk, fv, causal, 0, 0, 0, decay=(sel, lf))
                MIX0 = 4
            else:
                xr, gt = place("xr", [P, DB, S]), place("gt", [P, DB, S])
                t8 = place("t8", [P, DB, S], where=t_off["acc1"])
                r8, i8 = place("r8", [P, DB, S], where=t_off["h_hi"]), place("i8", [P, DB, S], where=t_off["h_lo"])
                wa = place("wa", [P, 8, 256], where=t_off["hid_hi"])
                wx = place("wx", [P, 8, 256], where=t_off["hid_lo"])
                xp = [place(f"xp{i}", [P, 3 + S + 1]) for i in range(2)]
                par = place("par", [P, 8, DB])
                sp8 = place("sp8", [P, 3, DB])

            with nc.Block() as block:
                @block.sync
                def _(sp):
                    def small(dst, src):
                        sp.dma_start(dst, src, allow_slow_non_contiguous=True).then_inc(sems["small"], 16)

                    for i, n in enumerate(("mix_pre_g_2", "mix_post_g_2", "ffn_pre_g_2", "ffn_post_g_2")):
                        small(gains[:, i, :], gain_view(a[n][layer]))
                    small(gain_f[:], gain_view(a["final_norm_w"]))
                    if even:
                        small(bf[:], a["ev_b_f_2"][0].rearrange("(p o) -> p o", o=1))
                        small(psc[:], gain_view(a["ev_pool_scale_2"][0]))
                    else:
                        for i in range(4):
                            small(par[:, i, :], gain_view(a["od_conv_w_2"][0, i]))
                        for i, n in enumerate(("od_conv_b_2", "od_b_a_2", "od_b_x_2", "od_lam_2")):
                            small(par[:, 4 + i, :], gain_view(a[n][0]))
                    load_slot(sp, 0, st.slots[0].pieces, None)
                    load_slot(sp, 1, st.slots[1].pieces, None)
                    if even:
                        sp.dma_start(sel[:], a["sel"]).then_inc(sems["consts"], 16)
                        sp.dma_start(pw[:], a["ev_pool_w_2"][0].rearrange("g d e -> d g e")).then_inc(sems["consts"], 16)
                    else:
                        for t, n in ((wa, "od_w_a_2"), (wx, "od_w_x_2")):
                            sp.dma_start(t[:], a[n][0].rearrange("h (b p) e -> p (h b) e", p=P)).then_inc(sems["consts"], 16)
                    for s in range(2, len(st.slots)):
                        load_slot(sp, s, st.slots[s].pieces, s - RING + 1)
                    with sp.Fori(0, CH) as c:
                        for j in range(SL):
                            s = SL * c + (S0 + j - RING + 1)
                            if j < 4:
                                rows = slice(512 * (j % 2), 512 * (j % 2) + 512)
                                col = bass.ds(512 * c + 256 * (j // 2), 256)
                                pieces = [(w[rows, col].rearrange("(k p) c -> p k c", p=P), 256 * q, 256)
                                          for q, w in enumerate((wg, wu))]
                            else:
                                src = wd[bass.ds(512 * c, 512), 512 * (j - 4):512 * (j - 4) + 512]
                                pieces = [(src.rearrange("(k p) c -> p k c", p=P), 0, 512)]
                            load_slot(sp, j, pieces, s)

                @block.gpsimd
                def _(pool):
                    stream_lo(pool, st)
                    with pool.Fori(0, CH) as c:
                        for j in range(SL):
                            split_lo(pool, j, KT, 512, SL * c + (S0 + j + 1))

                @block.tensor
                def _(pe):
                    def grp(g, blocks, hi=h_hi, lo=h_lo):
                        first, tiles = st.groups[g]
                        group(pe, g, first, tiles, blocks, hi, lo, g % 2)

                    pe.sem_inc(sems["bank_free"], BANKS)
                    for n in range(N0 + 1):
                        stats_pe(pe, n, 0)
                    pe.wait_ge(sems["h_lo_done"], DB)
                    if even:
                        grp(0, [(0, 0, P, None, 0)])
                        for g in (1, 2, 3):
                            grp(g, FEAT)
                        grp(4, TOK)
                        pe.wait_ge(sems["bank_free"], BANKS + HALF * GM)
                        pe.wait_ge(sems["consts"], 32)
                        for g in range(4):
                            pe.wait_ge(sems["pool_in"], g + 1)
                            pe.matmul(ps[:, 4 + g, :], pw[:, g, :], pooled[:, g, :], start=True,
                                      stop=True).then_inc(sems["pool_mm"], 1)
                        pe.wait_ge(sems["mix_lo"], MIX0)
                        pe.wait_ge(sems["f_done"], 1)
                        fox.tensor(pe, MIX0)
                        pe.wait_ge(sems["mix_lo"], MIX0 + TB)
                    else:
                        for g in range(4):
                            grp(g, FEAT)
                        pe.wait_ge(sems["bank_free"], BANKS + HALF * GM)
                        pe.wait_ge(sems["consts"], 32)
                        for u in range(2 * DB):
                            w, b = (wa, wx)[u // DB], u % DB
                            if u >= DB:
                                pe.wait_ge(sems["lru_r"], u - DB + 1)
                            for q in range(2):
                                mm = pe.matmul(ps[:, b, :], w[:, 2 * (b // 2) + q, P * (b % 2):P * (b % 2) + P],
                                               xr[:, 2 * (b // 2) + q, :], start=q == 0, stop=q == 1)
                            mm.then_inc(sems["lru_mm"], 1)
                        pe.wait_ge(sems["mix_lo"], DB)
                    grp(GM, FEAT, hid_hi, hid_lo)
                    grp(GM + 1, FEAT, hid_hi, hid_lo)
                    pe.wait_ge(sems["bank_free"], BANKS + HALF * (GU - 1))
                    stats_pe(pe, N0 + 1, HALF * (GU % 2))
                    pe.wait_ge(sems["rstd_ready"], N0 + 2)
                    stats_pe(pe, N0 + 2, HALF * (GU % 2))
                    pe.wait_ge(sems["h_lo_done"], 2 * DB)
                    grp(GU, FEAT)
                    pe.wait_ge(sems["hid_lo_done"], 2)
                    grp(GU + 1, FEAT, hid_hi, hid_lo)
                    grp(GU + 2, FEAT, hid_hi, hid_lo)
                    with pe.Fori(0, CH) as c:
                        for j in range(GC):
                            ring_of[0] = (0, 0, 0, 1)[j]
                            if j == 2:
                                pe.wait_ge(sems["hid_lo_done"], 4 * c + 6)
                            group(pe, GC * c + (G0 + j), SL * c + (S0 + (0, 2, 4, 5)[j]), kv if j < 2 else [KT], FEAT,
                                  *((h_hi, h_lo) if j < 2 else (hid_hi, hid_lo)), (G0 + j) % 2)
                    pe.wait_ge(sems["bank_free"], BANKS + HALF * (G0 + GC * CH))
                    stats_pe(pe, N0 + 3, 0)

                @block.scalar
                def _(act):
                    stream_hi(act, st, 0)
                    stream_hi(act, st, 1)
                    for n in range(N0 + 1):
                        stats_bank[n] = 0
                    if even:
                        stats_act(act, xb, 0, 1.0 / D)
                        stats_act(act, xb, 1, 1.0 / D, ready=("xup", 1))
                    else:
                        stats_act(act, xb, 0, 1.0 / D)
                    norm_split_act(act, 0)
                    if even:
                        for s in range(2, 6):
                            stream_hi(act, st, s)
                        act.wait_ge(sems["f_in"], 1)
                        alink(act, act.activation(lc[:], lf[:], ACT.Abs))
                        alink(act, act.activation(lc[:], lc[:], ACT.Exp, scale=-1.0))
                        sg["f_c"].by(act.activation(lc[:], lc[:], ACT.Ln, bias=1.0))
                        for s in range(6, 12):
                            stream_hi(act, st, s)
                        for g in range(4):
                            act.wait_ge(sems["pool_out"], g + 1)
                            sg["mix_hi"].by(act.activation(hid_hi[:, 4 + g, :], tmp[g % 2][:], ACT.Copy))
                        act.wait_ge(sems["mix_lo"], MIX0)
                        fox.scalar(act, MIX0)
                        nxt = 12
                    else:
                        act.wait_ge(sems["small"], 16 * 13)
                        alink(act, act.activation(sp8[:, 0, :], par[:, 7, :], ACT.Abs))
                        alink(act, act.activation(sp8[:, 0, :], sp8[:, 0, :], ACT.Exp, scale=-1.0))
                        sg["f_c"].by(act.activation(sp8[:, 0, :], sp8[:, 0, :], ACT.Ln, bias=1.0))
                        for s in range(2, 10):
                            stream_hi(act, st, s)
                        act.wait_ge(sems["f_done"], 1)
                        act.wait_ge(sems["bank_free"], BANKS + HALF * GM)
                        alink(act, act.activation(gt[:], gt[:], ACT.Gelu_apprx_tanh))
                        for u in range(2 * DB):
                            act.wait_ge(sems["lru_mm"], u + 1)
                            b = u % DB
                            sg["lru_r"].by(act.activation((r8, i8)[u // DB][:, b, :], ps[:, b, :], ACT.Sigmoid,
                                                          bias=par[:, 5 + u // DB, b:b + 1]))
                        act.wait_ge(sems["lru_r"], 2 * DB)
                        for b in range(DB):
                            sg["lru_t"].by(act.activation(t8[:, b, :], r8[:, b, :], ACT.Tanh, scale=sp8[:, 1, b:b + 1]))
                        act.wait_ge(sems["lru_t"], DB)
                        for b in range(DB):
                            sg["lru_a"].by(act.activation(r8[:, b, :], r8[:, b, :], ACT.Exp, scale=sp8[:, 2, b:b + 1]))
                        for b in range(DB):
                            act.wait_ge(sems["lru_b"], b + 1)
                            sg["gelu_done"].by(act.activation(t8[:, b, :], t8[:, b, :], ACT.Sqrt))
                        for b in range(DB):
                            act.wait_ge(sems["y_done"], b + 1)
                            sg["mix_hi"].by(act.activation(hid_hi[:, b, :], tmp[b % 2][:], ACT.Copy))
                        nxt = 10
                    for s in range(nxt, 2 * GU):
                        stream_hi(act, st, s)
                    stream_hi(act, st, 2 * GU)
                    stream_hi(act, st, 2 * GU + 1)
                    stats_bank[N0 + 1] = stats_bank[N0 + 2] = HALF * (GU % 2)
                    stats_act(act, ab, N0 + 1, 1.0 / D, ready=("m_done", 1))
                    stats_act(act, xb, N0 + 2, 1.0 / D, ready=("xup", DB * N0 + 1))
                    norm_split_act(act, 1)

                    def hi(c, j):
                        q, jj = divmod(j, SL)
                        cc = c + q
                        used = (("bank_ready", GC * HALF * cc + HALF * (G0 - 1)), ("bank_ready", GC * HALF * cc + HALF * G0),
                                ("slot_used", 2 * cc + (U0 + 1)), ("bank_ready", GC * HALF * cc + HALF * (G0 + 1)),
                                ("slot_used", 2 * cc + (U0 + 2)), ("bank_ready", GC * HALF * cc + HALF * (G0 + 2)))[jj]
                        split_hi(act, jj, KT, 512, 80 * cc + (land0[jj % 2] + (32, 32, 64, 64, 80, 80)[jj]), used)

                    def gated(g, n, ready, free):
                        act.wait_ge(sems["bank_free"], free)
                        for m in range(2):
                            act.wait_ge(sems["bank_ready"], ready + m + 1)
                            act.activation(tmp[m][:], ps[:, HALF * (g % 2) + m, :],
                                           ACT.Silu).then_inc(sems["relu_ready"], 1)
                        for m in range(2):
                            act.wait_ge(sems["v_ready"], n + m + 1)
                            act.activation(hid_hi[:, gated_at[0] + m, :], sq[m][:],
                                           ACT.Copy).then_inc(sems["hid_hi_done"], 1)

                    gated_at = [0]
                    gated(GU, 0, HALF * GU, BANKS + HALF * GU)
                    stream_hi(act, st, S0 - 2)
                    stream_hi(act, st, S0 - 1)
                    hi(0, 0)
                    hi(0, 1)

                    def chunk(c, last):
                        for j in range(2):
                            hi(c, 2 * j + 2)
                            gated_at[0] = 2 * j
                            gated(G0 + j, 4 * c + (2 + 2 * j), GC * HALF * c + HALF * (G0 + j),
                                  GC * HALF * c + (BANKS + HALF * (G0 + j)))
                            hi(c, 2 * j + 3)
                        if not last:
                            hi(c, 6)
                            hi(c, 7)

                    with act.Fori(0, CH - 1) as c:
                        chunk(c, False)
                    chunk(CH - 1, True)
                    act.wait_ge(sems["bank_free"], BANKS + HALF * (G0 + GC * CH))
                    stats_bank[N0 + 3] = 0
                    stats_act(act, ab, N0 + 3, 1.0 / D)

                @block.vector
                def _(dve):
                    dve.wait_ge(sems["small"], 16 * (7 if even else 13))
                    if even:
                        dve.wait_ge(sems["rstd_ready"], 1)
                        for k in range(DB):
                            sg["xup"].by(dve.scalar_tensor_tensor(out=x[:, k, :], in0=x[:, k, :], scalar=gain_f[:, k:k + 1],
                                                                  in1=rstd[:], op0=ALU.mult, op1=ALU.mult))
                        dve.wait_ge(sems["xup"], DB)
                    norm_split_dve(dve, gb(0), N0, 0)

                    def evac(g, m, o, bank_src=None):
                        dve.wait_ge(sems["bank_ready"], HALF * g + m + 1)
                        sg["bank_free"].by(dve.tensor_copy(o, ps[:, HALF * (g % 2) + m, :]))

                    if even:
                        for i in range(3):
                            link(dve, dve.memset(ub[i][:, 0:16], 0.0))
                        dve.wait_ge(sems["bank_ready"], HALF)
                        sg["bank_free"].by(dve.tensor_scalar(lf[:], ps[0:FOX_H, 0, :], bf[:], None, ALU.add), HALF)
                        dve.wait_ge(sems["bank_free"], BANKS + HALF)
                        dve.sem_inc(sems["f_in"], 1)
                        for m in range(4):
                            w = POOL_W[m]
                            dve.wait_ge(sems["bank_ready"], HALF + m + 1)
                            sg["bank_free"].by(dve.tensor_copy(ub[0][:, 16:], ps[:, HALF + m, :]))
                            dve.wait_ge(sems["bank_free"], sg["bank_free"].n + BANKS)
                            src, step, i = ub[0], 1, 1
                            while step < w:
                                link(dve, dve.tensor_tensor(ub[i][:, 16:], src[:, 16:], src[:, 16 - step:16 + S - step],
                                                            ALU.add))
                                src, step, i = ub[i], 2 * step, 3 - i
                            link(dve, dve.scalar_tensor_tensor(out=pooled[:, m, :], in0=src[:, 16:], scalar=1.0 / w,
                                                               in1=ub[0][:, 16:], op0=ALU.mult, op1=ALU.subtract))
                            link(dve, dve.tensor_tensor(t16[:], src[:, 16:32], tab[:, T_POOL + 16 * m:T_POOL + 16 * m + 16],
                                                        ALU.mult))
                            sg["pool_in"].by(dve.tensor_tensor(pooled[:, m, 0:16], t16[:], ub[0][:, 16:32], ALU.subtract))
                            dve.wait_ge(sems["pool_in"], m + 1)
                        dve.wait_ge(sems["f_c"], 1)
                        link(dve, dve.scalar_tensor_tensor(out=lc[:], in0=lf[:], scalar=0.0, in1=lc[:], op0=ALU.min,
                                                           op1=ALU.subtract))
                        link(dve, dve.tensor_tensor_scan(lf[:], tab[0:FOX_H, T_ONES:T_ONES + 1].to_broadcast([FOX_H, S]),
                                                         lc[:], 0.0, ALU.mult, ALU.add))
                        sg["f_done"].by(dve.tensor_scalar(lf[:], lf[:], -1.0 / SCALE, None, ALU.mult))
                        for g, t in ((2, fq), (3, fk), (4, fv)):
                            for m in range(4):
                                evac(g, m, t[:, m, :])
                        for g in range(4):
                            dve.wait_ge(sems["pool_mm"], g + 1)
                            if g >= 2:
                                dve.wait_ge(sems["mix_lo"], g - 1)
                            sg["pool_out"].by(dve.tensor_scalar(tmp[g % 2][:], ps[:, 4 + g, :], psc[:, g:g + 1], None, ALU.mult))
                            dve.wait_ge(sems["mix_hi"], g + 1)
                            sg["mix_lo"].by(dve.tensor_tensor(hid_lo[:, 4 + g, :], tmp[g % 2][:],
                                                              hid_hi[:, 4 + g, :].bitcast(F32), ALU.subtract))
                        dve.wait_ge(sems["mix_lo"], MIX0)
                        fox.vector(dve, MIX0)
                    else:
                        for i in range(2):
                            link(dve, dve.memset(xp[i][:, 0:3], 0.0))
                        dve.wait_ge(sems["f_c"], 1)
                        link(dve, dve.tensor_scalar(sp8[:, 1, :], par[:, 7, :], -1.0, 0.0, ALU.mult, ALU.max))
                        link(dve, dve.tensor_tensor(sp8[:, 0, :], sp8[:, 0, :], sp8[:, 1, :], ALU.add))
                        link(dve, dve.tensor_scalar(sp8[:, 1, :], sp8[:, 0, :], LRU_C, None, ALU.mult))
                        sg["f_done"].by(dve.tensor_scalar(sp8[:, 2, :], sp8[:, 0, :], -LRU_C, None, ALU.mult))
                        for b in range(DB):
                            g, m = b // 4, b % 4
                            q = xp[b % 2]
                            dve.wait_ge(sems["bank_ready"], HALF * g + m + 1)
                            sg["bank_free"].by(dve.tensor_copy(q[:, 3:3 + S], ps[:, HALF * (g % 2) + m, :]))
                            dve.wait_ge(sems["bank_free"], sg["bank_free"].n + BANKS)
                            link(dve, dve.tensor_scalar(xr[:, b, :], q[:, 0:S], par[:, 0, b:b + 1], par[:, 4, b:b + 1],
                                                        ALU.mult, ALU.add))
                            for i in range(1, 4):
                                link(dve, dve.scalar_tensor_tensor(out=xr[:, b, :], in0=q[:, i:i + S],
                                                                   scalar=par[:, i, b:b + 1], in1=xr[:, b, :],
                                                                   op0=ALU.mult, op1=ALU.add))
                        for g in (2, 3):
                            for m in range(4):
                                evac(g, m, gt[:, 4 * (g - 2) + m, :])
                        for b in range(DB):
                            dve.wait_ge(sems["lru_r"], DB + b + 1)
                            link(dve, dve.tensor_tensor(i8[:, b, :], i8[:, b, :], xr[:, b, :], ALU.mult))
                        for b in range(DB):
                            dve.wait_ge(sems["lru_a"], b + 1)
                            if b >= 2:
                                pass
                            link(dve, dve.tensor_tensor(xr[:, b, :], r8[:, b, :], r8[:, b, :], ALU.mult))
                            sg["lru_b"].by(dve.scalar_tensor_tensor(out=t8[:, b, :], in0=xr[:, b, :], scalar=1.0,
                                                                    in1=t8[:, b, :], op0=ALU.add, op1=ALU.mult))
                        for b in range(DB):
                            dve.wait_ge(sems["gelu_done"], b + 1)
                            link(dve, dve.tensor_tensor(i8[:, b, :], i8[:, b, :], t8[:, b, :], ALU.mult))
                            link(dve, dve.tensor_tensor_scan(xr[:, b, :], r8[:, b, :], i8[:, b, :], 0.0, ALU.mult, ALU.add))
                            if b >= 2:
                                dve.wait_ge(sems["mix_lo"], b - 1)
                            sg["y_done"].by(dve.tensor_tensor(tmp[b % 2][:], xr[:, b, :], gt[:, b, :], ALU.mult))
                            dve.wait_ge(sems["mix_hi"], b + 1)
                            sg["mix_lo"].by(dve.tensor_tensor(hid_lo[:, b, :], tmp[b % 2][:], hid_hi[:, b, :].bitcast(F32),
                                                              ALU.subtract))
                    for b in range(DB):
                        g, m = GM + b // 4, b % 4
                        dve.wait_ge(sems["bank_ready"], HALF * g + m + 1)
                        sg["m_done"].by(dve.tensor_copy(acc[:, b, :], ps[:, HALF * (g % 2) + m, :]))
                        if m == 3:
                            dve.wait_ge(sems["m_done"], b + 1)
                            dve.sem_inc(sems["bank_free"], HALF)
                    norm_post_dve(dve, ab, gb(1), N0 + 1, N0)
                    dve.wait_ge(sems["xup"], DB * (N0 + 1))
                    norm_split_dve(dve, gb(2), N0 + 2, 1)
                    dve.wait_ge(sems["h_lo_done"], 2 * DB)

                    def gated(g, n, at_block, ready, free):
                        for m in range(2):
                            dve.wait_ge(sems["relu_ready"], n + m + 1)
                            dve.wait_ge(sems["bank_ready"], ready + m + 3)
                            dve.tensor_tensor(sq[m][:], ps[:, HALF * (g % 2) + 2 + m, :], tmp[m][:],
                                              ALU.mult).then_inc(sems["v_ready"], 1)
                        dve.wait_ge(sems["v_ready"], n + 2)
                        dve.sem_inc(sems["bank_free"], HALF)
                        for m in range(2):
                            dve.wait_ge(sems["hid_hi_done"], n + m + 1)
                            dve.tensor_tensor(hid_lo[:, at_block + m, :], sq[m][:], hid_hi[:, at_block + m, :].bitcast(F32),
                                              ALU.subtract).then_inc(sems["hid_lo_done"], 1)
                        dve.wait_ge(sems["hid_lo_done"], n + 2)

                    gated(GU, 0, 0, HALF * GU, None)
                    for b in range(DB):
                        g, m = GU + 1 + b // 4, b % 4
                        dve.wait_ge(sems["bank_ready"], HALF * g + m + 1)
                        dve.tensor_copy(acc[:, b, :], ps[:, HALF * (g % 2) + m, :]).then_inc(sems["bank_free"], 1)
                    with dve.Fori(0, CH) as c:
                        for j in range(2):
                            gated(G0 + j, 4 * c + (2 + 2 * j), 2 * j, GC * HALF * c + HALF * (G0 + j), None)
                        for b in range(DB):
                            j, m = 2 + b // 4, b % 4
                            dve.wait_ge(sems["bank_ready"], GC * HALF * c + (HALF * (G0 + j) + m + 1))
                            dve.tensor_tensor(acc[:, b, :], acc[:, b, :], ps[:, HALF * ((G0 + j) % 2) + m, :],
                                              ALU.add).then_inc(sems["bank_free"], 1)
                    dve.wait_ge(sems["bank_free"], BANKS + HALF * (G0 + GC * CH))
                    norm_post_dve(dve, ab, gb(3), N0 + 3, N0 + 1)

        if DEPTH2 > 0:
            second_layer(0)
            clear()
        if DEPTH2 > 1:
            second_layer(1)
            clear()

        fresh()
        with nc.Block() as block:
            @block.tensor
            def _(pe):
                for t in range(TB):
                    for k in range(DB):
                        mm = pe.transpose(ps[:, 2 * t + k // 4, (k % 4) * P:(k % 4 + 1) * P], x[:, k, t * P:(t + 1) * P], ident)
                    mm.then_inc(sems["x_T"], 1)

            @block.vector
            def _(dve):
                for t in range(TB):
                    dve.wait_ge(sems["x_T"], t + 1)
                    dve.tensor_copy(xin[:, t, :].rearrange("p (a b) -> p a b", b=512),
                                    ps[:, 2 * t:2 * t + 2, :]).then_inc(sems["x_copied"], 1)

            @block.sync
            def _(sp):
                for t in range(TB):
                    sp.wait_ge(sems["x_copied"], t + 1)
                    sp.dma_start(out[0, t * P:(t + 1) * P, :], xin[:, t, :]).then_inc(sems["stored"], 16)
                if "dbg" in a:
                    sp.dma_start(a["dbg"], x[:]).then_inc(sems["stored"], 16)
                sp.wait_ge(sems["stored"], 16 * (TB + (1 if "dbg" in a else 0)))


def kernel(**inputs):
    import concourse.bacc as bacc
    from concourse.bass_utils import run_bass_kernel_spmd

    nc = bacc.Bacc("TRN2", target_bir_lowering=False, num_devices=1)
    arrays, args = {}, {}
    tab, rtab, sel = shape_tables()
    for name, v in dict(inputs, tab=tab, rtab=rtab, sel=sel).items():
        v = np.ascontiguousarray(v)
        arrays[f"in_{name}"] = v
        args[name] = nc.dram_tensor(f"in_{name}", v.shape, mybir.dt.from_np(v.dtype), kind="ExternalInput").ap()
    out = nc.dram_tensor("out", (1, S, D), F32, kind="ExternalOutput").ap()
    build(nc, args, out)
    r = run_bass_kernel_spmd(nc, [arrays], core_ids=[0])
    return r.results[0]["out"]
```

```python
from contextlib import ExitStack
from itertools import chain

import numpy as np
import concourse.bass as bass
from concourse import mybir

F32 = mybir.dt.float32
F32R = mybir.dt.float32r
ALU = mybir.AluOpType
ACT = mybir.ActivationFunctionType

P = 128
S = 512
TB = S // P
D = 1024
DB = D // P
HD = 64
DEPTH = 2
DEPTH2 = 2
RET_H, DSA_H, DIL_H, FOX_H, IDX_H = 4, 4, 8, 8, 8
TOPK = min(256, S // 4)
D_FF = 4096
D_FF2 = 2816
POOL_W = (2, 4, 8, 16)
EPS = 1e-6
LRU_C = 8.0
SCALE = HD ** -0.5
NEG = -1e30
TAKEN = -3e38
C_RET, C_DSA = 0, 1024
C_DSAQ, C_CKV, C_QIDX, C_KIDX, C_WIDX = 1024, 1280, 1408, 1920, 1984
C_DIL = 1992
N_IN = 3528
KT = 4
RING = 2
BANKS = 8
HALF = 4

T_IDENT, T_ONES, T_MEAN, T_ROT, T_LOGC, T_CAUSAL, T_POOL = 0, 128, 256, 384, 512, 1024, 1536
T_SHARED = 1600
T_COS, T_SIN, T_DECAY = 0, 512, 1024
T_RET = 1024 + RET_H * S


def shape_tables():
    f = np.float32
    q = np.arange(P)[:, None]
    t = np.zeros((P, T_SHARED), f)
    t[:, T_IDENT:T_IDENT + P] = np.eye(P)
    t[:, T_ONES:T_ONES + P] = 1.0
    half = (np.arange(P)[:, None] // HD) == (np.arange(P)[None] // HD)
    t[:, T_MEAN:T_MEAN + P] = half / HD
    for m in range(P):
        if m % HD < HD // 2:
            t[m + HD // 2, T_ROT + m] = -1.0
        else:
            t[m - HD // 2, T_ROT + m] = 1.0
    dist = q - (np.arange(S)[None] - (S - P))
    count = ((dist >= 0) & (dist <= 128)).astype(int)
    for dil, in ((4,), (16,)):
        count = count + ((dist >= 0) & (dist % dil == 0)).astype(int)
    t[:, T_LOGC:T_LOGC + S] = np.where(count > 0, np.log(np.maximum(count, 1)) / SCALE, NEG)
    t[:, T_CAUSAL:T_CAUSAL + S] = np.where(dist >= 0, 0.0, NEG)
    for g, w in enumerate(POOL_W):
        t[:, T_POOL + 16 * g:T_POOL + 16 * g + 16] = 1.0 / np.minimum(np.arange(16) + 1, w)
    r = np.zeros((P, T_RET), f)
    inv = (f(10000.0) ** (-np.arange(HD // 2, dtype=f) / f(HD // 2))).astype(f)
    ang = np.arange(S, dtype=f)[None] * inv[np.arange(P) % (HD // 2)][:, None]
    r[:, T_COS:T_COS + S] = np.cos(ang.astype(np.float64))
    r[:, T_SIN:T_SIN + S] = np.sin(ang.astype(np.float64))
    diff = np.arange(S)[None] - q
    for h in range(RET_H):
        lg = np.log(1.0 - 2.0 ** (-5.0 - h))
        r[:, T_DECAY + h * S:T_DECAY + (h + 1) * S] = np.where(diff >= 0, np.exp(diff * lg), 0.0) * SCALE
    sel = np.zeros((FOX_H, FOX_H * P), f)
    for h in range(FOX_H):
        sel[h, h * P:(h + 1) * P] = 1.0
    return t, r, sel


class Signal:

    def __init__(self, sem):
        self.sem = sem
        self.n = 0

    def by(self, ins, k=1):
        ins.then_inc(self.sem, k)
        self.n += k
        return ins


def build(nc, a, out):
    ctx = ExitStack()
    with ctx:
        at = [16512]

        def place(name, shape, dt=F32, where=None):
            size = int(np.prod(shape[1:])) * 4
            off = where
            if where is None:
                off = at[0]
                at[0] += -(-size // 32) * 32
                assert at[0] <= 229368, (name, at[0])
            t = nc.alloc_sbuf_tensor_at(name, shape, dt, offset=off)
            t_off[name] = off
            return t

        t_off = {}
        x = place("x", [P, DB, S])
        h_hi, h_lo = place("h_hi", [P, DB, S], F32R), place("h_lo", [P, DB, S], F32R)
        hid_hi, hid_lo = place("hid_hi", [P, DB, S], F32R), place("hid_lo", [P, DB, S], F32R)
        raw = [place(f"raw{i}", [P, KT, 512]) for i in range(RING)]
        w_hi = [place(f"w_hi{i}", [P, KT, 512], F32R) for i in range(RING)]
        w_lo = [place(f"w_lo{i}", [P, KT, 512], F32R) for i in range(RING)]
        tab = place("tab", [P, T_SHARED])
        gains = place("gains", [P, 4, DB])
        sq = [place(f"sq{i}", [P, S]) for i in range(2)]
        rstd = place("rstd", [P, S])
        tmp = [place(f"tmp{i}", [P, S]) for i in range(2)]
        ssum = place("ssum", [P, S])
        p_more = place("p_more", [P, S])
        pT_more = place("pT_more", [P, S])
        stat = place("stat", [P, 4 * P])
        region = at[0]
        ident = tab[:, T_IDENT:T_IDENT + P]
        ones = tab[:, T_ONES:T_ONES + P]
        mean_m = tab[:, T_MEAN:T_MEAN + P]
        rot_m = tab[:, T_ROT:T_ROT + P]
        p_t = [place(f"p{i}", [P, S], where=t_off[n]) for i, n in enumerate(("sq0", "sq1", "ssum", "p_more"))]
        pT = [place(f"pT{i}", [P, TB, P], where=t_off[n]) for i, n in enumerate(("tmp0", "tmp1", "pT_more"))]
        post_t = [tmp[0], tmp[1], pT_more]
        on = place("on", [P, 8, HD], where=t_off["rstd"])
        sx, sn, sd, sr = (stat[:, 0:64], stat[:, 64:128], stat[:, 128:192], stat[:, 192:256])
        xin = place("xin", [P, TB, D], where=t_off["hid_hi"])

        ps = ctx.enter_context(nc.psum_tensor("ps", [P, BANKS, 512], F32))

        names = (
            "loaded0 loaded1 hi_split lo_split slot_used bank_ready bank_free consts small "
            "sq_ready sq_used ln_done rstd_ready normed h_hi_done h_lo_done "
            "dve_link act_link relu_ready hid_hi_done hid_lo_done v_ready "
            "idx_ready idx_relu idx_used kv_up kv_out ckv_in ckv_n ret_rot ret_rotd ret_s ret_p ret_o ret_hi ret_lo head_w head_w_T head_w_ready pool_hi pool_lo "
            "gn_in gn_mean gn_c gn_sq gn_var gn_rstd gn_out mix_hi mix_lo g_silu "
            "s_ready s_masked nmax p_ready pT_ready pT_copied pv_done o_norm oT_ready "
            "ssq_done post x_T x_copied stored f_in f_c f_done pool_in pool_mm pool_out bias_ready "
            "conv_done xi_done root_done lru_mm lru_r lru_t lru_a lru_b gelu_done y_done m_done xup").split()
        sems = {n: ctx.enter_context(nc.semaphore(n)) for n in names}
        sg = {}

        def fresh():
            for n in names:
                sg[n] = Signal(sems[n])

        class Slot:
            def __init__(self, pieces, rows):
                self.pieces, self.rows = pieces, rows
                self.width = sum(n for _, _, n in pieces)

        class Stream:

            def __init__(self):
                self.slots, self.groups = [], []
                self.need = [0, 0]
                self.landed = []

            def group(self, w, cols, tiles, r0=0):
                first = len(self.slots)
                done = 0
                for n in tiles:
                    pieces, c = [], 0
                    for (col, wid) in cols:
                        src = w[r0 + P * done:r0 + P * (done + n), col:col + wid]
                        pieces.append((src.rearrange("(k p) c -> p k c", p=P), c, wid))
                        c += wid
                    s = Slot(pieces, n)
                    r = len(self.slots) % RING
                    self.need[r] += 16 * len(pieces)
                    self.landed.append(self.need[r])
                    self.slots.append(s)
                    done += n
                self.groups.append((first, list(tiles)))

            def group_pairs(self, parts, tiles):
                first = len(self.slots)
                done = 0
                for n in tiles:
                    pieces, c = [], 0
                    for w, col, wid in parts:
                        src = w[P * done:P * (done + n), col:col + wid]
                        pieces.append((src.rearrange("(k p) c -> p k c", p=P), c, wid))
                        c += wid
                    self.need[len(self.slots) % RING] += 16 * len(pieces)
                    self.landed.append(self.need[len(self.slots) % RING])
                    self.slots.append(Slot(pieces, n))
                    done += n
                self.groups.append((first, list(tiles)))

            def used(self, s):
                for g, (first, tiles) in enumerate(self.groups):
                    if first <= s < first + len(tiles):
                        if s == first + len(tiles) - 1:
                            return "bank_ready", HALF * (g + 1)
                        before = sum(len(t) - 1 for _, t in self.groups[:g])
                        return "slot_used", before + s - first + 1

        def load_slot(sp, s, pieces, wait):
            if wait is not None:
                sp.wait_ge(sems["lo_split"], wait)
            for src, c, wid in pieces:
                sp.dma_start(raw[s % RING][:, 0:src.shape[1], c:c + wid], src).then_inc(
                    sems[f"loaded{s % RING}"], 16)

        def split_hi(act, s, rows, width, landed, used):
            act.wait_ge(sems[f"loaded{s % RING}"], landed)
            if used is not None:
                act.wait_ge(sems[used[0]], used[1])
            act.activation(w_hi[s % RING][:, 0:rows, 0:width], raw[s % RING][:, 0:rows, 0:width],
                           ACT.Copy).then_inc(sems["hi_split"], 1)

        def split_lo(pool, s, rows, width, count):
            pool.wait_ge(sems["hi_split"], count)
            pool.tensor_tensor(w_lo[s % RING][:, 0:rows, 0:width], raw[s % RING][:, 0:rows, 0:width],
                               w_hi[s % RING][:, 0:rows, 0:width].bitcast(F32),
                               ALU.subtract).then_inc(sems["lo_split"], 1)

        def stream_sp(sp, st):
            for s, slot in enumerate(st.slots):
                load_slot(sp, s, slot.pieces, s - RING + 1 if s >= RING else None)

        def stream_hi(act, st, s):
            if s < len(st.slots):
                slot = st.slots[s]
                split_hi(act, s, slot.rows, slot.width, st.landed[s], st.used(s - RING) if s >= RING else None)

        def stream_lo(pool, st, s0, s1):
            for s in range(s0, s1):
                slot = st.slots[s]
                split_lo(pool, s, slot.rows, slot.width, s + 1)

        def group_tiles(pe, g, s0, tiles, blocks, act_hi, act_lo, half, k0=0, ready=None, before=None):
            k_at = k0
            total = sum(tiles)
            nb = len({b[0] for b in blocks})
            freed = HALF * g if before is None else BANKS + HALF * before
            for i, nk in enumerate(tiles):
                s = s0 + i
                r = (i + s0_ring(s0)) % RING
                pe.wait_ge(sems["lo_split"], s + 1)
                last_slot = i == len(tiles) - 1

                def tile(m, k):
                    bank, c, n, tok, off = blocks[m]
                    kk = k_at + k
                    first, last = kk == k0, kk == k0 + total - 1
                    if first and off == 0:
                        pe.wait_ge(sems["bank_free"], freed + (bank + 1 if nb == HALF else HALF))
                    whi, wlo = w_hi[r][:, k, c:c + n], w_lo[r][:, k, c:c + n]
                    if tok is None:
                        o = ps[0:n, half * HALF + bank, :]
                        pairs = ((whi, act_hi[:, kk, :]), (whi, act_lo[:, kk, :]), (wlo, act_hi[:, kk, :]))
                    else:
                        t0 = tok * P
                        o = ps[:, half * HALF + bank, off:off + n]
                        ahi, alo = act_hi[:, kk, t0:t0 + P], act_lo[:, kk, t0:t0 + P]
                        pairs = ((ahi, whi), (ahi, wlo), (alo, whi))
                    for q, (lh, rh) in enumerate(pairs):
                        mm = pe.matmul(o, lh, rh, start=first and q == 0 and off == 0, stop=last and q == 2,
                                       skip_group_check=True)
                    if k < nk - 1:
                        return
                    if last_slot and m == len(blocks) - 1:
                        mm.then_inc(sems["bank_ready"], HALF - nb + 1)
                    elif last_slot and blocks[m + 1][0] != bank:
                        mm.then_inc(sems["bank_ready"], 1)
                    elif not last_slot and m == len(blocks) - 1:
                        mm.then_inc(sems["slot_used"], 1)

                if ready is None:
                    for m in range(len(blocks)):
                        for k in range(nk):
                            tile(m, k)
                            yield
                else:
                    for k in range(nk):
                        pe.wait_ge(sems[ready[0]], ready[1] + (k_at + k))
                        for m in range(len(blocks)):
                            tile(m, k)
                            yield
                k_at += nk

        def group(*args, **kw):
            for _ in group_tiles(*args, **kw):
                pass

        class Pace:

            def __init__(self, tiles, first, steps):
                self.tiles, self.first, self.steps = tiles, first, steps

            def upto(self, i):
                return max(0, min(self.tiles, -(-self.tiles * (i - self.first + 1) // self.steps)))

            def step_of(self, t):
                return next(i for i in range(self.first - 1, 100) if self.upto(i) >= t)

            def emit(self, i, tiles):
                for _ in range(self.upto(i) - self.upto(i - 1)):
                    next(tiles, None)

        ring_of = [0]

        def s0_ring(s0):
            return s0 % RING if isinstance(s0, int) else ring_of[0]

        FEAT = [(b, b * P, P, None, 0) for b in range(4)]

        lens = []

        def stats_act(act, src, n, scale, ready=None, between=()):
            used = sum(v - 1 for v in lens[:n])
            for k in range(lens[n]):
                if ready is not None:
                    act.wait_ge(sems[ready[0]], ready[1] + k)
                if k >= 3:
                    act.wait_ge(sems["sq_used"], used + k - 2)
                sg["sq_ready"].by(act.activation((sq[k % 2] if k else ssum)[:], src(k), ACT.Square))
            for f in between:
                f()
            alink(act, act.activation(spare[:], one[:], ACT.Ln))
            act.wait_ge(sems["ssq_done"], n + 1)
            sg["ln_done"].by(act.activation(rstd[:], ps[:, stats_bank[n], :], ACT.Ln, scale=scale, bias=eps_c))
            act.wait_ge(sems["ln_done"], sg["ln_done"].n)
            sg["rstd_ready"].by(act.activation(rstd[:], rstd[:], ACT.Exp, scale=-0.5))

        stats_bank = {}

        def stats_add(dve, n, k):
            if k == 0:
                return
            dve.wait_ge(sems["sq_ready"], sum(lens[:n]) + k + 1)
            if k >= 2:
                dve.wait_ge(sems["sq_used"], sum(v - 1 for v in lens[:n]) + k - 1)
            sg["sq_used"].by(dve.tensor_tensor(ssum[:], ssum[:], sq[k % 2][:], ALU.add))

        def stats_pe(pe, n, bank):
            stats_bank[n] = bank
            if lens[n] == 1:
                pe.wait_ge(sems["sq_ready"], sum(lens[:n]) + 1)
            else:
                pe.wait_ge(sems["sq_used"], sum(v - 1 for v in lens[:n + 1]))
            pe.matmul(ps[:, bank, :], ones, ssum[:], start=True, stop=True).then_inc(sems["ssq_done"], 1)

        def norm_split_dve(dve, gain, n, m):
            if n is not None:
                dve.wait_ge(sems["rstd_ready"], n + 1)

            def scaled(k):
                if k >= 2:
                    dve.wait_ge(sems["h_lo_done"], DB * m + k - 1)
                sg["normed"].by(dve.scalar_tensor_tensor(out=tmp[k % 2][:], in0=x[:, k, :], scalar=gain(k),
                                                         in1=rstd[:], op0=ALU.mult, op1=ALU.mult))

            scaled(0)
            for k in range(DB):
                if k + 1 < DB:
                    scaled(k + 1)
                dve.wait_ge(sems["h_hi_done"], DB * m + k + 1)
                sg["h_lo_done"].by(dve.tensor_tensor(h_lo[:, k, :], tmp[k % 2][:], h_hi[:, k, :].bitcast(F32),
                                                     ALU.subtract))

        def norm_split_act(act, m):
            for k in range(DB):
                act.wait_ge(sems["normed"], DB * m + k + 1)
                sg["h_hi_done"].by(act.activation(h_hi[:, k, :], tmp[k % 2][:], ACT.Copy))

        def norm_post(dve, src, gain, n, m, n_next=None, x0=0):
            dve.wait_ge(sems["rstd_ready"], n + 1)
            for k in range(DB + 2):
                if k < DB:
                    if k >= 3:
                        dve.wait_ge(sems["xup"], x0 + DB * m + k - 2)
                    sg["post"].by(dve.scalar_tensor_tensor(out=post_t[k % 3][:], in0=src(k), scalar=gain(k),
                                                           in1=rstd[:], op0=ALU.mult, op1=ALU.mult))
                if n_next is not None and k >= 2:
                    stats_add(dve, n_next, k - 2)

        def norm_post_pool(pool, m):
            for k in range(DB):
                pool.wait_ge(sems["post"], DB * m + k + 1)
                sg["xup"].by(pool.tensor_tensor(x[:, k, :], x[:, k, :], post_t[k % 3][:], ALU.add))

        def link(dve, ins):
            sg["dve_link"].by(ins)
            dve.wait_ge(sems["dve_link"], sg["dve_link"].n)

        def alink(act, ins):
            sg["act_link"].by(ins)
            act.wait_ge(sems["act_link"], sg["act_link"].n)

        class Attention:

            def __init__(self, heads, q, k, v, bias, mix0, u0, b0, decay=None):
                self.H, self.q, self.k, self.v, self.bias = heads, q, k, v, bias
                self.mix0, self.u0, self.b0, self.decay = mix0, u0, b0, decay
                self.units = [(qb, h) for qb in range(TB) for h in range(heads)]

            SB, PB, TS = 2, 4, 3
            TURN, VAL = 3, 5

            def scores(self, pe, i):
                qb, h = self.units[i]
                u = self.u0 + i
                n = (qb + 1) * P
                if i >= self.SB:
                    pe.wait_ge(sems["s_masked"], u - self.SB + 1)
                p0 = HD * (h % 2)
                o = ps[:, i % self.SB, 0:n]
                mm = pe.matmul(o, self.q[p0:p0 + HD, h // 2, qb * P:(qb + 1) * P],
                               self.k[p0:p0 + HD, h // 2, 0:n], start=True, stop=self.decay is None)
                if self.decay is not None:
                    sel, negc = self.decay
                    mm = pe.matmul(o, sel[:, h * P:(h + 1) * P], negc[:, 0:n], start=False, stop=True)
                mm.then_inc(sems["s_ready"], 1)

            def turn(self, pe, i):
                qb, h = self.units[i]
                u = self.u0 + i
                pe.wait_ge(sems["p_ready"], u + 1)
                if i >= 1:
                    pe.wait_ge(sems["pT_copied"], u)
                if self.backs:
                    pe.wait_ge(sems["mix_lo"], self.l0 + self.backs)
                for kb in range(qb + 1):
                    mm = pe.transpose(ps[:, 2, kb * P:(kb + 1) * P],
                                      p_t[i % self.PB][:, kb * P:(kb + 1) * P], ident)
                mm.then_inc(sems["pT_ready"], 1)

            def values(self, pe, i):
                qb, h = self.units[i]
                u = self.u0 + i
                pe.wait_ge(sems["pT_copied"], u + 1)
                if h == 0 and qb >= 1:
                    pe.wait_ge(sems["o_norm"], self.b0 + qb)
                for kb in range(qb + 1):
                    mm = pe.matmul(ps[:, 3, h * HD:(h + 1) * HD], pT[i % self.TS][:, kb, :],
                                   self.v[:, kb, h * HD:(h + 1) * HD], start=kb == 0, stop=kb == qb,
                                   skip_group_check=True)
                mm.then_inc(sems["pv_done"], 1)

            def back(self, pe, qb, turned):
                pe.wait_ge(sems["o_norm"], self.b0 + qb + 1)
                pe.wait_ge(sems["pT_copied"], self.u0 + turned)
                for j in range(self.H // 2):
                    mm = pe.transpose(ps[:, 2, j * P:(j + 1) * P],
                                      on[:, 2 * j:2 * j + 2, :].rearrange("p a b -> p (a b)"), ident)
                mm.then_inc(sems["oT_ready"], 1)
                self.backs += 1

            def at_end(self, i, lag):
                j = i - lag
                return j // self.H if 0 <= j < len(self.units) and j % self.H == self.H - 1 else None

            def steps(self):
                return len(self.units) + self.VAL + 3

            def tensor(self, pe, l0, beside):
                self.l0, self.backs = l0, 0
                n = len(self.units)
                for i in range(self.steps()):
                    if i < n:
                        self.scores(pe, i)
                    if self.TURN <= i < n + self.TURN:
                        self.turn(pe, i - self.TURN)
                    beside(i)
                    if self.VAL <= i < n + self.VAL:
                        self.values(pe, i - self.VAL)
                    qb = self.at_end(i, self.VAL + 2)
                    if qb is not None:
                        self.back(pe, qb, min(n, i - self.TURN + 1))

            def mask(self, dve, i):
                qb, h = self.units[i]
                u = self.u0 + i
                w = (qb + 1) * P
                dve.wait_ge(sems["s_ready"], u + 1)
                if i >= self.PB:
                    dve.wait_ge(sems["pT_ready"], u - self.PB + 1)
                sg["s_masked"].by(dve.tensor_tensor_reduce(
                    out=p_t[i % self.PB][:, 0:w], in0=ps[:, i % self.SB, 0:w], in1=self.bias(qb), scale=1.0,
                    scalar=TAKEN, op0=ALU.add, op1=ALU.max, accum_out=sx[:, i:i + 1]))

            def negate(self, dve, i):
                dve.wait_ge(sems["s_masked"], self.u0 + i + 1)
                sg["nmax"].by(dve.tensor_scalar(sn[:, i:i + 1], sx[:, i:i + 1], -SCALE, None, ALU.mult))

            def vector(self, dve, l0, beside):
                n = len(self.units)
                for i in range(self.steps()):
                    if i < n:
                        self.mask(dve, i)
                        self.negate(dve, i)
                    qb = self.at_end(i, self.VAL)
                    if qb is not None:
                        dve.wait_ge(sems["pv_done"], self.u0 + (qb + 1) * self.H)
                        if qb >= 1:
                            dve.wait_ge(sems["oT_ready"], self.b0 + qb)
                        a0, a1 = qb * self.H, (qb + 1) * self.H
                        link(dve, dve.reciprocal(sr[:, a0:a1], sd[:, a0:a1]))
                        sg["o_norm"].by(dve.tensor_tensor(
                            on[:, 0:self.H, :],
                            ps[:, 3, 0:self.H * HD].rearrange("p (h d) -> p h d", d=HD),
                            sr[:, a0:a1].unsqueeze(2).to_broadcast([P, self.H, HD]), ALU.mult))
                    qb = self.at_end(i, self.VAL + 2)
                    if qb is not None:
                        dve.wait_ge(sems["mix_hi"], l0 + qb + 1)
                        hb = self.H // 2
                        sl = (slice(None), slice(self.mix0, self.mix0 + hb), slice(qb * P, (qb + 1) * P))
                        sg["mix_lo"].by(dve.tensor_tensor(
                            hid_lo[sl], ps[:, 2, 0:hb * P].rearrange("p (a b) -> p a b", b=P),
                            hid_hi[sl].bitcast(F32), ALU.subtract))
                    beside(i)

            def scalar(self, act, l0, beside):
                n = len(self.units)
                for i in range(self.steps()):
                    if i < n:
                        qb, h = self.units[i]
                        u = self.u0 + i
                        w = (qb + 1) * P
                        act.wait_ge(sems["nmax"], u + 1)
                        sg["p_ready"].by(act.activation(p_t[i % self.PB][:, 0:w], p_t[i % self.PB][:, 0:w], ACT.Exp,
                                                        bias=sn[:, i:i + 1], scale=SCALE, accum_out=sd[:, i:i + 1]))
                    j = i - self.TURN
                    if 0 <= j < n:
                        qb, h = self.units[j]
                        u = self.u0 + j
                        act.wait_ge(sems["pT_ready"], u + 1)
                        if j >= self.TS:
                            act.wait_ge(sems["pv_done"], u - self.TS + 1)
                        sg["pT_copied"].by(act.activation(
                            pT[j % self.TS][:, 0:qb + 1, :].rearrange("p a b -> p (a b)"),
                            ps[:, 2, 0:(qb + 1) * P], ACT.Copy))
                    qb = self.at_end(i, self.VAL + 2)
                    if qb is not None:
                        hb = self.H // 2
                        act.wait_ge(sems["oT_ready"], self.b0 + qb + 1)
                        sg["mix_hi"].by(act.activation(
                            hid_hi[:, self.mix0:self.mix0 + hb, qb * P:(qb + 1) * P],
                            ps[:, 2, 0:hb * P].rearrange("p (a b) -> p a b", b=P), ACT.Copy))
                    beside(i)

        def causal(qb):
            return tab[:, T_CAUSAL + S - P - qb * P:T_CAUSAL + S]

        def logc(qb):
            return tab[:, T_LOGC + S - P - qb * P:T_LOGC + S]

        def clear():
            nc.all_engine_barrier()
            ids = sorted(s.num for s in sems.values())
            assert ids == list(range(ids[0], ids[0] + len(ids)))
            nc.sync.sem_clear(range(ids[0], ids[-1] + 1))
            nc.all_engine_barrier()

        def gain_view(v):
            return v.rearrange("(k p) -> p k", p=P)

        eps_c = place("eps", [P, 1])[:, 0:1]
        one, spare = place("one", [P, 1]), place("spare", [P, 1])
        region = at[0]

        fresh()
        lens[:] = [DB]
        with nc.Block() as block:
            @block.sync
            def _(sp):
                sp.dma_start(xin[:], a["x"][0].rearrange("(t p) d -> p t d", p=P)).then_inc(sems["small"], 16)
                sp.dma_start(tab[:], a["tab"]).then_inc(sems["consts"], 16)

            @block.tensor
            def _(pe):
                pe.wait_ge(sems["small"], 16)
                pe.wait_ge(sems["consts"], 16)
                for k in range(DB):
                    for t in range(TB):
                        mm = pe.transpose(ps[:, k, t * P:(t + 1) * P], xin[:, t, k * P:(k + 1) * P], ident)
                    mm.then_inc(sems["x_T"], 1)
                stats_pe(pe, 0, 0)

            @block.scalar
            def _(act):
                stats_bank[0] = 0
                stats_act(act, lambda k: x[:, k, :], 0, 1.0 / D, ready=("x_copied", 2))

            @block.vector
            def _(dve):
                dve.memset(one[:], 1.0)
                dve.memset(eps_c, EPS).then_inc(sems["x_copied"], 1)
                for k in range(DB):
                    dve.wait_ge(sems["x_T"], k + 1)
                    dve.tensor_copy(x[:, k, :], ps[:, k, :]).then_inc(sems["x_copied"], 1)
                    if k >= 1:
                        stats_add(dve, 0, k - 1)
                stats_add(dve, 0, DB - 1)
        clear()

        def first_layer(L):
            fresh()
            at[0] = region
            dsaq = place("dsaq", [P, 2, S])
            dil_q, dil_k = place("dil_q", [P, 4, S]), place("dil_k", [P, 4, S])
            dil_v = place("dil_v", [P, TB, 512])
            dsa_k, dsa_v = place("dsa_k", [P, 2, S]), place("dsa_v", [P, TB, 256])
            sc = [None] + [place(f"sc{q}", [P, (q + 1) * P]) for q in range(1, TB)]
            w_uk, w_uv = place("w_uk", [P, 256]), place("w_uv", [P, 256])
            widx = place("widx", [P, TB, IDX_H])
            top8 = place("top8", [P, 8])
            head_w = stat[0:IDX_H, :]
            q_idx = place("q_idx", [P, 4, S], where=t_off["hid_hi"] + 4 * 2048)
            retqk = place("retqk", [P, 4, S])
            retv = place("retv", [P, TB, 256], where=t_off["hid_hi"])
            gate = place("gate", [P, 2, S], where=t_off["hid_lo"])
            ckv = place("ckv", [P, S], where=t_off["hid_lo"] + 2 * 2048)
            kk = place("kk", [P, S], where=t_off["hid_lo"] + 3 * 2048)
            rl = p_t
            rtab = place("rtab", [P, T_RET], where=t_off["h_hi"])
            st_b = [place(f"ret_st{i}", [P, S], where=t_off["h_lo"] + i * 2048) for i in range(4)]
            gn = [place(f"gn{i}", [P, S], where=t_off["h_lo"] + (4 + i) * 2048) for i in range(2)]

            lens[:] = [1, DB, DB]
            w_in = a["w_in"][L]
            st = Stream()
            kv = [KT, KT]
            st.group(w_in, [(C_CKV, P), (C_KIDX, HD), (C_KIDX, HD), (C_WIDX, IDX_H)], kv)
            st.group(w_in, [(C_QIDX, 512)], kv)
            st.group(w_in, [(C_DIL, 512)], kv)
            st.group(w_in, [(C_DIL + 512, 512)], kv)
            st.group(w_in, [(C_DIL + 1024, 512)], kv)
            st.group(w_in, [(C_DSAQ, 256), (C_RET + 768, 256)], kv)
            st.group(w_in, [(C_RET, 512)], kv)
            st.group(w_in, [(C_RET + 512, 256)], kv)
            G_MIX = len(st.groups)
            for r0 in (512, 0):
                st.group(a["w_out"][L], [(0, 512)], [KT], r0=r0)
                st.group(a["w_out"][L], [(512, 512)], [KT], r0=r0)
            beside_groups = range(2, G_MIX + 2)

            def half_of(g):
                return 1 if g in beside_groups else g % 2

            def before(g):
                return next((p for p in range(g - 1, -1, -1) if half_of(p) == half_of(g)), None)
            G0, S0 = len(st.groups), len(st.slots)
            U0 = sum(len(t) - 1 for _, t in st.groups)
            CH = D_FF // D
            land0 = list(st.need)
            TOK = lambda n: [(t, 0, n, t, 0) for t in range(TB)]
            dil = Attention(DIL_H, dil_q, dil_k, dil_v, logc, 4, 0, 0)
            dsa = Attention(DSA_H, dsaq, dsa_k, dsa_v,
                            lambda q: causal(q) if q == 0 else sc[q][:], 2, TB * DIL_H, TB)
            idx_pace = Pace(2 * 32, 0, 24)
            dil_pace = Pace(3 * 32, 0, dil.steps() - 3)
            out_a, out_b = Pace(16, 0, 4), Pace(16, 19, 5)
            ROT, RET, GN = 5, 8, 17
            units = [(qb, h) for qb in range(1, TB) for h in range(IDX_H)]

            with nc.Block() as block:
                @block.sync
                def _(sp):
                    for i, n in enumerate(("attn_norm_w", "mlp_norm_w")):
                        sp.dma_start(gains[:, i, :], gain_view(a[n][L]), allow_slow_non_contiguous=True).then_inc(sems["small"], 16)
                    sp.dma_start(gains[:, 2, 0:2], a["ret_norm_w"][L].rearrange("(b h) d -> (h d) b", h=2), allow_slow_non_contiguous=True).then_inc(sems["small"], 16)
                    sp.dma_start(gains[:, 2, 2:3], a["dsa_kv_norm_w"][L].rearrange("(p o) -> p o", o=1), allow_slow_non_contiguous=True).then_inc(sems["small"], 16)
                    load_slot(sp, 0, st.slots[0].pieces, None)
                    load_slot(sp, 1, st.slots[1].pieces, None)
                    sp.dma_start(w_uk[:], a["dsa_w_uk"][L]).then_inc(sems["consts"], 16)
                    sp.dma_start(w_uv[:], a["dsa_w_uv"][L]).then_inc(sems["consts"], 16)
                    for s in range(2, len(st.slots)):
                        load_slot(sp, s, st.slots[s].pieces, s - RING + 1)
                        if s == 2 * G_MIX + 1:
                            sp.wait_ge(sems["bank_ready"], HALF * G_MIX)
                            sp.dma_start(rtab[:], a["rtab"]).then_inc(sems["consts"], 16)
                    with sp.Fori(0, CH) as c:
                        for j in range(8):
                            col = 512 * (j % 4 // 2)
                            if j < 4:
                                src = a["w_up"][L, 512 * (j % 2):512 * (j % 2) + 512, bass.ds(D * c + col, 512)]
                            else:
                                src = a["w_down"][L, bass.ds(D * c + 512 * (j % 2), 512), col:col + 512]
                            load_slot(sp, j, [(src.rearrange("(k p) c -> p k c", p=P), 0, 512)],
                                      8 * c + S0 + j - RING + 1)

                @block.gpsimd
                def _(pool):
                    stream_lo(pool, st, 0, len(st.slots))
                    with pool.Fori(0, CH) as c:
                        for j in range(8):
                            split_lo(pool, j, KT, 512, 8 * c + S0 + j + 1)

                @block.tensor
                def _(pe):
                    def tiles_of(g, blocks, hi=h_hi, lo=h_lo, ready=None, k0=0):
                        first, tiles = st.groups[g]
                        return group_tiles(pe, g, first, tiles, blocks, hi, lo, half_of(g), k0, ready=ready,
                                           before=before(g))

                    def grp(*args, **kw):
                        for _ in tiles_of(*args, **kw):
                            pass

                    pe.sem_inc(sems["bank_free"], BANKS)
                    grp(0, [(0, 0, P, None, 0), (1, P, P, None, 0), (2, 2 * P, IDX_H, None, 0)],
                        ready=("h_lo_done", 1))
                    grp(1, FEAT)
                    tiles = chain(tiles_of(2, FEAT), tiles_of(3, FEAT))
                    pe.wait_ge(sems["bank_free"], BANKS + HALF)
                    stats_pe(pe, 0, 3)
                    pe.wait_ge(sems["head_w"], 1)
                    for t in range(TB):
                        mm = pe.transpose(ps[:, 2, t * IDX_H:(t + 1) * IDX_H], head_w[:, t * P:(t + 1) * P],
                                          ident[0:IDX_H, 0:IDX_H])
                    mm.then_inc(sems["head_w_T"], 1)
                    for i, (qb, h) in enumerate(units):
                        idx_pace.emit(i, tiles)
                        if i == 2:
                            pe.wait_ge(sems["head_w_ready"], 1)
                        if i == 0:
                            pe.wait_ge(sems["bank_free"], BANKS + 2 * HALF)
                        if i >= 3:
                            pe.wait_ge(sems["idx_relu"], i - 2)
                        p0 = HD * (h % 2)
                        pe.matmul(ps[:, i % 3, 0:(qb + 1) * P], q_idx[p0:p0 + HD, h // 2, qb * P:(qb + 1) * P],
                                  kk[p0:p0 + HD, 0:(qb + 1) * P], start=True, stop=True).then_inc(sems["idx_ready"], 1)
                    tiles = tiles_of(4, TOK(512))
                    for _ in range(16):
                        next(tiles)
                    pe.wait_ge(sems["idx_relu"], len(units))
                    pe.wait_ge(sems["ckv_n"], 1)
                    pe.wait_ge(sems["consts"], 16 * 2)
                    for j in range(2):
                        pe.matmul(ps[:, j, :], w_uk[:, j * P:(j + 1) * P], ckv[:], start=True,
                                  stop=True).then_inc(sems["kv_up"], 1)
                    for t in range(TB):
                        pe.matmul(ps[:, 2 + t // 2, 256 * (t % 2):256 * (t % 2) + 256], ckv[:, t * P:(t + 1) * P],
                                  w_uv[:], start=True, stop=True, skip_group_check=True).then_inc(sems["kv_up"], 1)
                    for _ in tiles:
                        pass
                    pe.wait_ge(sems["kv_out"], 4)
                    pe.wait_ge(sems["bank_free"], BANKS + HALF * 5)
                    tiles = chain(tiles_of(5, FEAT), tiles_of(6, FEAT), tiles_of(7, TOK(256)))
                    dil.tensor(pe, 0, lambda i: dil_pace.emit(i, tiles))
                    pe.wait_ge(sems["mix_lo"], TB)
                    pe.wait_ge(sems["bias_ready"], 3)
                    tiles_a = tiles_of(G_MIX, FEAT, hid_hi, hid_lo, k0=KT)
                    tiles_b = tiles_of(G_MIX + 1, FEAT, hid_hi, hid_lo, k0=KT)
                    ru = [(h, kb) for h in range(RET_H) for kb in range(TB)]

                    def retention(i):
                        out_a.emit(i, tiles_a)
                        if i == ROT:
                            pe.wait_ge(sems["bank_free"], BANKS + HALF * (G_MIX + 1))
                        if ROT <= i < ROT + 2:
                            for j in (2 * (i - ROT), 2 * (i - ROT) + 1):
                                pe.matmul(ps[:, 4 + j, :], rot_m, retqk[:, j, :], start=True,
                                          stop=True).then_inc(sems["ret_rot"], 1)
                        if i == RET:
                            pe.wait_ge(sems["ret_rotd"], 4)
                        for u in (2 * (i - RET), 2 * (i - RET) + 1):
                            if 0 <= u < len(ru):
                                h, kb = ru[u]
                                p0, w = HD * (h % 2), S - kb * P
                                if u >= 2:
                                    pe.wait_ge(sems["ret_p"], u - 1)
                                pe.matmul(ps[:, 4 + u % 2, 0:w], retqk[p0:p0 + HD, 2 + h // 2, kb * P:(kb + 1) * P],
                                          retqk[p0:p0 + HD, h // 2, kb * P:S], start=True,
                                          stop=True).then_inc(sems["ret_s"], 1)
                        for u in (2 * (i - RET) - 2, 2 * (i - RET) - 1):
                            if 0 <= u < len(ru):
                                h, kb = ru[u]
                                p0, w = HD * (h % 2), S - kb * P
                                pe.wait_ge(sems["ret_p"], u + 1)
                                pe.matmul(ps[p0:p0 + HD, 6 + h // 2, kb * P:S], retv[:, kb, h * HD:(h + 1) * HD],
                                          st_b[u % 4][:, 0:w], start=kb == 0, stop=kb == TB - 1,
                                          skip_group_check=True).then_inc(sems["ret_o"], 1)
                        for j in range(2):
                            if i == GN:
                                pe.wait_ge(sems["gn_in"], j + 1)
                                pe.matmul(ps[:, 4 + j, :], mean_m, gn[j][:], start=True,
                                          stop=True).then_inc(sems["gn_mean"], 1)
                            if i == GN + 1:
                                pe.wait_ge(sems["gn_sq"], j + 1)
                                pe.matmul(ps[:, 6 + j, :], mean_m, st_b[j][:], start=True,
                                          stop=True).then_inc(sems["gn_var"], 1)
                        if i == GN + 2:
                            pe.wait_ge(sems["gn_rstd"], 2)
                        out_b.emit(i, tiles_b)

                    dsa.tensor(pe, TB, retention)
                    pe.wait_ge(sems["mix_lo"], 2 * TB)
                    pe.wait_ge(sems["ret_lo"], 2)
                    grp(G_MIX + 2, FEAT, hid_hi, hid_lo)
                    grp(G_MIX + 3, FEAT, hid_hi, hid_lo)
                    pe.wait_ge(sems["bank_free"], BANKS + HALF * (G0 - 1))
                    stats_pe(pe, 1, HALF * (G0 % 2))
                    with pe.Fori(0, CH) as c:
                        for j in range(4):
                            ring_of[0] = 0
                            ready = {0: ("h_lo_done", DB + 1), 2: ("hid_lo_done", 8 * c + 1)}.get(j)
                            group(pe, 4 * c + (G0 + j), 8 * c + (S0 + 2 * j), kv, FEAT,
                                  *((h_hi, h_lo) if j < 2 else (hid_hi, hid_lo)), (G0 + j) % 2, ready=ready)
                    pe.wait_ge(sems["bank_free"], BANKS + HALF * (G0 + 4 * CH - 1))
                    stats_pe(pe, 2, HALF * (G0 % 2))

                @block.scalar
                def _(act):
                    stream_hi(act, st, 0)
                    stream_hi(act, st, 1)
                    norm_split_act(act, 0)
                    stream_hi(act, st, 2)
                    stream_hi(act, st, 3)
                    stream_hi(act, st, 4)
                    act.wait_ge(sems["ckv_in"], 1)
                    stats_bank[0] = 3
                    stats_act(act, lambda k: ckv[:], 0, 1.0 / P)
                    stream_hi(act, st, 5)

                    def hi_beside(i, pace, s0, slots):
                        for s in slots:
                            if pace.step_of(16 * (s - s0 - 1)) == i:
                                stream_hi(act, st, s)

                    for i, (qb, h) in enumerate(units):
                        act.wait_ge(sems["idx_ready"], i + 1)
                        if i >= 2:
                            act.wait_ge(sems["idx_used"], i - 1)
                        else:
                            act.wait_ge(sems["ckv_n"], 1)
                        sg["idx_relu"].by(act.activation(rl[i % 2][:, 0:(qb + 1) * P],
                                                         ps[:, i % 3, 0:(qb + 1) * P], ACT.Relu))
                        hi_beside(i, idx_pace, 4, range(6, 9))
                    for s in range(9, 12):
                        stream_hi(act, st, s)

                    def beside_dil(i):
                        hi_beside(i, dil_pace, 10, range(12, 17))
                        if i == len(dil.units) + 1:
                            act.wait_ge(sems["bank_free"], BANKS + HALF * 6)
                            alink(act, act.activation(gate[:], gate[:], ACT.Silu))

                    dil.scalar(act, 0, beside_dil)
                    stream_hi(act, st, 17)

                    def retention(i):
                        if i == 4:
                            stream_hi(act, st, 18)
                        for j in range(2):
                            if i == GN:
                                act.wait_ge(sems["gn_c"], j + 1)
                                sg["gn_sq"].by(act.activation(st_b[j][:], gn[j][:], ACT.Square))
                            if i == GN + 1:
                                act.wait_ge(sems["gn_var"], j + 1)
                                alink(act, act.activation(st_b[j][:], ps[:, 6 + j, :], ACT.Ln, bias=eps_c))
                        for j in range(2):
                            if i == GN + 1:
                                sg["gn_rstd"].by(act.activation(st_b[j][:], st_b[j][:], ACT.Exp, scale=-0.5))
                            if i == GN + 2:
                                act.wait_ge(sems["gn_out"], j + 1)
                                sg["ret_hi"].by(act.activation(hid_hi[:, j, :], gn[j][:], ACT.Copy))

                    dsa.scalar(act, TB, retention)
                    stream_hi(act, st, 19)

                    def hi(c, j):
                        if j % 2 == 0:
                            used = ("slot_used", 4 * c + (U0 + j // 2)) if not isinstance(c, int) else ("slot_used", 4 * c + U0 + j // 2)
                        else:
                            used = ("bank_ready", 16 * c + HALF * (G0 + j // 2))
                        split_hi(act, j, KT, 512, 64 * c + (land0[j % 2] + 16 * (j // 2 + 1)), used)

                    split_hi(act, 0, KT, 512, land0[0] + 16, ("bank_ready", HALF * (G0 - 1)))
                    stats_bank[1] = stats_bank[2] = HALF * (G0 % 2)
                    stats_act(act, lambda k: x[:, k, :], 1, 1.0 / D, ready=("bank_free", BANKS + HALF * (G0 - 2) + 1),
                              between=[lambda: hi(0, 1)])
                    norm_split_act(act, 1)

                    def chunk(c, last):
                        for j in range(4):
                            hi_a = not (last and j == 3)
                            if hi_a:
                                hi(c, 2 * j + 2)
                            if j < 2:
                                for m in range(4):
                                    n_in = 4 * j + m
                                    n = 8 * c + n_in
                                    act.wait_ge(sems["bank_ready"], 16 * c + (HALF * (G0 + j) + m + 1))
                                    act.wait_ge(sems["bank_free"], 16 * c + (HALF * (G0 + j) + m + 7))
                                    if n_in >= 2:
                                        act.wait_ge(sems["hid_hi_done"], 8 * c + (n_in - 1))
                                    act.activation(tmp[m % 2][:], ps[:, HALF * ((G0 + j) % 2) + m, :],
                                                   ACT.Relu).then_inc(sems["relu_ready"], 1)
                                    act.wait_ge(sems["relu_ready"], n + 1)
                                    act.activation(hid_hi[:, 4 * j + m, :], tmp[m % 2][:],
                                                   ACT.Square).then_inc(sems["hid_hi_done"], 1)
                            if hi_a:
                                hi(c, 2 * j + 3)

                    with act.Fori(0, CH - 1) as c:
                        chunk(c, False)
                    chunk(CH - 1, True)
                    stats_act(act, lambda k: x[:, k, :], 2, 1.0 / D,
                              ready=("bank_free", BANKS + HALF * (G0 + 4 * CH - 2) + 1))

                @block.vector
                def _(dve):
                    dve.wait_ge(sems["small"], 16 * 4)
                    norm_split_dve(dve, lambda k: gains[:, 0, k:k + 1], None, 0)

                    def evac(g, m, o, width=512):
                        dve.wait_ge(sems["bank_ready"], HALF * g + m + 1)
                        sg["bank_free"].by(dve.tensor_copy(o, ps[:, HALF * half_of(g) + m, 0:width]))

                    dve.wait_ge(sems["bank_ready"], HALF)
                    sg["bank_free"].by(dve.tensor_copy(kk[:], ps[:, 1, :]))
                    sg["ckv_in"].by(dve.tensor_copy(ckv[:], ps[:, 0, :]))
                    dve.wait_ge(sems["ckv_in"], 1)
                    sg["head_w"].by(dve.tensor_scalar(head_w, ps[0:IDX_H, 2, :], IDX_H ** -0.5 * HD ** -0.5, None,
                                                      ALU.mult))
                    dve.wait_ge(sems["head_w"], 1)
                    dve.sem_inc(sems["bank_free"], 3)
                    sg["bank_free"].n += 3
                    for m in range(4):
                        evac(1, m, q_idx[:, m, :])
                    dve.wait_ge(sems["head_w_T"], 1)
                    sg["head_w_ready"].by(dve.tensor_copy(widx[:].rearrange("p a b -> p (a b)"), ps[:, 2, 0:TB * IDX_H]))
                    dve.wait_ge(sems["rstd_ready"], 1)
                    sg["ckv_n"].by(dve.scalar_tensor_tensor(out=ckv[:], in0=ckv[:], scalar=gains[:, 2, 2:3],
                                                            in1=rstd[:], op0=ALU.mult, op1=ALU.mult))

                    def evac_beside(i, pace, outs):
                        for n, (g, m, o, width) in enumerate(outs):
                            if pace.step_of(32 * (n // 4) + 16 + 4 * (m + 1)) + 1 == i:
                                evac(g, m, o, width)

                    idx_outs = [(g, m, t[:, m, :], 512) for g, t in ((2, dil_q), (3, dil_k)) for m in range(4)]
                    dve.wait_ge(sems["head_w_ready"], 1)
                    for i, (qb, h) in enumerate(units):
                        w = (qb + 1) * P
                        dve.wait_ge(sems["idx_relu"], i + 1)
                        wt = widx[:, qb, h:h + 1]
                        if h == 0:
                            sg["idx_used"].by(dve.tensor_scalar(sc[qb][:], rl[i % 2][:, 0:w], wt, None, ALU.mult))
                        else:
                            dve.wait_ge(sems["idx_used"], i)
                            sg["idx_used"].by(dve.scalar_tensor_tensor(out=sc[qb][:], in0=rl[i % 2][:, 0:w], scalar=wt,
                                                                       in1=sc[qb][:], op0=ALU.mult, op1=ALU.add))
                        evac_beside(i, idx_pace, idx_outs)
                    evac_beside(len(units), idx_pace, idx_outs)
                    dve.wait_ge(sems["idx_used"], len(units))
                    for qb in range(1, TB):
                        sg["dve_link"].by(dve.tensor_tensor(sc[qb][:], sc[qb][:], causal(qb), ALU.add))
                    dve.wait_ge(sems["dve_link"], sg["dve_link"].n)
                    rounds = [(qb, r) for r in range(TOPK // 8) for qb in range(1, TB)]

                    def take(n):
                        for _ in range(min(n, len(rounds))):
                            qb, r = rounds.pop(0)
                            link(dve, dve.max(top8[:], sc[qb][:]))
                            link(dve, dve.match_replace(sc[qb][:], top8[:], sc[qb][:], TAKEN))

                    take(6)
                    dve.wait_ge(sems["kv_up"], 2)
                    sg["kv_out"].by(dve.tensor_copy(dsa_k[:, 0, :], ps[:, 0, :]))
                    sg["kv_out"].by(dve.tensor_copy(dsa_k[:, 1, :], ps[:, 1, :]))
                    dve.wait_ge(sems["kv_up"], 6)
                    sg["kv_out"].by(dve.tensor_copy(dsa_v[:, 0:2, :].rearrange("p a b -> p (a b)"), ps[:, 2, :]))
                    sg["kv_out"].by(dve.tensor_copy(dsa_v[:, 2:4, :].rearrange("p a b -> p (a b)"), ps[:, 3, :]))
                    take(3)
                    for m in range(4):
                        evac(4, m, dil_v[:, m, :])
                    dil_outs = [(5, m, (dsaq[:, m, :] if m < 2 else gate[:, m - 2, :]), 512) for m in range(4)]
                    dil_outs += [(6, m, retqk[:, m, :], 512) for m in range(4)]
                    dil_outs += [(7, m, retv[:, m, :], 256) for m in range(4)]

                    def beside_dil(i):
                        evac_beside(i, dil_pace, dil_outs)
                        take(1)

                    dil.vector(dve, 0, beside_dil)
                    take(len(rounds))
                    for qb in range(1, TB):
                        sg["bias_ready"].by(dve.tensor_scalar(sc[qb][:], sc[qb][:], -2e38, NEG, ALU.is_gt, ALU.mult))
                    dve.wait_ge(sems["bias_ready"], 3)
                    dve.wait_ge(sems["mix_lo"], TB)

                    def add_out(g, m):
                        b = 4 * ((g - G_MIX) % 2) + m
                        dve.wait_ge(sems["bank_ready"], HALF * g + m + 1)
                        sg["bank_free"].by(dve.tensor_tensor(x[:, b, :], x[:, b, :], ps[:, HALF * half_of(g) + m, :],
                                                             ALU.add))

                    def retention(i):
                        if 1 <= i <= 4:
                            add_out(G_MIX, i - 1)
                        if i == ROT:
                            dve.wait_ge(sems["consts"], 16 * 3)
                        if ROT <= i < ROT + 2:
                            for j in (2 * (i - ROT), 2 * (i - ROT) + 1):
                                dve.wait_ge(sems["ret_rot"], j + 1)
                                sg["dve_link"].by(dve.tensor_tensor(st_b[0][:], ps[:, 4 + j, :], rtab[:, T_SIN:T_SIN + S],
                                                                    ALU.mult))
                                link(dve, dve.tensor_tensor(st_b[1][:], retqk[:, j, :], rtab[:, T_COS:T_COS + S], ALU.mult))
                                sg["ret_rotd"].by(dve.tensor_tensor(retqk[:, j, :], st_b[0][:], st_b[1][:], ALU.add))
                                dve.wait_ge(sems["ret_rotd"], j + 1)
                        for u in (2 * (i - RET), 2 * (i - RET) + 1):
                            if 0 <= u < RET_H * TB:
                                h, kb = divmod(u, TB)
                                w = S - kb * P
                                dve.wait_ge(sems["ret_s"], u + 1)
                                if u >= 4:
                                    dve.wait_ge(sems["ret_o"], u - 3)
                                sg["ret_p"].by(dve.tensor_tensor(st_b[u % 4][:, 0:w], ps[:, 4 + u % 2, 0:w],
                                                                 rtab[:, T_DECAY + h * S:T_DECAY + h * S + w], ALU.mult))
                        if i == GN - 1:
                            for j in range(2):
                                dve.wait_ge(sems["ret_o"], 2 * TB * (j + 1))
                                sg["gn_in"].by(dve.tensor_copy(gn[j][:], ps[:, 6 + j, :]))
                        if i == GN:
                            dve.wait_ge(sems["gn_in"], 2)
                            for j in range(2):
                                dve.wait_ge(sems["gn_mean"], j + 1)
                                sg["gn_c"].by(dve.tensor_tensor(gn[j][:], gn[j][:], ps[:, 4 + j, :], ALU.subtract))
                        if i == GN + 1:
                            for j in range(2):
                                dve.wait_ge(sems["gn_rstd"], j + 1)
                                link(dve, dve.scalar_tensor_tensor(out=gn[j][:], in0=gn[j][:], scalar=gains[:, 2, j:j + 1],
                                                                   in1=st_b[j][:], op0=ALU.mult, op1=ALU.mult))
                                sg["gn_out"].by(dve.tensor_tensor(gn[j][:], gn[j][:], gate[:, j, :], ALU.mult))
                        if i == GN + 2:
                            for j in range(2):
                                dve.wait_ge(sems["gn_out"], j + 1)
                                dve.wait_ge(sems["ret_hi"], j + 1)
                                sg["ret_lo"].by(dve.tensor_tensor(hid_lo[:, j, :], gn[j][:], hid_hi[:, j, :].bitcast(F32),
                                                                  ALU.subtract))

                    dsa.vector(dve, TB, retention)
                    for m in range(4):
                        add_out(G_MIX + 1, m)
                    dve.wait_ge(sems["bank_free"], BANKS + HALF * (G_MIX + 2))
                    for b in range(DB):
                        add_out(G_MIX + 2 + b // 4, b % 4)
                        if b >= 1:
                            stats_add(dve, 1, b - 1)
                    stats_add(dve, 1, DB - 1)
                    dve.wait_ge(sems["bank_free"], BANKS + HALF * G0)
                    norm_split_dve(dve, lambda k: gains[:, 1, k:k + 1], 1, 1)
                    dve.wait_ge(sems["h_lo_done"], 2 * DB)

                    def chunk(c, last):
                        for j in range(4):
                            for m in range(4):
                                bank = HALF * ((G0 + j) % 2) + m
                                if j < 2:
                                    n = 4 * j + m
                                    dve.wait_ge(sems["relu_ready"], 8 * c + (n + 1))
                                    dve.scalar_tensor_tensor(out=sq[m % 2][:], in0=ps[:, bank, :], scalar=0.0,
                                                             in1=tmp[m % 2][:], op0=ALU.max,
                                                             op1=ALU.mult).then_inc(sems["bank_free"], 1)
                                    dve.wait_ge(sems["bank_free"], 16 * c + (BANKS + HALF * (G0 + j) + m + 1))
                                    dve.wait_ge(sems["hid_hi_done"], 8 * c + (n + 1))
                                    dve.tensor_tensor(hid_lo[:, n, :], sq[m % 2][:], hid_hi[:, n, :].bitcast(F32),
                                                      ALU.subtract).then_inc(sems["hid_lo_done"], 1)
                                    dve.wait_ge(sems["hid_lo_done"], 8 * c + (n + 1))
                                else:
                                    b = 4 * (j - 2) + m
                                    dve.wait_ge(sems["bank_ready"], 16 * c + (HALF * (G0 + j) + m + 1))
                                    dve.tensor_tensor(x[:, b, :], x[:, b, :], ps[:, bank, :],
                                                      ALU.add).then_inc(sems["bank_free"], 1)
                                    if last and b >= 1:
                                        stats_add(dve, 2, b - 1)

                    with dve.Fori(0, CH - 1) as c:
                        chunk(c, False)
                    chunk(CH - 1, True)
                    stats_add(dve, 2, DB - 1)

        with nc.Fori(0, DEPTH) as L:
            first_layer(L)
            clear()

        acc = None

        def second_layer(layer):
            fresh()
            at[0] = region
            even = layer == 0
            acc = place(f"acc{layer}", [P, DB, S])
            gain_f = place(f"gain_f{layer}", [P, DB])
            st = Stream()
            kv = [KT, KT]
            if even:
                w_in = a["ev_w_in_2"][0]
                F = 512
                st.group(w_in, [(3 * F, P)], kv)
                st.group(w_in, [(0, 512)], kv)
                st.group(w_in, [(F, 512)], kv)
                st.group(w_in, [(2 * F, 512)], kv)
                st.group(w_in, [(3 * F + FOX_H, 512)], kv)
                w_out = a["ev_w_out_2"][0]
                beside_groups = range(4, 7)
                for n in range(2):
                    st.group(w_out, [(512 * n, 512)], [KT], r0=512)
            else:
                w_in = a["od_w_in_2"][0]
                for c in (2, 3, 0, 1):
                    st.group(w_in, [(512 * c, 512)], kv)
                w_out = a["od_w_out_2"][0]
                beside_groups = range(2, 4)
            GM = len(st.groups)
            for n in range(2):
                st.group(w_out, [(512 * n, 512)], [KT] if even else kv)

            def half_of(g):
                return 1 if g in beside_groups else g % 2

            def before(g):
                return next((p for p in range(g - 1, -1, -1) if half_of(p) == half_of(g)), None)
            wg, wu, wd = (a[n][layer] for n in ("ffn_w_gate_2", "ffn_w_up_2", "ffn_w_down_2"))
            CH = D_FF2 // 512
            R0 = CH * 512

            def up_group(col, width):
                st.group_pairs(((wg, col, width), (wu, col, width)), kv)

            up_group(R0, D_FF2 - R0)
            st.group(wd, [(0, 512)], [(D_FF2 - R0) // P], r0=R0)
            st.group(wd, [(512, 512)], [(D_FF2 - R0) // P], r0=R0)
            G0, S0 = len(st.groups), len(st.slots)
            GU = GM + 2
            U0 = sum(len(t) - 1 for _, t in st.groups)
            land0 = list(st.need)
            SL, GC = 6, 4
            lens[:] = [DB] * (5 if even else 3)
            N0 = 1 if even else 0
            TOK = [(t, 0, 512, t, 0) for t in range(TB)]
            gb = lambda i: (lambda k: gains[:, i, k:k + 1])
            xb = lambda k: x[:, k, :]
            ab = lambda k: acc[:, k, :]
            macc = place("macc", [P, DB, S], where=t_off["h_lo"]) if even else acc
            mb = lambda k: macc[:, k, :]
            SU = st.groups[GU][0]

            if even:
                fq, fk = place("fq", [P, 4, S]), place("fk", [P, 4, S])
                fv = place("fv", [P, TB, 512])
                bf = place("bf", [FOX_H, 1])
                lf, lc = place("lf", [FOX_H, S]), place("lc", [FOX_H, S])
                sel = place("sel_t", [FOX_H, FOX_H * P], where=t_off["acc0"])
                pw = place("pw", [P, 4, P], where=t_off["acc0"] + 4096)
                psc = place("psc", [P, 4])
                pooled = place("pooled", [P, 4, S], where=t_off["acc0"] + 4096 + 2048)
                ub = [place(f"ub{i}", [P, 16 + S]) for i in range(3)]
                t16 = place("t16", [P, 16])
                fox = Attention(FOX_H, fq, fk, fv, causal, 0, 0, 0, decay=(sel, lf))
                pool_pace = Pace(32, 0, 14)
                PM = 18
                out_a, out_b = Pace(16, 24, 8), Pace(16, 32, 8)
            else:
                xr, gt = place("xr", [P, DB, S]), place("gt", [P, DB, S])
                r8 = place("r8", [P, DB, S], where=t_off["acc1"])
                t8 = [place(f"t8_{b}", [P, S], where=t_off["hid_lo"] + 2048 * b if b < 4 else
                            t_off[("sq0", "sq1", "ssum", "p_more")[b - 4]]) for b in range(DB)]
                i_t = [place(f"i_t{i}", [P, S], where=t_off[n]) for i, n in enumerate(("pT_more", "rstd"))]
                wa = place("wa", [P, 8, 256], where=t_off["hid_hi"] + 4 * 2048)
                wx = place("wx", [P, 8, 256], where=t_off["hid_lo"] + 4 * 2048)
                lru = [(w, 2 * hd + e) for hd in range(4) for w in range(2) for e in range(2)]
                lru_pace = Pace(40, 0, len(lru))
                xp = [place(f"xp{i}", [P, 3 + S + 1]) for i in range(2)]
                par = place("par", [P, 8, DB])
                sp8 = place("sp8", [P, 3, DB])

            with nc.Block() as block:
                @block.sync
                def _(sp):
                    def small(dst, src):
                        sp.dma_start(dst, src, allow_slow_non_contiguous=True).then_inc(sems["small"], 16)

                    for i, n in enumerate(("mix_pre_g_2", "mix_post_g_2", "ffn_pre_g_2", "ffn_post_g_2")):
                        small(gains[:, i, :], gain_view(a[n][layer]))
                    small(gain_f[:], gain_view(a["final_norm_w"]))
                    if even:
                        small(bf[:], a["ev_b_f_2"][0].rearrange("(p o) -> p o", o=1))
                        small(psc[:], gain_view(a["ev_pool_scale_2"][0]))
                    else:
                        for i in range(4):
                            small(par[:, i, :], gain_view(a["od_conv_w_2"][0, i]))
                        for i, n in enumerate(("od_conv_b_2", "od_b_a_2", "od_b_x_2", "od_lam_2")):
                            small(par[:, 4 + i, :], gain_view(a[n][0]))
                    load_slot(sp, 0, st.slots[0].pieces, None)
                    load_slot(sp, 1, st.slots[1].pieces, None)
                    if even:
                        sp.dma_start(sel[:], a["sel"]).then_inc(sems["consts"], 16)
                        sp.dma_start(pw[:], a["ev_pool_w_2"][0].rearrange("g d e -> d g e")).then_inc(sems["consts"], 16)
                    else:
                        for t, n in ((wa, "od_w_a_2"), (wx, "od_w_x_2")):
                            sp.dma_start(t[:], a[n][0].rearrange("h (b p) e -> p (h b) e", p=P)).then_inc(sems["consts"], 16)
                    for s in range(2, len(st.slots)):
                        load_slot(sp, s, st.slots[s].pieces, s - RING + 1)
                    with sp.Fori(0, CH) as c:
                        for j in range(SL):
                            s = SL * c + (S0 + j - RING + 1)
                            if j < 4:
                                rows = slice(512 * (j % 2), 512 * (j % 2) + 512)
                                col = bass.ds(512 * c + 256 * (j // 2), 256)
                                pieces = [(w[rows, col].rearrange("(k p) c -> p k c", p=P), 256 * q, 256)
                                          for q, w in enumerate((wg, wu))]
                            else:
                                src = wd[bass.ds(512 * c, 512), 512 * (j - 4):512 * (j - 4) + 512]
                                pieces = [(src.rearrange("(k p) c -> p k c", p=P), 0, 512)]
                            load_slot(sp, j, pieces, s)

                @block.gpsimd
                def _(pool):
                    stream_lo(pool, st, 0, SU + 2)
                    norm_post_pool(pool, 0)
                    stream_lo(pool, st, SU + 2, len(st.slots))
                    with pool.Fori(0, CH) as c:
                        for j in range(SL):
                            split_lo(pool, j, KT, 512, SL * c + (S0 + j + 1))
                    norm_post_pool(pool, 1)

                @block.tensor
                def _(pe):
                    def tiles_of(g, blocks, hi=h_hi, lo=h_lo, ready=None, k0=0):
                        first, tiles = st.groups[g]
                        return group_tiles(pe, g, first, tiles, blocks, hi, lo, half_of(g), k0, ready=ready,
                                           before=before(g))

                    def grp(*args, **kw):
                        for _ in tiles_of(*args, **kw):
                            pass

                    pe.sem_inc(sems["bank_free"], BANKS)
                    if even:
                        stats_pe(pe, 0, 0)
                        grp(0, [(0, 0, P, None, 0)], ready=("h_lo_done", 1))
                        for g in (1, 2):
                            grp(g, FEAT)
                        grp(3, TOK)
                        pe.wait_ge(sems["bank_free"], BANKS + HALF * 4)
                        pe.wait_ge(sems["consts"], 32)
                        pe.wait_ge(sems["f_done"], 1)
                        pool_tiles = tiles_of(4, FEAT)
                        tiles_a = tiles_of(5, FEAT, hid_hi, hid_lo, k0=KT)
                        tiles_b = tiles_of(6, FEAT, hid_hi, hid_lo, k0=KT)

                        def pooling(i):
                            pool_pace.emit(i, pool_tiles)
                            g = i - PM
                            if 0 <= g < 4:
                                pe.wait_ge(sems["pool_in"], g + 1)
                                pe.matmul(ps[:, 4 + g, :], pw[:, g, :], pooled[:, g, :], start=True,
                                          stop=True).then_inc(sems["pool_mm"], 1)
                            if i == out_a.first:
                                pe.wait_ge(sems["pool_lo"], 4)
                            out_a.emit(i, tiles_a)
                            out_b.emit(i, tiles_b)

                        fox.tensor(pe, 0, pooling)
                        pe.wait_ge(sems["mix_lo"], TB)
                    else:
                        grp(0, FEAT, ready=("h_lo_done", 1))
                        grp(1, FEAT)
                        tiles = chain(tiles_of(2, FEAT), tiles_of(3, FEAT))
                        pe.wait_ge(sems["bank_free"], BANKS + HALF)
                        pe.wait_ge(sems["consts"], 32)
                        for u, (w, b) in enumerate(lru):
                            pe.wait_ge(sems["conv_done"], 2 * (b // 2) + 2)
                            if u >= 4:
                                pe.wait_ge(sems["lru_r"], u - 3)
                            for q in range(2):
                                mm = pe.matmul(ps[:, u % 4, :], (wa, wx)[w][:, 2 * (b // 2) + q, P * (b % 2):P * (b % 2) + P],
                                               xr[:, 2 * (b // 2) + q, :], start=q == 0, stop=q == 1)
                            mm.then_inc(sems["lru_mm"], 1)
                            lru_pace.emit(u, tiles)
                        for _ in tiles:
                            pass
                        pe.wait_ge(sems["lru_r"], len(lru))
                    grp(GM, FEAT, hid_hi, hid_lo, ready=None if even else ("mix_lo", 1))
                    grp(GM + 1, FEAT, hid_hi, hid_lo)
                    pe.wait_ge(sems["bank_free"], BANKS + HALF * (GU - 1))
                    stats_pe(pe, N0, HALF * (GU % 2))
                    pe.wait_ge(sems["rstd_ready"], N0 + 1)
                    stats_pe(pe, N0 + 1, HALF * (GU % 2))
                    grp(GU, FEAT, ready=("h_lo_done", DB + 1))
                    grp(GU + 1, FEAT, hid_hi, hid_lo, ready=("hid_lo_done", 1))
                    grp(GU + 2, FEAT, hid_hi, hid_lo)
                    with pe.Fori(0, CH) as c:
                        for j in range(GC):
                            ring_of[0] = (0, 0, 0, 1)[j]
                            group(pe, GC * c + (G0 + j), SL * c + (S0 + (0, 2, 4, 5)[j]), kv if j < 2 else [KT], FEAT,
                                  *((h_hi, h_lo) if j < 2 else (hid_hi, hid_lo)), (G0 + j) % 2,
                                  ready=("hid_lo_done", 4 * c + 3) if j == 2 else None)
                    pe.wait_ge(sems["bank_free"], BANKS + HALF * (G0 + GC * CH - 1))
                    stats_pe(pe, N0 + 2, HALF * (G0 % 2))
                    if even:
                        pe.wait_ge(sems["rstd_ready"], N0 + 3)
                        stats_pe(pe, N0 + 3, HALF * (G0 % 2))

                @block.scalar
                def _(act):
                    stream_hi(act, st, 0)
                    stream_hi(act, st, 1)
                    stats_bank[0] = 0
                    if even:
                        stats_act(act, xb, 0, 1.0 / D, ready=("xup", 1))
                    norm_split_act(act, 0)
                    if even:
                        for s in range(2, 4):
                            stream_hi(act, st, s)
                        act.wait_ge(sems["f_in"], 1)
                        alink(act, act.activation(lc[:], lf[:], ACT.Abs))
                        alink(act, act.activation(lc[:], lc[:], ACT.Exp, scale=-1.0))
                        sg["f_c"].by(act.activation(lc[:], lc[:], ACT.Ln, bias=1.0))
                        for s in range(4, 10):
                            stream_hi(act, st, s)

                        def pooling(i):
                            for s, step in ((10, pool_pace.step_of(16)), (11, pool_pace.step_of(32)),
                                            (12, out_a.step_of(16))):
                                if i == step:
                                    stream_hi(act, st, s)
                            g = i - PM
                            if 0 <= g < 4:
                                act.wait_ge(sems["pool_out"], g + 1)
                                sg["pool_hi"].by(act.activation(hid_hi[:, 4 + g, :], ub[g % 2][:, 16:], ACT.Copy))

                        fox.scalar(act, 0, pooling)
                        nxt = 13
                    else:
                        act.wait_ge(sems["small"], 16 * 13)
                        alink(act, act.activation(sp8[:, 0, :], par[:, 7, :], ACT.Abs))
                        alink(act, act.activation(sp8[:, 0, :], sp8[:, 0, :], ACT.Exp, scale=-1.0))
                        sg["f_c"].by(act.activation(sp8[:, 0, :], sp8[:, 0, :], ACT.Ln, bias=1.0))
                        for s in range(2, 6):
                            stream_hi(act, st, s)
                        act.wait_ge(sems["f_done"], 1)

                        def gates(u0, u1):
                            for u in range(u0, u1):
                                w, b = lru[u]
                                act.wait_ge(sems["lru_mm"], u + 1)
                                if w == 1 and b >= 2:
                                    act.wait_ge(sems["xi_done"], b - 1)
                                sg["lru_r"].by(act.activation(i_t[b % 2][:] if w else r8[:, b, :], ps[:, u % 4, :],
                                                              ACT.Sigmoid, bias=par[:, 5 + w, b:b + 1]))
                                for s, t in ((6, 16), (7, 32)):
                                    if lru_pace.step_of(t) == u:
                                        stream_hi(act, st, s)

                        def decay(b0):
                            for b in range(b0, b0 + 4):
                                sg["lru_t"].by(act.activation(t8[b][:], r8[:, b, :], ACT.Tanh, scale=sp8[:, 1, b:b + 1]))
                            act.wait_ge(sems["lru_t"], b0 + 4)
                            for b in range(b0, b0 + 4):
                                alink(act, act.activation(r8[:, b, :], r8[:, b, :], ACT.Exp, scale=sp8[:, 2, b:b + 1]))
                                if b >= 2:
                                    act.wait_ge(sems["lru_b"], b - 1)
                                else:
                                    act.wait_ge(sems["conv_done"], DB)
                                sg["lru_a"].by(act.activation(xp[b % 2][:, 0:S], r8[:, b, :], ACT.Square))

                        def roots(b0):
                            for b in range(b0, b0 + 4):
                                act.wait_ge(sems["lru_b"], b + 1)
                                sg["root_done"].by(act.activation(t8[b][:], t8[b][:], ACT.Sqrt))

                        def gelu(n):
                            act.wait_ge(sems["bank_free"], BANKS + HALF * (3 + n))
                            sg["gelu_done"].by(act.activation(gt[:, 4 * n:4 * n + 4, :], gt[:, 4 * n:4 * n + 4, :],
                                                              ACT.Gelu_apprx_tanh))

                        def mixed(b0):
                            for b in range(b0, b0 + 4):
                                act.wait_ge(sems["y_done"], b + 1)
                                sg["mix_hi"].by(act.activation(hid_hi[:, b, :], tmp[b % 2][:], ACT.Copy))

                        gates(0, 8)
                        act.wait_ge(sems["lru_r"], 8)
                        decay(0)
                        roots(0)
                        gates(8, 16)
                        act.wait_ge(sems["lru_r"], 16)
                        gelu(0)
                        decay(4)
                        stream_hi(act, st, 8)
                        mixed(0)
                        roots(4)
                        stream_hi(act, st, 9)
                        gelu(1)
                        mixed(4)
                        nxt = 10
                    for s in range(nxt, SU + 1):
                        stream_hi(act, st, s)
                    stats_bank[N0] = stats_bank[N0 + 1] = HALF * (GU % 2)
                    stats_act(act, mb, N0, 1.0 / D, ready=("m_done", 1),
                              between=[lambda: stream_hi(act, st, SU + 1)])
                    stats_act(act, xb, N0 + 1, 1.0 / D, ready=("xup", DB * N0 + 1))
                    norm_split_act(act, 1)

                    def hi(c, j):
                        q, jj = divmod(j, SL)
                        cc = c + q
                        used = (("bank_ready", GC * HALF * cc + HALF * (G0 - 1)), ("bank_ready", GC * HALF * cc + HALF * G0),
                                ("slot_used", 2 * cc + (U0 + 1)), ("bank_ready", GC * HALF * cc + HALF * (G0 + 1)),
                                ("slot_used", 2 * cc + (U0 + 2)), ("bank_ready", GC * HALF * cc + HALF * (G0 + 2)))[jj]
                        split_hi(act, jj, KT, 512, 80 * cc + (land0[jj % 2] + (32, 32, 64, 64, 80, 80)[jj]), used)

                    def gated(g, n, ready, free):
                        act.wait_ge(sems["bank_free"], free)
                        for m in range(2):
                            act.wait_ge(sems["bank_ready"], ready + m + 1)
                            act.activation(tmp[m][:], ps[:, HALF * (g % 2) + m, :],
                                           ACT.Silu).then_inc(sems["relu_ready"], 1)
                        for m in range(2):
                            act.wait_ge(sems["v_ready"], n + m + 1)
                            act.activation(hid_hi[:, gated_at[0] + m, :], sq[m][:],
                                           ACT.Copy).then_inc(sems["hid_hi_done"], 1)

                    gated_at = [0]
                    gated(GU, 0, HALF * GU, BANKS + HALF * GU)
                    stream_hi(act, st, S0 - 2)
                    stream_hi(act, st, S0 - 1)
                    hi(0, 0)
                    hi(0, 1)

                    def chunk(c, last):
                        for j in range(2):
                            hi(c, 2 * j + 2)
                            gated_at[0] = 2 * j
                            gated(G0 + j, 4 * c + (2 + 2 * j), GC * HALF * c + HALF * (G0 + j),
                                  GC * HALF * c + (BANKS + HALF * (G0 + j)))
                            hi(c, 2 * j + 3)
                        if not last:
                            hi(c, 6)
                            hi(c, 7)

                    with act.Fori(0, CH - 1) as c:
                        chunk(c, False)
                    chunk(CH - 1, True)
                    stats_bank[N0 + 2] = stats_bank[N0 + 3] = HALF * (G0 % 2)
                    stats_act(act, ab, N0 + 2, 1.0 / D, ready=("bank_free", BANKS + HALF * (G0 + GC * CH - 2) + 1))
                    if even:
                        stats_act(act, xb, N0 + 3, 1.0 / D, ready=("xup", DB * (N0 + 1) + 1))

                @block.vector
                def _(dve):
                    dve.wait_ge(sems["small"], 16 * (7 if even else 13))
                    if even:
                        for k in range(DB):
                            sg["xup"].by(dve.scalar_tensor_tensor(out=x[:, k, :], in0=x[:, k, :], scalar=gain_f[:, k:k + 1],
                                                                  in1=rstd[:], op0=ALU.mult, op1=ALU.mult))
                            if k >= 1:
                                stats_add(dve, 0, k - 1)
                        stats_add(dve, 0, DB - 1)
                        dve.wait_ge(sems["xup"], DB)
                    norm_split_dve(dve, gb(0), 0 if even else None, 0)

                    def evac(g, m, o):
                        dve.wait_ge(sems["bank_ready"], HALF * g + m + 1)
                        sg["bank_free"].by(dve.tensor_copy(o, ps[:, HALF * half_of(g) + m, :]))

                    if even:
                        for i in range(3):
                            link(dve, dve.memset(ub[i][:, 0:16], 0.0))
                        dve.wait_ge(sems["bank_ready"], HALF)
                        sg["bank_free"].by(dve.tensor_scalar(lf[:], ps[0:FOX_H, 0, :], bf[:], None, ALU.add), HALF)
                        dve.wait_ge(sems["bank_free"], BANKS + HALF)
                        dve.sem_inc(sems["f_in"], 1)
                        for m in range(4):
                            evac(1, m, fq[:, m, :])
                        dve.wait_ge(sems["f_c"], 1)
                        link(dve, dve.scalar_tensor_tensor(out=lc[:], in0=lf[:], scalar=0.0, in1=lc[:], op0=ALU.min,
                                                           op1=ALU.subtract))
                        link(dve, dve.tensor_tensor_scan(lf[:], tab[0:FOX_H, T_ONES:T_ONES + 1].to_broadcast([FOX_H, S]),
                                                         lc[:], 0.0, ALU.mult, ALU.add))
                        sg["f_done"].by(dve.tensor_scalar(lf[:], lf[:], -1.0 / SCALE, None, ALU.mult))
                        for g, t in ((2, fk), (3, fv)):
                            for m in range(4):
                                evac(g, m, t[:, m, :])

                        def pool_block(m):
                            w = POOL_W[m]
                            evac(4, m, ub[0][:, 16:])
                            dve.wait_ge(sems["bank_free"], sg["bank_free"].n + BANKS)
                            src, step, i = ub[0], 1, 1
                            while step < w:
                                link(dve, dve.tensor_tensor(ub[i][:, 16:], src[:, 16:], src[:, 16 - step:16 + S - step],
                                                            ALU.add))
                                src, step, i = ub[i], 2 * step, 3 - i
                            link(dve, dve.scalar_tensor_tensor(out=pooled[:, m, :], in0=src[:, 16:], scalar=1.0 / w,
                                                               in1=ub[0][:, 16:], op0=ALU.mult, op1=ALU.subtract))
                            link(dve, dve.tensor_tensor(t16[:], src[:, 16:32], tab[:, T_POOL + 16 * m:T_POOL + 16 * m + 16],
                                                        ALU.mult))
                            sg["pool_in"].by(dve.tensor_tensor(pooled[:, m, 0:16], t16[:], ub[0][:, 16:32], ALU.subtract))
                            dve.wait_ge(sems["pool_in"], m + 1)

                        def pooling(i):
                            for m in range(4):
                                if i == pool_pace.step_of(16 + 4 * (m + 1)) + 1:
                                    pool_block(m)
                            g = i - PM
                            if 1 <= g <= 4:
                                dve.wait_ge(sems["pool_hi"], g)
                                sg["pool_lo"].by(dve.tensor_tensor(hid_lo[:, 3 + g, :], ub[(g - 1) % 2][:, 16:],
                                                                   hid_hi[:, 3 + g, :].bitcast(F32), ALU.subtract))
                            if 0 <= g < 4:
                                dve.wait_ge(sems["pool_mm"], g + 1)
                                if g >= 2:
                                    dve.wait_ge(sems["pool_lo"], g - 1)
                                sg["pool_out"].by(dve.tensor_scalar(ub[g % 2][:, 16:], ps[:, 4 + g, :], psc[:, g:g + 1],
                                                                    None, ALU.mult))
                            for m in range(4):
                                if i == out_a.step_of(4 * (m + 1)) + 1:
                                    evac(5, m, macc[:, m, :])
                                if i == out_b.step_of(4 * (m + 1)) + 1:
                                    evac(6, m, macc[:, 4 + m, :])

                        fox.vector(dve, 0, pooling)
                        evac(6, 3, macc[:, 7, :])
                        dve.wait_ge(sems["bank_free"], BANKS + HALF * GM)
                    else:
                        for i in range(2):
                            link(dve, dve.memset(xp[i][:, 0:3], 0.0))
                        dve.wait_ge(sems["f_c"], 1)
                        link(dve, dve.tensor_scalar(sp8[:, 1, :], par[:, 7, :], -1.0, 0.0, ALU.mult, ALU.max))
                        link(dve, dve.tensor_tensor(sp8[:, 0, :], sp8[:, 0, :], sp8[:, 1, :], ALU.add))
                        link(dve, dve.tensor_scalar(sp8[:, 1, :], sp8[:, 0, :], LRU_C, None, ALU.mult))
                        sg["f_done"].by(dve.tensor_scalar(sp8[:, 2, :], sp8[:, 0, :], -LRU_C, None, ALU.mult))
                        for b in range(DB):
                            g, m = b // 4, b % 4
                            q = xp[b % 2]
                            dve.wait_ge(sems["bank_ready"], HALF * g + m + 1)
                            sg["bank_free"].by(dve.tensor_copy(q[:, 3:3 + S], ps[:, HALF * (g % 2) + m, :]))
                            dve.wait_ge(sems["bank_free"], sg["bank_free"].n + BANKS)
                            link(dve, dve.tensor_scalar(xr[:, b, :], q[:, 0:S], par[:, 0, b:b + 1], par[:, 4, b:b + 1],
                                                        ALU.mult, ALU.add))
                            for i in range(1, 4):
                                ins = dve.scalar_tensor_tensor(out=xr[:, b, :], in0=q[:, i:i + S],
                                                               scalar=par[:, i, b:b + 1], in1=xr[:, b, :],
                                                               op0=ALU.mult, op1=ALU.add)
                                if i < 3:
                                    link(dve, ins)
                                else:
                                    sg["conv_done"].by(ins)
                            dve.wait_ge(sems["conv_done"], b + 1)

                        def gated_input(b0):
                            for b in range(b0, b0 + 4):
                                dve.wait_ge(sems["lru_r"], lru.index((1, b)) + 1)
                                dve.wait_ge(sems["lru_mm"], 4 * (b // 2) + 4)
                                sg["xi_done"].by(dve.tensor_tensor(xr[:, b, :], xr[:, b, :], i_t[b % 2][:], ALU.mult))

                        def variance(b0):
                            for b in range(b0, b0 + 4):
                                dve.wait_ge(sems["lru_a"], b + 1)
                                sg["lru_b"].by(dve.scalar_tensor_tensor(out=t8[b][:], in0=xp[b % 2][:, 0:S], scalar=1.0,
                                                                        in1=t8[b][:], op0=ALU.add, op1=ALU.mult))

                        def recur(b0):
                            for b in range(b0, b0 + 4):
                                dve.wait_ge(sems["root_done"], b + 1)
                                link(dve, dve.tensor_tensor(t8[b][:], xr[:, b, :], t8[b][:], ALU.mult))
                                sg["dve_link"].by(dve.tensor_tensor_scan(xr[:, b, :], r8[:, b, :], t8[b][:], 0.0,
                                                                         ALU.mult, ALU.add))
                            dve.wait_ge(sems["dve_link"], sg["dve_link"].n)

                        def mixed(n):
                            dve.wait_ge(sems["gelu_done"], n + 1)
                            for b in range(4 * n, 4 * n + 5):
                                if b < 4 * n + 4:
                                    if b >= 2:
                                        dve.wait_ge(sems["mix_lo"], b - 1)
                                    sg["y_done"].by(dve.tensor_tensor(tmp[b % 2][:], xr[:, b, :], gt[:, b, :], ALU.mult))
                                if b > 4 * n:
                                    dve.wait_ge(sems["mix_hi"], b)
                                    sg["mix_lo"].by(dve.tensor_tensor(hid_lo[:, b - 1, :], tmp[(b - 1) % 2][:],
                                                                      hid_hi[:, b - 1, :].bitcast(F32), ALU.subtract))

                        gated_input(0)
                        variance(0)
                        for m in range(4):
                            evac(2, m, gt[:, m, :])
                        recur(0)
                        gated_input(4)
                        variance(4)
                        mixed(0)
                        recur(4)
                        for m in range(4):
                            evac(3, m, gt[:, 4 + m, :])
                        mixed(1)
                    for b in range(DB):
                        g, m = GM + b // 4, b % 4
                        dve.wait_ge(sems["bank_ready"], HALF * g + m + 1)
                        if even:
                            sg["m_done"].by(dve.tensor_tensor(macc[:, b, :], macc[:, b, :], ps[:, HALF * half_of(g) + m, :],
                                                              ALU.add))
                        else:
                            sg["m_done"].by(dve.tensor_copy(acc[:, b, :], ps[:, HALF * half_of(g) + m, :]))
                        if b >= 1:
                            stats_add(dve, N0, b - 1)
                        if m == 3:
                            dve.wait_ge(sems["m_done"], b + 1)
                            dve.sem_inc(sems["bank_free"], HALF)
                    stats_add(dve, N0, DB - 1)
                    norm_post(dve, mb, gb(1), N0, 0, n_next=N0 + 1, x0=DB * N0)
                    dve.wait_ge(sems["xup"], DB * (N0 + 1))
                    norm_split_dve(dve, gb(2), N0 + 1, 1)
                    dve.wait_ge(sems["h_lo_done"], 2 * DB)

                    def gated(g, n, at_block, ready, free):
                        for m in range(2):
                            dve.wait_ge(sems["relu_ready"], n + m + 1)
                            dve.wait_ge(sems["bank_ready"], ready + m + 3)
                            dve.tensor_tensor(sq[m][:], ps[:, HALF * (g % 2) + 2 + m, :], tmp[m][:],
                                              ALU.mult).then_inc(sems["v_ready"], 1)
                        dve.wait_ge(sems["v_ready"], n + 2)
                        dve.sem_inc(sems["bank_free"], HALF)
                        for m in range(2):
                            dve.wait_ge(sems["hid_hi_done"], n + m + 1)
                            dve.tensor_tensor(hid_lo[:, at_block + m, :], sq[m][:], hid_hi[:, at_block + m, :].bitcast(F32),
                                              ALU.subtract).then_inc(sems["hid_lo_done"], 1)
                        dve.wait_ge(sems["hid_lo_done"], n + 2)

                    gated(GU, 0, 0, HALF * GU, None)
                    for b in range(DB):
                        g, m = GU + 1 + b // 4, b % 4
                        dve.wait_ge(sems["bank_ready"], HALF * g + m + 1)
                        dve.tensor_copy(acc[:, b, :], ps[:, HALF * (g % 2) + m, :]).then_inc(sems["bank_free"], 1)

                    def chunk(c, last):
                        for j in range(2):
                            gated(G0 + j, 4 * c + (2 + 2 * j), 2 * j, GC * HALF * c + HALF * (G0 + j), None)
                        for b in range(DB):
                            j, m = 2 + b // 4, b % 4
                            dve.wait_ge(sems["bank_ready"], GC * HALF * c + (HALF * (G0 + j) + m + 1))
                            dve.tensor_tensor(acc[:, b, :], acc[:, b, :], ps[:, HALF * ((G0 + j) % 2) + m, :],
                                              ALU.add).then_inc(sems["bank_free"], 1)
                            if last and b >= 1:
                                stats_add(dve, N0 + 2, b - 1)

                    with dve.Fori(0, CH - 1) as c:
                        chunk(c, False)
                    chunk(CH - 1, True)
                    stats_add(dve, N0 + 2, DB - 1)
                    norm_post(dve, ab, gb(3), N0 + 2, 1, n_next=N0 + 3 if even else None, x0=DB * N0)

        if DEPTH2 > 0:
            second_layer(0)
            clear()
        if DEPTH2 > 1:
            second_layer(1)
            clear()

        fresh()
        with nc.Block() as block:
            @block.tensor
            def _(pe):
                for t in range(TB):
                    for k in range(DB):
                        mm = pe.transpose(ps[:, 2 * t + k // 4, (k % 4) * P:(k % 4 + 1) * P], x[:, k, t * P:(t + 1) * P], ident)
                    mm.then_inc(sems["x_T"], 1)

            @block.vector
            def _(dve):
                for t in range(TB):
                    dve.wait_ge(sems["x_T"], t + 1)
                    dve.tensor_copy(xin[:, t, :].rearrange("p (a b) -> p a b", b=512),
                                    ps[:, 2 * t:2 * t + 2, :]).then_inc(sems["x_copied"], 1)

            @block.sync
            def _(sp):
                for t in range(TB):
                    sp.wait_ge(sems["x_copied"], t + 1)
                    sp.dma_start(out[0, t * P:(t + 1) * P, :], xin[:, t, :]).then_inc(sems["stored"], 16)
                if "dbg" in a:
                    sp.dma_start(a["dbg"], x[:]).then_inc(sems["stored"], 16)
                sp.wait_ge(sems["stored"], 16 * (TB + (1 if "dbg" in a else 0)))


def kernel(**inputs):
    import concourse.bacc as bacc
    from concourse.bass_utils import run_bass_kernel_spmd

    nc = bacc.Bacc("TRN2", target_bir_lowering=False, num_devices=1)
    arrays, args = {}, {}
    tab, rtab, sel = shape_tables()
    for name, v in dict(inputs, tab=tab, rtab=rtab, sel=sel).items():
        v = np.ascontiguousarray(v)
        arrays[f"in_{name}"] = v
        args[name] = nc.dram_tensor(f"in_{name}", v.shape, mybir.dt.from_np(v.dtype), kind="ExternalInput").ap()
    out = nc.dram_tensor("out", (1, S, D), F32, kind="ExternalOutput").ap()
    build(nc, args, out)
    r = run_bass_kernel_spmd(nc, [arrays], core_ids=[0])
    return r.results[0]["out"]
```

```python
from contextlib import ExitStack
from itertools import chain

import numpy as np
import concourse.bass as bass
from concourse import mybir

F32 = mybir.dt.float32
F32R = mybir.dt.float32r
ALU = mybir.AluOpType
ACT = mybir.ActivationFunctionType

P = 128
S = 512
TB = S // P
D = 1024
DB = D // P
HD = 64
DEPTH = 2
DEPTH2 = 2
RET_H, DSA_H, DIL_H, FOX_H, IDX_H = 4, 4, 8, 8, 8
TOPK = min(256, S // 4)
D_FF = 4096
D_FF2 = 2816
POOL_W = (2, 4, 8, 16)
EPS = 1e-6
LRU_C = 8.0
SCALE = HD ** -0.5
NEG = -1e30
TAKEN = -3e38
C_RET, C_DSA = 0, 1024
C_DSAQ, C_CKV, C_QIDX, C_KIDX, C_WIDX = 1024, 1280, 1408, 1920, 1984
C_DIL = 1992
N_IN = 3528
KT = 4
RING = 2
BANKS = 8
HALF = 4

T_IDENT, T_ONES, T_MEAN, T_ROT, T_LOGC, T_CAUSAL, T_POOL = 0, 128, 256, 384, 512, 1024, 1536
T_SHARED = 1600
T_COS, T_SIN, T_DECAY = 0, 512, 1024
T_RET = 1024 + RET_H * S


def shape_tables():
    f = np.float32
    q = np.arange(P)[:, None]
    t = np.zeros((P, T_SHARED), f)
    t[:, T_IDENT:T_IDENT + P] = np.eye(P)
    t[:, T_ONES:T_ONES + P] = 1.0
    half = (np.arange(P)[:, None] // HD) == (np.arange(P)[None] // HD)
    t[:, T_MEAN:T_MEAN + P] = half / HD
    for m in range(P):
        if m % HD < HD // 2:
            t[m + HD // 2, T_ROT + m] = -1.0
        else:
            t[m - HD // 2, T_ROT + m] = 1.0
    dist = q - (np.arange(S)[None] - (S - P))
    count = ((dist >= 0) & (dist <= 128)).astype(int)
    for dil, in ((4,), (16,)):
        count = count + ((dist >= 0) & (dist % dil == 0)).astype(int)
    t[:, T_LOGC:T_LOGC + S] = np.where(count > 0, np.log(np.maximum(count, 1)) / SCALE, NEG)
    t[:, T_CAUSAL:T_CAUSAL + S] = np.where(dist >= 0, 0.0, NEG)
    for g, w in enumerate(POOL_W):
        t[:, T_POOL + 16 * g:T_POOL + 16 * g + 16] = 1.0 / np.minimum(np.arange(16) + 1, w)
    r = np.zeros((P, T_RET), f)
    inv = (f(10000.0) ** (-np.arange(HD // 2, dtype=f) / f(HD // 2))).astype(f)
    ang = np.arange(S, dtype=f)[None] * inv[np.arange(P) % (HD // 2)][:, None]
    r[:, T_COS:T_COS + S] = np.cos(ang.astype(np.float64))
    r[:, T_SIN:T_SIN + S] = np.sin(ang.astype(np.float64))
    diff = np.arange(S)[None] - q
    for h in range(RET_H):
        lg = np.log(1.0 - 2.0 ** (-5.0 - h))
        r[:, T_DECAY + h * S:T_DECAY + (h + 1) * S] = np.where(diff >= 0, np.exp(diff * lg), 0.0) * SCALE
    sel = np.zeros((FOX_H, FOX_H * P), f)
    for h in range(FOX_H):
        sel[h, h * P:(h + 1) * P] = 1.0
    return t, r, sel


class Signal:

    def __init__(self, sem):
        self.sem = sem
        self.n = 0

    def by(self, ins, k=1):
        ins.then_inc(self.sem, k)
        self.n += k
        return ins


def build(nc, a, out):
    ctx = ExitStack()
    with ctx:
        at = [16512]

        def place(name, shape, dt=F32, where=None):
            size = int(np.prod(shape[1:])) * 4
            off = where
            if where is None:
                off = at[0]
                at[0] += -(-size // 32) * 32
                assert at[0] <= 229368, (name, at[0])
            t = nc.alloc_sbuf_tensor_at(name, shape, dt, offset=off)
            t_off[name] = off
            return t

        t_off = {}
        x = place("x", [P, DB, S])
        h_hi, h_lo = place("h_hi", [P, DB, S], F32R), place("h_lo", [P, DB, S], F32R)
        hid_hi, hid_lo = place("hid_hi", [P, DB, S], F32R), place("hid_lo", [P, DB, S], F32R)
        raw = [place(f"raw{i}", [P, KT, 512]) for i in range(RING)]
        w_hi = [place(f"w_hi{i}", [P, KT, 512], F32R) for i in range(RING)]
        w_lo = [place(f"w_lo{i}", [P, KT, 512], F32R) for i in range(RING)]
        tab = place("tab", [P, T_SHARED])
        gains = place("gains", [P, 3, DB])
        gains_2, gain_f = place("gains_2", [P, DEPTH2, 4, DB]), place("gain_f", [P, DB])
        bf, psc = place("bf", [FOX_H, 1]), place("psc", [P, 4])
        wf, wf_hi, wf_lo = (place(n, [P, DB, FOX_H], t) for n, t in (("wf", F32), ("wf_hi", F32R), ("wf_lo", F32R)))
        par = place("par", [P, 8, DB])
        sq = [place(f"sq{i}", [P, S]) for i in range(2)]
        rstd = place("rstd", [P, S])
        tmp = [place(f"tmp{i}", [P, S]) for i in range(2)]
        ssum = place("ssum", [P, S])
        p_more = place("p_more", [P, S])
        pT_more = place("pT_more", [P, S])
        stat = place("stat", [P, 4 * P])
        ident = tab[:, T_IDENT:T_IDENT + P]
        ones = tab[:, T_ONES:T_ONES + P]
        mean_m = tab[:, T_MEAN:T_MEAN + P]
        rot_m = tab[:, T_ROT:T_ROT + P]
        p_t = [place(f"p{i}", [P, S], where=t_off[n]) for i, n in enumerate(("sq0", "sq1", "ssum", "p_more"))]
        pT = [place(f"pT{i}", [P, TB, P], where=t_off[n]) for i, n in enumerate(("tmp0", "tmp1", "pT_more"))]
        post_t = [tmp[0], tmp[1], pT_more]
        on = place("on", [P, 8, HD], where=t_off["rstd"])
        sx, sn, sd, sr = (stat[:, 0:64], stat[:, 64:128], stat[:, 128:192], stat[:, 192:256])
        xin = place("xin", [P, TB, D], where=t_off["hid_hi"])

        ps = ctx.enter_context(nc.psum_tensor("ps", [P, BANKS, 512], F32))

        names = (
            "loaded0 loaded1 hi_split lo_split slot_used bank_ready bank_free consts small sq_ready "
            "sq_used ln_done rstd_ready normed h_hi_done h_lo_done dve_link act_link relu_ready "
            "hid_hi_done hid_lo_done v_ready idx_ready idx_relu idx_used kv_up kv_out ckv_in ckv_n "
            "ret_rot ret_cos ret_rotd ret_s ret_p ret_o ret_hi ret_lo head_w head_w_T head_w_ready "
            "pool_hi pool_lo gn_in gn_mean gn_c gn_sq gn_var gn_rstd gn_out mix_hi mix_lo s_ready "
            "s_masked nmax p_ready pT_ready pT_copied pv_done o_norm oT_ready ssq_done post x_loaded0 "
            "x_loaded1 x_loaded2 x_loaded3 x_out0 x_out1 x_out2 x_out3 prefetched0 prefetched next_hi "
            "next_lo wf_in wf_split x_T x_copied stored f_mm f_in f_c f_done pool_in pool_mm pool_out "
            "bias_ready conv_done xi_done root_done lru_mm lru_r lru_t lru_a lru_b gelu_done y_done "
            "m_done xup").split()
        sems = {n: ctx.enter_context(nc.semaphore(n)) for n in names}
        sg = {}

        def fresh():
            for n in names:
                sg[n] = Signal(sems[n])

        class Slot:
            def __init__(self, pieces, rows):
                self.pieces, self.rows = pieces, rows
                self.width = sum(n for _, _, n in pieces)

        class Stream:

            def __init__(self, there=0):
                self.slots, self.groups = [], []
                self.need = [0, 0]
                self.landed = []
                self.there = there

            def land(self, pieces):
                s = len(self.slots)
                if s >= self.there:
                    self.need[s % RING] += 16 * len(pieces)
                self.landed.append(None if s < self.there else self.need[s % RING])

            def group(self, w, cols, tiles, r0=0):
                first = len(self.slots)
                done = 0
                for n in tiles:
                    pieces, c = [], 0
                    for (col, wid) in cols:
                        src = w[r0 + P * done:r0 + P * (done + n), col:col + wid]
                        pieces.append((src.rearrange("(k p) c -> p k c", p=P), c, wid))
                        c += wid
                    s = Slot(pieces, n)
                    self.land(pieces)
                    self.slots.append(s)
                    done += n
                self.groups.append((first, list(tiles)))

            def group_pairs(self, parts, tiles):
                first = len(self.slots)
                done = 0
                for n in tiles:
                    pieces, c = [], 0
                    for w, col, wid in parts:
                        src = w[P * done:P * (done + n), col:col + wid]
                        pieces.append((src.rearrange("(k p) c -> p k c", p=P), c, wid))
                        c += wid
                    self.land(pieces)
                    self.slots.append(Slot(pieces, n))
                    done += n
                self.groups.append((first, list(tiles)))

            def used(self, s):
                for g, (first, tiles) in enumerate(self.groups):
                    if first <= s < first + len(tiles):
                        if s == first + len(tiles) - 1:
                            return "bank_ready", HALF * (g + 1)
                        before = sum(len(t) - 1 for _, t in self.groups[:g])
                        return "slot_used", before + s - first + 1

        def load_slot(sp, s, pieces, wait):
            if wait is not None:
                sp.wait_ge(sems["lo_split"], wait)
            for src, c, wid in pieces:
                sp.dma_start(raw[s % RING][:, 0:src.shape[1], c:c + wid], src).then_inc(
                    sems[f"loaded{s % RING}"], 16)

        def split_hi(act, s, rows, width, landed, used):
            if landed is not None:
                act.wait_ge(sems[f"loaded{s % RING}"], landed)
            if used is not None:
                act.wait_ge(sems[used[0]], used[1])
            act.activation(w_hi[s % RING][:, 0:rows, 0:width], raw[s % RING][:, 0:rows, 0:width],
                           ACT.Copy).then_inc(sems["hi_split"], 1)

        def split_lo(pool, s, rows, width, count):
            pool.wait_ge(sems["hi_split"], count)
            pool.tensor_tensor(w_lo[s % RING][:, 0:rows, 0:width], raw[s % RING][:, 0:rows, 0:width],
                               w_hi[s % RING][:, 0:rows, 0:width].bitcast(F32),
                               ALU.subtract).then_inc(sems["lo_split"], 1)

        def stream_sp(sp, st):
            for s, slot in enumerate(st.slots):
                load_slot(sp, s, slot.pieces, s - RING + 1 if s >= RING else None)

        def next_hi(act, width):
            act.wait_ge(sems["prefetched0"], 64 if width < 512 else 16)
            sg["next_hi"].by(act.activation(w_hi[0][:, :, 0:width], raw[0][:, :, 0:width], ACT.Copy))

        def next_lo(pool, width):
            pool.wait_ge(sems["next_hi"], 1)
            pool.tensor_tensor(w_lo[0][:, :, 0:width], raw[0][:, :, 0:width], w_hi[0][:, :, 0:width].bitcast(F32),
                               ALU.subtract).then_inc(sems["next_lo"], 1)
            pool.wait_ge(sems["next_lo"], 1)

        def stream_hi(act, st, s):
            if s == 0 and st.there:
                act.sem_inc(sems["hi_split"], 1)
            elif s < len(st.slots):
                slot = st.slots[s]
                split_hi(act, s, slot.rows, slot.width, st.landed[s], st.used(s - RING) if s >= RING else None)

        def stream_lo(pool, st, s0, s1):
            for s in range(s0, s1):
                slot = st.slots[s]
                if s == 0 and st.there:
                    pool.sem_inc(sems["lo_split"], 1)
                    continue
                split_lo(pool, s, slot.rows, slot.width, s + 1)

        def group_tiles(pe, g, s0, tiles, blocks, act_hi, act_lo, half, k0=0, ready=None, before=None):
            k_at = k0
            total = sum(tiles)
            nb = len({b[0] for b in blocks})
            freed = HALF * g if before is None else BANKS + HALF * before
            for i, nk in enumerate(tiles):
                s = s0 + i
                r = (i + s0_ring(s0)) % RING
                pe.wait_ge(sems["lo_split"], s + 1)
                last_slot = i == len(tiles) - 1

                def tile(m, k):
                    bank, c, n, tok, off = blocks[m]
                    kk = k_at + k
                    first, last = kk == k0, kk == k0 + total - 1
                    if first and off == 0:
                        pe.wait_ge(sems["bank_free"], freed + (bank + 1 if nb == HALF else HALF))
                    whi, wlo = w_hi[r][:, k, c:c + n], w_lo[r][:, k, c:c + n]
                    if tok is None:
                        o = ps[0:n, half * HALF + bank, :]
                        pairs = ((whi, act_hi[:, kk, :]), (whi, act_lo[:, kk, :]), (wlo, act_hi[:, kk, :]))
                    else:
                        t0 = tok * P
                        o = ps[:, half * HALF + bank, off:off + n]
                        ahi, alo = act_hi[:, kk, t0:t0 + P], act_lo[:, kk, t0:t0 + P]
                        pairs = ((ahi, whi), (ahi, wlo), (alo, whi))
                    for q, (lh, rh) in enumerate(pairs):
                        mm = pe.matmul(o, lh, rh, start=first and q == 0 and off == 0, stop=last and q == 2,
                                       skip_group_check=True)
                    if k < nk - 1:
                        return
                    if last_slot and m == len(blocks) - 1:
                        mm.then_inc(sems["bank_ready"], HALF - nb + 1)
                    elif last_slot and blocks[m + 1][0] != bank:
                        mm.then_inc(sems["bank_ready"], 1)
                    elif not last_slot and m == len(blocks) - 1:
                        mm.then_inc(sems["slot_used"], 1)

                if ready is None or i > 0:
                    if ready is not None:
                        pe.wait_ge(sems[ready[0]], ready[1] + (k_at + nk - 1))
                    for m in range(len(blocks)):
                        for k in range(nk):
                            tile(m, k)
                            yield
                else:
                    for k in range(nk):
                        pe.wait_ge(sems[ready[0]], ready[1] + (k_at + k))
                        for m in range(len(blocks)):
                            tile(m, k)
                            yield
                k_at += nk

        def group(*args, **kw):
            for _ in group_tiles(*args, **kw):
                pass

        class Pace:

            def __init__(self, tiles, first, steps):
                self.tiles, self.first, self.steps = tiles, first, steps

            def upto(self, i):
                return max(0, min(self.tiles, -(-self.tiles * (i - self.first + 1) // self.steps)))

            def step_of(self, t):
                return next(i for i in range(self.first - 1, 100) if self.upto(i) >= t)

            def emit(self, i, tiles):
                for _ in range(self.upto(i) - self.upto(i - 1)):
                    next(tiles, None)

        ring_of = [0]

        def s0_ring(s0):
            return s0 % RING if isinstance(s0, int) else ring_of[0]

        FEAT = [(b, b * P, P, None, 0) for b in range(4)]

        lens = []

        def adds(n):
            return sum(max(v - 2, 0) for v in lens[:n])

        def stats_act(act, src, n, scale, ready=None, between=None):
            used = adds(n)
            for k in range(lens[n]):
                if ready is not None:
                    act.wait_ge(sems[ready[0]], ready[1] + k)
                if k >= 3:
                    act.wait_ge(sems["sq_used"], used + k - 2)
                sg["sq_ready"].by(act.activation((sq[k % 2] if k else ssum)[:], src(k), ACT.Square))
            if between is not None:
                between()
            alink(act, act.activation(spare[:], one[:], ACT.Ln))
            act.wait_ge(sems["ssq_done"], n + 1)
            sg["ln_done"].by(act.activation(rstd[:], ps[:, stats_bank[n], :], ACT.Ln, scale=scale, bias=eps_c))
            act.wait_ge(sems["ln_done"], sg["ln_done"].n)
            sg["rstd_ready"].by(act.activation(rstd[:], rstd[:], ACT.Exp, scale=-0.5))

        stats_bank = {}

        def stats_add(dve, n, k):
            if k == 0 or k == DB - 1:
                return
            dve.wait_ge(sems["sq_ready"], sum(lens[:n]) + k + 1)
            if k >= 2:
                dve.wait_ge(sems["sq_used"], adds(n) + k - 1)
            sg["sq_used"].by(dve.tensor_tensor(ssum[:], ssum[:], sq[k % 2][:], ALU.add))

        def stats_pe(pe, n, bank):
            stats_bank[n] = bank
            if lens[n] == 1:
                pe.wait_ge(sems["sq_ready"], sum(lens[:n]) + 1)
                mm = pe.matmul(ps[:, bank, :], ones, ssum[:], start=True, stop=True)
            else:
                pe.wait_ge(sems["sq_used"], adds(n + 1))
                pe.matmul(ps[:, bank, :], ones, ssum[:], start=True, stop=False)
                pe.wait_ge(sems["sq_ready"], sum(lens[:n + 1]))
                mm = pe.matmul(ps[:, bank, :], ones, sq[(DB - 1) % 2][:], start=False, stop=True)
            mm.then_inc(sems["ssq_done"], 1)

        def norm_split_dve(dve, gain, n, m):
            if n is not None:
                dve.wait_ge(sems["rstd_ready"], n + 1)

            def scaled(k):
                if k >= 2:
                    dve.wait_ge(sems["h_lo_done"], DB * m + k - 1)
                sg["normed"].by(dve.scalar_tensor_tensor(out=tmp[k % 2][:], in0=x[:, k, :], scalar=gain(k),
                                                         in1=rstd[:], op0=ALU.mult, op1=ALU.mult))

            scaled(0)
            for k in range(DB):
                if k + 1 < DB:
                    scaled(k + 1)
                dve.wait_ge(sems["h_hi_done"], DB * m + k + 1)
                sg["h_lo_done"].by(dve.tensor_tensor(h_lo[:, k, :], tmp[k % 2][:], h_hi[:, k, :].bitcast(F32),
                                                     ALU.subtract))

        def norm_split_act(act, m, after_first=None):
            for k in range(DB):
                if k == 1 and after_first is not None:
                    after_first()
                act.wait_ge(sems["normed"], DB * m + k + 1)
                sg["h_hi_done"].by(act.activation(h_hi[:, k, :], tmp[k % 2][:], ACT.Copy))

        def norm_post(dve, src, gain, n, m, n_next=None, x0=0):
            dve.wait_ge(sems["rstd_ready"], n + 1)
            for k in range(DB + 2):
                if k < DB:
                    if k >= 3:
                        dve.wait_ge(sems["xup"], x0 + DB * m + k - 2)
                    sg["post"].by(dve.scalar_tensor_tensor(out=post_t[k % 3][:], in0=src(k), scalar=gain(k),
                                                           in1=rstd[:], op0=ALU.mult, op1=ALU.mult))
                if n_next is not None and k >= 2:
                    stats_add(dve, n_next, k - 2)

        def norm_post_pool(pool, m):
            for k in range(DB):
                pool.wait_ge(sems["post"], DB * m + k + 1)
                sg["xup"].by(pool.tensor_tensor(x[:, k, :], x[:, k, :], post_t[k % 3][:], ALU.add))

        def link(dve, ins):
            sg["dve_link"].by(ins)
            dve.wait_ge(sems["dve_link"], sg["dve_link"].n)

        def alink(act, ins):
            sg["act_link"].by(ins)
            act.wait_ge(sems["act_link"], sg["act_link"].n)

        class Attention:

            def __init__(self, heads, q, k, v, bias, mix0, u0, b0, decay=None):
                self.H, self.q, self.k, self.v, self.bias = heads, q, k, v, bias
                self.mix0, self.u0, self.b0, self.decay = mix0, u0, b0, decay
                self.units = [(qb, h) for qb in range(TB) for h in range(heads)]

            SB, PB, TS = 2, 4, 3
            TURN, VAL = 3, 5

            def scores(self, pe, i):
                qb, h = self.units[i]
                u = self.u0 + i
                n = (qb + 1) * P
                if i >= self.SB:
                    pe.wait_ge(sems["s_masked"], u - self.SB + 1)
                p0 = HD * (h % 2)
                o = ps[:, i % self.SB, 0:n]
                mm = pe.matmul(o, self.q[p0:p0 + HD, h // 2, qb * P:(qb + 1) * P],
                               self.k[p0:p0 + HD, h // 2, 0:n], start=True, stop=self.decay is None)
                if self.decay is not None:
                    sel, negc = self.decay
                    mm = pe.matmul(o, sel[:, h * P:(h + 1) * P], negc[:, 0:n], start=False, stop=True)
                mm.then_inc(sems["s_ready"], 1)

            def turn(self, pe, i):
                qb, h = self.units[i]
                u = self.u0 + i
                pe.wait_ge(sems["p_ready"], u + 1)
                if i >= 1:
                    pe.wait_ge(sems["pT_copied"], u)
                if self.backs:
                    pe.wait_ge(sems["mix_lo"], self.l0 + self.backs)
                for kb in range(qb + 1):
                    mm = pe.transpose(ps[:, 2, kb * P:(kb + 1) * P],
                                      p_t[i % self.PB][:, kb * P:(kb + 1) * P], ident)
                mm.then_inc(sems["pT_ready"], 1)

            def values(self, pe, i):
                qb, h = self.units[i]
                u = self.u0 + i
                pe.wait_ge(sems["pT_copied"], u + 1)
                if h == 0 and qb >= 1:
                    pe.wait_ge(sems["o_norm"], self.b0 + qb)
                for kb in range(qb + 1):
                    mm = pe.matmul(ps[:, 3, h * HD:(h + 1) * HD], pT[i % self.TS][:, kb, :],
                                   self.v[:, kb, h * HD:(h + 1) * HD], start=kb == 0, stop=kb == qb,
                                   skip_group_check=True)
                mm.then_inc(sems["pv_done"], 1)

            def back(self, pe, qb, turned):
                pe.wait_ge(sems["o_norm"], self.b0 + qb + 1)
                pe.wait_ge(sems["pT_copied"], self.u0 + turned)
                for j in range(self.H // 2):
                    mm = pe.transpose(ps[:, 2, j * P:(j + 1) * P],
                                      on[:, 2 * j:2 * j + 2, :].rearrange("p a b -> p (a b)"), ident)
                mm.then_inc(sems["oT_ready"], 1)
                self.backs += 1

            def at_end(self, i, lag):
                j = i - lag
                return j // self.H if 0 <= j < len(self.units) and j % self.H == self.H - 1 else None

            def steps(self):
                return len(self.units) + self.VAL + 3

            def tensor(self, pe, l0, beside):
                self.l0, self.backs = l0, 0
                n = len(self.units)
                for i in range(self.steps()):
                    if i < n:
                        self.scores(pe, i)
                    if self.TURN <= i < n + self.TURN:
                        self.turn(pe, i - self.TURN)
                    beside(i)
                    if self.VAL <= i < n + self.VAL:
                        self.values(pe, i - self.VAL)
                    qb = self.at_end(i, self.VAL + 2)
                    if qb is not None:
                        self.back(pe, qb, min(n, i - self.TURN + 1))

            def mask(self, dve, i):
                qb, h = self.units[i]
                u = self.u0 + i
                w = (qb + 1) * P
                dve.wait_ge(sems["s_ready"], u + 1)
                if i >= self.PB:
                    dve.wait_ge(sems["pT_ready"], u - self.PB + 1)
                sg["s_masked"].by(dve.tensor_tensor_reduce(
                    out=p_t[i % self.PB][:, 0:w], in0=ps[:, i % self.SB, 0:w], in1=self.bias(qb), scale=1.0,
                    scalar=TAKEN, op0=ALU.add, op1=ALU.max, accum_out=sx[:, i:i + 1]))

            def negate(self, dve, i):
                dve.wait_ge(sems["s_masked"], self.u0 + i + 1)
                sg["nmax"].by(dve.tensor_scalar(sn[:, i:i + 1], sx[:, i:i + 1], -SCALE, None, ALU.mult))

            def vector(self, dve, l0, beside):
                n = len(self.units)
                for i in range(self.steps()):
                    if i < n:
                        self.mask(dve, i)
                        self.negate(dve, i)
                    qb = self.at_end(i, self.VAL)
                    if qb is not None:
                        dve.wait_ge(sems["pv_done"], self.u0 + (qb + 1) * self.H)
                        if qb >= 1:
                            dve.wait_ge(sems["oT_ready"], self.b0 + qb)
                        a0, a1 = qb * self.H, (qb + 1) * self.H
                        link(dve, dve.reciprocal(sr[:, a0:a1], sd[:, a0:a1]))
                        sg["o_norm"].by(dve.tensor_tensor(
                            on[:, 0:self.H, :],
                            ps[:, 3, 0:self.H * HD].rearrange("p (h d) -> p h d", d=HD),
                            sr[:, a0:a1].unsqueeze(2).to_broadcast([P, self.H, HD]), ALU.mult))
                    qb = self.at_end(i, self.VAL + 2)
                    if qb is not None:
                        dve.wait_ge(sems["mix_hi"], l0 + qb + 1)
                        hb = self.H // 2
                        sl = (slice(None), slice(self.mix0, self.mix0 + hb), slice(qb * P, (qb + 1) * P))
                        sg["mix_lo"].by(dve.tensor_tensor(
                            hid_lo[sl], ps[:, 2, 0:hb * P].rearrange("p (a b) -> p a b", b=P),
                            hid_hi[sl].bitcast(F32), ALU.subtract))
                    beside(i)

            def scalar(self, act, l0, beside):
                n = len(self.units)
                for i in range(self.steps()):
                    if i < n:
                        qb, h = self.units[i]
                        u = self.u0 + i
                        w = (qb + 1) * P
                        act.wait_ge(sems["nmax"], u + 1)
                        sg["p_ready"].by(act.activation(p_t[i % self.PB][:, 0:w], p_t[i % self.PB][:, 0:w], ACT.Exp,
                                                        bias=sn[:, i:i + 1], scale=SCALE, accum_out=sd[:, i:i + 1]))
                    j = i - self.TURN
                    if 0 <= j < n:
                        qb, h = self.units[j]
                        u = self.u0 + j
                        act.wait_ge(sems["pT_ready"], u + 1)
                        if j >= self.TS:
                            act.wait_ge(sems["pv_done"], u - self.TS + 1)
                        sg["pT_copied"].by(act.activation(
                            pT[j % self.TS][:, 0:qb + 1, :].rearrange("p a b -> p (a b)"),
                            ps[:, 2, 0:(qb + 1) * P], ACT.Copy))
                    qb = self.at_end(i, self.VAL + 2)
                    if qb is not None:
                        hb = self.H // 2
                        act.wait_ge(sems["oT_ready"], self.b0 + qb + 1)
                        sg["mix_hi"].by(act.activation(
                            hid_hi[:, self.mix0:self.mix0 + hb, qb * P:(qb + 1) * P],
                            ps[:, 2, 0:hb * P].rearrange("p (a b) -> p a b", b=P), ACT.Copy))
                    beside(i)

        def causal(qb):
            return tab[:, T_CAUSAL + S - P - qb * P:T_CAUSAL + S]

        def logc(qb):
            return tab[:, T_LOGC + S - P - qb * P:T_LOGC + S]

        def clear():
            nc.all_engine_barrier()
            ids = sorted(s.num for s in sems.values())
            assert ids == list(range(ids[0], ids[0] + len(ids)))
            nc.sync.sem_clear(range(ids[0], ids[-1] + 1))
            nc.all_engine_barrier()

        def gain_view(v):
            return v.rearrange("(k p) -> p k", p=P)

        eps_c = place("eps", [P, 1])[:, 0:1]
        one, spare = place("one", [P, 1]), place("spare", [P, 1])
        region = at[0]

        LATENT_COLS = [(C_CKV, P), (C_KIDX, HD), (C_KIDX, HD), (C_WIDX, IDX_H)]

        LATENT = sum(wid for _, wid in LATENT_COLS)

        def load_first(sp, L, sem, waits=(None, None)):
            n = 0
            for i, v in enumerate((a["attn_norm_w"], a["mlp_norm_w"])):
                sp.dma_start(gains[:, i, :], gain_view(v[L]), allow_slow_non_contiguous=True).then_inc(sem, 16)
            sp.dma_start(gains[:, 2, 0:2], a["ret_norm_w"][L].rearrange("(b h) d -> (h d) b", h=2),
                         allow_slow_non_contiguous=True).then_inc(sem, 16)
            sp.dma_start(gains[:, 2, 2:3], a["dsa_kv_norm_w"][L].rearrange("(p o) -> p o", o=1),
                         allow_slow_non_contiguous=True).then_inc(sem, 16)
            n += 4 * 16
            for s in range(2):
                if waits[s] is not None:
                    sp.wait_ge(sems["lo_split"], waits[s])
                c = 0
                for col, wid in LATENT_COLS:
                    src = a["w_in"][L, 512 * s:512 * s + 512, col:col + wid]
                    sp.dma_start(raw[s][:, :, c:c + wid], src.rearrange("(k p) c -> p k c", p=P)).then_inc(
                        sem if s else sems["prefetched0"], 16)
                    c += wid
                    n += 16 * s
            return n

        fresh()
        lens[:] = [DB]
        with nc.Block() as block:
            @block.sync
            def _(sp):
                sp.dma_start(tab[:, 0:T_MEAN], a["tab"][:, 0:T_MEAN]).then_inc(sems["consts"], 16)
                for t in range(TB):
                    sp.dma_start(xin[:, t, :], a["x"][0, t * P:(t + 1) * P, :]).then_inc(sems[f"x_loaded{t}"], 16)
                count = load_first(sp, 0, sems["small"])
                sp.dma_start(tab[:, T_MEAN:], a["tab"][:, T_MEAN:]).then_inc(sems["small"], 16)

                def small(dst, src):
                    sp.dma_start(dst, src, allow_slow_non_contiguous=True).then_inc(sems["small"], 16)

                for layer in range(DEPTH2):
                    for i, n in enumerate(("mix_pre_g_2", "mix_post_g_2", "ffn_pre_g_2", "ffn_post_g_2")):
                        small(gains_2[:, layer, i, :], gain_view(a[n][layer]))
                small(gain_f[:], gain_view(a["final_norm_w"]))
                sp.dma_start(wf[:], a["ev_w_in_2"][0, :, 1536:1536 + FOX_H].rearrange("(k p) c -> p k c", p=P),
                             allow_slow_non_contiguous=True).then_inc(sems["wf_in"], 16)
                small(bf[:], a["ev_b_f_2"][0].rearrange("(p o) -> p o", o=1))
                small(psc[:], gain_view(a["ev_pool_scale_2"][0]))
                for i in range(4):
                    small(par[:, i, :], gain_view(a["od_conv_w_2"][0, i]))
                for i, n in enumerate(("od_conv_b_2", "od_b_a_2", "od_b_x_2", "od_lam_2")):
                    small(par[:, 4 + i, :], gain_view(a[n][0]))
                sp.wait_ge(sems["small"], count + 16 * (1 + 4 * DEPTH2 + 3 + 8))

            @block.tensor
            def _(pe):
                pe.wait_ge(sems["consts"], 16)
                for t in range(TB):
                    pe.wait_ge(sems[f"x_loaded{t}"], 16)
                    for k in range(DB):
                        mm = pe.transpose(ps[:, k, t * P:(t + 1) * P], xin[:, t, k * P:(k + 1) * P], ident)
                        if t == TB - 1:
                            mm.then_inc(sems["x_T"], 1)
                stats_pe(pe, 0, 0)

            @block.scalar
            def _(act):
                stats_bank[0] = 0
                stats_act(act, lambda k: x[:, k, :], 0, 1.0 / D, ready=("x_copied", 2))
                act.wait_ge(sems["wf_in"], 16)
                sg["wf_split"].by(act.activation(wf_hi[:], wf[:], ACT.Copy))
                next_hi(act, LATENT)

            @block.gpsimd
            def _(pool):
                pool.wait_ge(sems["wf_split"], 1)
                sg["wf_split"].by(pool.tensor_tensor(wf_lo[:], wf[:], wf_hi[:].bitcast(F32), ALU.subtract))
                next_lo(pool, LATENT)

            @block.vector
            def _(dve):
                dve.memset(one[:], 1.0)
                dve.memset(eps_c, EPS).then_inc(sems["x_copied"], 1)
                for k in range(DB):
                    dve.wait_ge(sems["x_T"], k + 1)
                    dve.tensor_copy(x[:, k, :], ps[:, k, :]).then_inc(sems["x_copied"], 1)
                    if k >= 1:
                        stats_add(dve, 0, k - 1)
                stats_add(dve, 0, DB - 1)
        clear()

        def first_layer(L):
            fresh()
            at[0] = region
            dsaq = place("dsaq", [P, 2, S])
            dil_q, dil_k = place("dil_q", [P, 4, S]), place("dil_k", [P, 4, S])
            dil_v = place("dil_v", [P, TB, 512])
            dsa_k, dsa_v = place("dsa_k", [P, 2, S]), place("dsa_v", [P, TB, 256])
            sc = [None] + [place(f"sc{q}", [P, (q + 1) * P]) for q in range(1, TB)]
            w_uk, w_uv = place("w_uk", [P, 256]), place("w_uv", [P, 256])
            widx = place("widx", [P, TB, IDX_H])
            top8 = place("top8", [P, 8])
            head_w = stat[0:IDX_H, :]
            q_idx = place("q_idx", [P, 4, S], where=t_off["hid_hi"] + 4 * 2048)
            retqk = place("retqk", [P, 4, S])
            retv = place("retv", [P, TB, 256], where=t_off["hid_hi"])
            gate = place("gate", [P, 2, S], where=t_off["hid_lo"])
            ckv = place("ckv", [P, S], where=t_off["hid_lo"] + 2 * 2048)
            kk = place("kk", [P, S], where=t_off["hid_lo"] + 3 * 2048)
            rl = p_t
            rtab = place("rtab", [P, T_RET], where=t_off["h_hi"])
            st_b = [place(f"ret_st{i}", [P, S], where=t_off["h_lo"] + i * 2048) for i in range(4)]
            gn = [place(f"gn{i}", [P, S], where=t_off["h_lo"] + (4 + i) * 2048) for i in range(2)]

            lens[:] = [1, DB, DB]
            w_in = a["w_in"][L]
            st = Stream(there=2)
            kv = [KT, KT]
            st.group(w_in, LATENT_COLS, kv)
            st.group(w_in, [(C_QIDX, 512)], kv)
            st.group(w_in, [(C_DIL, 512)], kv)
            st.group(w_in, [(C_DIL + 512, 512)], kv)
            st.group(w_in, [(C_DIL + 1024, 512)], kv)
            st.group(w_in, [(C_DSAQ, 256), (C_RET + 768, 256)], kv)
            st.group(w_in, [(C_RET, 512)], kv)
            st.group(w_in, [(C_RET + 512, 256)], kv)
            G_MIX = len(st.groups)
            for r0 in (512, 0):
                st.group(a["w_out"][L], [(0, 512)], [KT], r0=r0)
                st.group(a["w_out"][L], [(512, 512)], [KT], r0=r0)
            beside_groups = range(2, G_MIX + 2)

            def half_of(g):
                return 1 if g in beside_groups else g % 2

            def before(g):
                return next((p for p in range(g - 1, -1, -1) if half_of(p) == half_of(g)), None)
            G0, S0 = len(st.groups), len(st.slots)
            U0 = sum(len(t) - 1 for _, t in st.groups)
            CH = D_FF // D
            land0 = list(st.need)
            TOK = lambda n: [(t, 0, n, t, 0) for t in range(TB)]
            dil = Attention(DIL_H, dil_q, dil_k, dil_v, logc, 4, 0, 0)
            dsa = Attention(DSA_H, dsaq, dsa_k, dsa_v,
                            lambda q: causal(q) if q == 0 else sc[q][:], 2, TB * DIL_H, TB)
            idx_pace = Pace(2 * 32, 0, 24)
            dil_pace = Pace(3 * 32, 0, dil.steps() - 3)
            out_a, out_b = Pace(16, 0, 3), Pace(16, 16, 8)
            ROT, RET, GN = 4, 6, 15
            units = [(qb, h) for qb in range(1, TB) for h in range(IDX_H)]

            with nc.Block() as block:
                @block.sync
                def _(sp):
                    sp.dma_start(w_uk[:], a["dsa_w_uk"][L]).then_inc(sems["consts"], 16)
                    sp.dma_start(w_uv[:], a["dsa_w_uv"][L]).then_inc(sems["consts"], 16)
                    for s in range(2, len(st.slots)):
                        load_slot(sp, s, st.slots[s].pieces, s - RING + 1)
                        if s == 2 * G_MIX + 1:
                            sp.wait_ge(sems["bank_ready"], HALF * G_MIX)
                            sp.dma_start(rtab[:], a["rtab"]).then_inc(sems["consts"], 16)
                    with sp.Fori(0, CH) as c:
                        for j in range(8):
                            col = 512 * (j % 4 // 2)
                            if j < 4:
                                src = a["w_up"][L, 512 * (j % 2):512 * (j % 2) + 512, bass.ds(D * c + col, 512)]
                            else:
                                src = a["w_down"][L, bass.ds(D * c + 512 * (j % 2), 512), col:col + 512]
                            load_slot(sp, j, [(src.rearrange("(k p) c -> p k c", p=P), 0, 512)],
                                      8 * c + S0 + j - RING + 1)
                    total = S0 + 8 * CH
                    n = load_first(sp, DEPTH - 1 - L, sems["prefetched"], (total - 1, total))
                    sp.wait_ge(sems["prefetched"], n)

                @block.gpsimd
                def _(pool):
                    stream_lo(pool, st, 0, 2 * G_MIX + 2)
                    pool.wait_ge(sems["consts"], 16 * 3)
                    pool.wait_ge(sems["bank_free"], BANKS + HALF * 7)
                    for j in range(4):
                        sg["ret_cos"].by(pool.tensor_tensor(st_b[j][:], retqk[:, j, :], rtab[:, T_COS:T_COS + S],
                                                            ALU.mult))
                    stream_lo(pool, st, 2 * G_MIX + 2, len(st.slots))
                    with pool.Fori(0, CH) as c:
                        for j in range(8):
                            split_lo(pool, j, KT, 512, 8 * c + S0 + j + 1)
                    next_lo(pool, LATENT)

                @block.tensor
                def _(pe):
                    def tiles_of(g, blocks, hi=h_hi, lo=h_lo, ready=None, k0=0):
                        first, tiles = st.groups[g]
                        return group_tiles(pe, g, first, tiles, blocks, hi, lo, half_of(g), k0, ready=ready,
                                           before=before(g))

                    def grp(*args, **kw):
                        for _ in tiles_of(*args, **kw):
                            pass

                    pe.sem_inc(sems["bank_free"], BANKS)
                    grp(0, [(0, 0, P, None, 0), (1, P, P, None, 0), (2, 2 * P, IDX_H, None, 0)],
                        ready=("h_lo_done", 1))
                    grp(1, FEAT)
                    tiles = chain(tiles_of(2, FEAT), tiles_of(3, FEAT))
                    pe.wait_ge(sems["bank_free"], BANKS + HALF)
                    stats_pe(pe, 0, 3)
                    pe.wait_ge(sems["head_w"], 1)
                    for t in range(TB):
                        mm = pe.transpose(ps[:, 2, t * IDX_H:(t + 1) * IDX_H], head_w[:, t * P:(t + 1) * P],
                                          ident[0:IDX_H, 0:IDX_H])
                    mm.then_inc(sems["head_w_T"], 1)
                    for i, (qb, h) in enumerate(units):
                        idx_pace.emit(i, tiles)
                        if i == 2:
                            pe.wait_ge(sems["head_w_ready"], 1)
                        if i == 0:
                            pe.wait_ge(sems["bank_free"], BANKS + 2 * HALF)
                        if i >= 3:
                            pe.wait_ge(sems["idx_relu"], i - 2)
                        p0 = HD * (h % 2)
                        pe.matmul(ps[:, i % 3, 0:(qb + 1) * P], q_idx[p0:p0 + HD, h // 2, qb * P:(qb + 1) * P],
                                  kk[p0:p0 + HD, 0:(qb + 1) * P], start=True, stop=True).then_inc(sems["idx_ready"], 1)
                    tiles = tiles_of(4, TOK(512))
                    for _ in range(16):
                        next(tiles)
                    pe.wait_ge(sems["idx_relu"], len(units))
                    pe.wait_ge(sems["ckv_n"], 1)
                    pe.wait_ge(sems["consts"], 16 * 2)
                    for j in range(2):
                        pe.matmul(ps[:, j, :], w_uk[:, j * P:(j + 1) * P], ckv[:], start=True,
                                  stop=True).then_inc(sems["kv_up"], 1)
                    for t in range(TB):
                        pe.matmul(ps[:, 2 + t // 2, 256 * (t % 2):256 * (t % 2) + 256], ckv[:, t * P:(t + 1) * P],
                                  w_uv[:], start=True, stop=True, skip_group_check=True).then_inc(sems["kv_up"], 1)
                    for _ in tiles:
                        pass
                    pe.wait_ge(sems["kv_out"], 4)
                    pe.wait_ge(sems["bank_free"], BANKS + HALF * 5)
                    tiles = chain(tiles_of(5, FEAT), tiles_of(6, FEAT), tiles_of(7, TOK(256)))
                    dil.tensor(pe, 0, lambda i: dil_pace.emit(i, tiles))
                    tiles_a = tiles_of(G_MIX, FEAT, hid_hi, hid_lo, k0=KT)
                    tiles_b = tiles_of(G_MIX + 1, FEAT, hid_hi, hid_lo, k0=KT)
                    ru = [(h, kb) for h in range(RET_H) for kb in range(TB)]

                    def retention(i):
                        if i == 0:
                            pe.wait_ge(sems["mix_lo"], TB)
                        out_a.emit(i, tiles_a)
                        if i == ROT:
                            pe.wait_ge(sems["bank_free"], BANKS + HALF * (G_MIX + 1))
                        if ROT <= i < ROT + 2:
                            for j in (2 * (i - ROT), 2 * (i - ROT) + 1):
                                pe.matmul(ps[:, 4 + j, :], rot_m, retqk[:, j, :], start=True,
                                          stop=True).then_inc(sems["ret_rot"], 1)
                        if i == RET:
                            pe.wait_ge(sems["ret_rotd"], 4)
                        for u in (2 * (i - RET), 2 * (i - RET) + 1):
                            if 0 <= u < len(ru):
                                h, kb = ru[u]
                                p0, w = HD * (h % 2), S - kb * P
                                if u >= 2:
                                    pe.wait_ge(sems["ret_p"], u - 1)
                                pe.matmul(ps[:, 4 + u % 2, 0:w], retqk[p0:p0 + HD, 2 + h // 2, kb * P:(kb + 1) * P],
                                          retqk[p0:p0 + HD, h // 2, kb * P:S], start=True,
                                          stop=True).then_inc(sems["ret_s"], 1)
                        for u in (2 * (i - RET) - 2, 2 * (i - RET) - 1):
                            if 0 <= u < len(ru):
                                h, kb = ru[u]
                                p0, w = HD * (h % 2), S - kb * P
                                pe.wait_ge(sems["ret_p"], u + 1)
                                pe.matmul(ps[p0:p0 + HD, 6 + h // 2, kb * P:S], retv[:, kb, h * HD:(h + 1) * HD],
                                          st_b[u % 4][:, 0:w], start=kb == 0, stop=kb == TB - 1,
                                          skip_group_check=True).then_inc(sems["ret_o"], 1)
                        for j in range(2):
                            if i == GN:
                                pe.wait_ge(sems["gn_in"], j + 1)
                                pe.matmul(ps[:, 4 + j, :], mean_m, gn[j][:], start=True,
                                          stop=True).then_inc(sems["gn_mean"], 1)
                            if i == GN + 1:
                                pe.wait_ge(sems["gn_sq"], j + 1)
                                pe.matmul(ps[:, 6 + j, :], mean_m, st_b[j][:], start=True,
                                          stop=True).then_inc(sems["gn_var"], 1)
                        if i == out_b.step_of(9):
                            pe.wait_ge(sems["gn_rstd"], 2)
                        out_b.emit(i, tiles_b)

                    dsa.tensor(pe, TB, retention)
                    pe.wait_ge(sems["mix_lo"], 2 * TB)
                    pe.wait_ge(sems["ret_lo"], 2)
                    grp(G_MIX + 2, FEAT, hid_hi, hid_lo)
                    grp(G_MIX + 3, FEAT, hid_hi, hid_lo)
                    pe.wait_ge(sems["bank_free"], BANKS + HALF * (G0 - 1))
                    stats_pe(pe, 1, HALF * (G0 % 2))
                    with pe.Fori(0, CH) as c:
                        for j in range(4):
                            ring_of[0] = 0
                            ready = {0: ("h_lo_done", DB + 1), 2: ("hid_lo_done", 8 * c + 1)}.get(j)
                            group(pe, 4 * c + (G0 + j), 8 * c + (S0 + 2 * j), kv, FEAT,
                                  *((h_hi, h_lo) if j < 2 else (hid_hi, hid_lo)), (G0 + j) % 2, ready=ready)
                    pe.wait_ge(sems["bank_free"], BANKS + HALF * (G0 + 4 * CH - 1))
                    stats_pe(pe, 2, HALF * (G0 % 2))

                @block.scalar
                def _(act):
                    stream_hi(act, st, 0)
                    norm_split_act(act, 0, after_first=lambda: stream_hi(act, st, 1))
                    stream_hi(act, st, 2)
                    stream_hi(act, st, 3)
                    stream_hi(act, st, 4)
                    act.wait_ge(sems["ckv_in"], 1)
                    stats_bank[0] = 3
                    stats_act(act, lambda k: ckv[:], 0, 1.0 / P)
                    stream_hi(act, st, 5)

                    def hi_beside(i, pace, s0, slots):
                        for s in slots:
                            if pace.step_of(16 * (s - s0 - 1)) == i:
                                stream_hi(act, st, s)

                    for i, (qb, h) in enumerate(units):
                        act.wait_ge(sems["idx_ready"], i + 1)
                        if i >= 2:
                            act.wait_ge(sems["idx_used"], i - 1)
                        else:
                            act.wait_ge(sems["ckv_n"], 1)
                        sg["idx_relu"].by(act.activation(rl[i % 2][:, 0:(qb + 1) * P],
                                                         ps[:, i % 3, 0:(qb + 1) * P], ACT.Relu))
                        hi_beside(i, idx_pace, 4, range(6, 9))
                    for s in range(9, 12):
                        stream_hi(act, st, s)

                    def beside_dil(i):
                        hi_beside(i, dil_pace, 10, range(12, 17))
                        if i == len(dil.units) + 1:
                            act.wait_ge(sems["bank_free"], BANKS + HALF * 6)
                            alink(act, act.activation(gate[:], gate[:], ACT.Silu))

                    dil.scalar(act, 0, beside_dil)
                    stream_hi(act, st, 17)

                    def retention(i):
                        if i == 4:
                            stream_hi(act, st, 18)
                        for j in range(2):
                            if i == GN:
                                act.wait_ge(sems["gn_c"], j + 1)
                                sg["gn_sq"].by(act.activation(st_b[j][:], gn[j][:], ACT.Square))
                            if i == GN + 1:
                                act.wait_ge(sems["gn_var"], j + 1)
                                alink(act, act.activation(st_b[j][:], ps[:, 6 + j, :], ACT.Ln, bias=eps_c))
                        for j in range(2):
                            if i == GN + 1:
                                sg["gn_rstd"].by(act.activation(st_b[j][:], st_b[j][:], ACT.Exp, scale=-0.5))
                            if i == GN + 2:
                                act.wait_ge(sems["gn_out"], j + 1)
                                sg["ret_hi"].by(act.activation(hid_hi[:, j, :], gn[j][:], ACT.Copy))

                    dsa.scalar(act, TB, retention)
                    stream_hi(act, st, 19)

                    def hi(c, j):
                        if j % 2 == 0:
                            used = ("slot_used", 4 * c + (U0 + j // 2))
                        else:
                            used = ("bank_ready", 16 * c + HALF * (G0 + j // 2))
                        split_hi(act, j, KT, 512, 64 * c + (land0[j % 2] + 16 * (j // 2 + 1)), used)

                    split_hi(act, 0, KT, 512, land0[0] + 16, ("bank_ready", HALF * (G0 - 1)))
                    stats_bank[1] = stats_bank[2] = HALF * (G0 % 2)
                    stats_act(act, lambda k: x[:, k, :], 1, 1.0 / D, ready=("bank_free", BANKS + HALF * (G0 - 2) + 1))
                    norm_split_act(act, 1, after_first=lambda: hi(0, 1))

                    def chunk(c, last):
                        for j in range(4):
                            hi_a = not (last and j == 3)
                            if hi_a:
                                hi(c, 2 * j + 2)
                            if j < 2:
                                for m in range(4):
                                    n_in = 4 * j + m
                                    n = 8 * c + n_in
                                    act.wait_ge(sems["bank_ready"], 16 * c + (HALF * (G0 + j) + m + 1))
                                    act.wait_ge(sems["bank_free"], 16 * c + (HALF * (G0 + j) + m + 7))
                                    if n_in >= 2:
                                        act.wait_ge(sems["hid_hi_done"], 8 * c + (n_in - 1))
                                    act.activation(tmp[m % 2][:], ps[:, HALF * ((G0 + j) % 2) + m, :],
                                                   ACT.Relu).then_inc(sems["relu_ready"], 1)
                                    act.wait_ge(sems["relu_ready"], n + 1)
                                    act.activation(hid_hi[:, 4 * j + m, :], tmp[m % 2][:],
                                                   ACT.Square).then_inc(sems["hid_hi_done"], 1)
                            if hi_a:
                                hi(c, 2 * j + 3)

                    with act.Fori(0, CH - 1) as c:
                        chunk(c, False)
                    chunk(CH - 1, True)
                    stats_act(act, lambda k: x[:, k, :], 2, 1.0 / D,
                              ready=("bank_free", BANKS + HALF * (G0 + 4 * CH - 2) + 1),
                              between=lambda: next_hi(act, LATENT))

                @block.vector
                def _(dve):
                    norm_split_dve(dve, lambda k: gains[:, 0, k:k + 1], None, 0)

                    def evac(g, m, o, width=512):
                        dve.wait_ge(sems["bank_ready"], HALF * g + m + 1)
                        sg["bank_free"].by(dve.tensor_copy(o, ps[:, HALF * half_of(g) + m, 0:width]))

                    dve.wait_ge(sems["bank_ready"], HALF)
                    sg["bank_free"].by(dve.tensor_copy(kk[:], ps[:, 1, :]))
                    sg["ckv_in"].by(dve.tensor_copy(ckv[:], ps[:, 0, :]))
                    dve.wait_ge(sems["ckv_in"], 1)
                    sg["head_w"].by(dve.tensor_scalar(head_w, ps[0:IDX_H, 2, :], IDX_H ** -0.5 * HD ** -0.5, None,
                                                      ALU.mult))
                    dve.wait_ge(sems["head_w"], 1)
                    dve.sem_inc(sems["bank_free"], 3)
                    sg["bank_free"].n += 3
                    for m in range(4):
                        evac(1, m, q_idx[:, m, :])
                    dve.wait_ge(sems["head_w_T"], 1)
                    sg["head_w_ready"].by(dve.tensor_copy(widx[:].rearrange("p a b -> p (a b)"), ps[:, 2, 0:TB * IDX_H]))
                    dve.wait_ge(sems["rstd_ready"], 1)
                    sg["ckv_n"].by(dve.scalar_tensor_tensor(out=ckv[:], in0=ckv[:], scalar=gains[:, 2, 2:3],
                                                            in1=rstd[:], op0=ALU.mult, op1=ALU.mult))

                    def evac_beside(i, pace, outs):
                        for n, (g, m, o, width) in enumerate(outs):
                            if pace.step_of(32 * (n // 4) + 16 + 4 * (m + 1)) + 1 == i:
                                evac(g, m, o, width)

                    idx_outs = [(g, m, t[:, m, :], 512) for g, t in ((2, dil_q), (3, dil_k)) for m in range(4)]
                    dve.wait_ge(sems["head_w_ready"], 1)
                    for i, (qb, h) in enumerate(units):
                        w = (qb + 1) * P
                        dve.wait_ge(sems["idx_relu"], i + 1)
                        wt = widx[:, qb, h:h + 1]
                        if h == 0:
                            sg["idx_used"].by(dve.tensor_scalar(sc[qb][:], rl[i % 2][:, 0:w], wt, None, ALU.mult))
                        else:
                            dve.wait_ge(sems["idx_used"], i)
                            sg["idx_used"].by(dve.scalar_tensor_tensor(out=sc[qb][:], in0=rl[i % 2][:, 0:w], scalar=wt,
                                                                       in1=sc[qb][:], op0=ALU.mult, op1=ALU.add))
                        evac_beside(i, idx_pace, idx_outs)
                    evac_beside(len(units), idx_pace, idx_outs)
                    dve.wait_ge(sems["idx_used"], len(units))
                    for qb in range(1, TB):
                        sg["dve_link"].by(dve.tensor_tensor(sc[qb][:], sc[qb][:], causal(qb), ALU.add))
                    dve.wait_ge(sems["dve_link"], sg["dve_link"].n)
                    rounds = [(qb, r) for r in range(TOPK // 8) for qb in range(1, TB)]

                    def take(n):
                        for _ in range(min(n, len(rounds))):
                            qb, r = rounds.pop(0)
                            link(dve, dve.max(top8[:], sc[qb][:]))
                            link(dve, dve.match_replace(sc[qb][:], top8[:], sc[qb][:], TAKEN))

                    take(8)
                    dve.wait_ge(sems["kv_up"], 2)
                    sg["kv_out"].by(dve.tensor_copy(dsa_k[:, 0, :], ps[:, 0, :]))
                    sg["kv_out"].by(dve.tensor_copy(dsa_k[:, 1, :], ps[:, 1, :]))
                    dve.wait_ge(sems["kv_up"], 6)
                    sg["kv_out"].by(dve.tensor_copy(dsa_v[:, 0:2, :].rearrange("p a b -> p (a b)"), ps[:, 2, :]))
                    sg["kv_out"].by(dve.tensor_copy(dsa_v[:, 2:4, :].rearrange("p a b -> p (a b)"), ps[:, 3, :]))
                    take(5)
                    for m in range(4):
                        evac(4, m, dil_v[:, m, :])
                    dil_outs = [(5, m, (dsaq[:, m, :] if m < 2 else gate[:, m - 2, :]), 512) for m in range(4)]
                    dil_outs += [(6, m, retqk[:, m, :], 512) for m in range(4)]
                    dil_outs += [(7, m, retv[:, m, :], 256) for m in range(4)]

                    def beside_dil(i):
                        evac_beside(i, dil_pace, dil_outs)
                        if i == dil.steps() - 3:
                            take(len(rounds))
                            for qb in range(1, TB):
                                sg["bias_ready"].by(dve.tensor_scalar(sc[qb][:], sc[qb][:], -2e38, NEG, ALU.is_gt,
                                                                      ALU.mult))
                        else:
                            take(1)

                    dil.vector(dve, 0, beside_dil)
                    dve.wait_ge(sems["bias_ready"], 3)
                    dve.wait_ge(sems["mix_lo"], TB)

                    def add_out(g, m):
                        b = 4 * ((g - G_MIX) % 2) + m
                        dve.wait_ge(sems["bank_ready"], HALF * g + m + 1)
                        sg["bank_free"].by(dve.tensor_tensor(x[:, b, :], x[:, b, :], ps[:, HALF * half_of(g) + m, :],
                                                             ALU.add))

                    def retention(i):
                        for m in range(4):
                            if out_a.step_of(4 * (m + 1)) + 1 == i:
                                add_out(G_MIX, m)
                        if i == ROT:
                            dve.wait_ge(sems["consts"], 16 * 3)
                        if ROT <= i < ROT + 2:
                            for j in (2 * (i - ROT), 2 * (i - ROT) + 1):
                                dve.wait_ge(sems["ret_rot"], j + 1)
                                link(dve, dve.tensor_tensor(gn[j % 2][:], ps[:, 4 + j, :], rtab[:, T_SIN:T_SIN + S],
                                                            ALU.mult))
                                dve.wait_ge(sems["ret_cos"], j + 1)
                                sg["ret_rotd"].by(dve.tensor_tensor(retqk[:, j, :], gn[j % 2][:], st_b[j][:], ALU.add))
                                dve.wait_ge(sems["ret_rotd"], j + 1)
                        for u in (2 * (i - RET), 2 * (i - RET) + 1):
                            if 0 <= u < RET_H * TB:
                                h, kb = divmod(u, TB)
                                w = S - kb * P
                                dve.wait_ge(sems["ret_s"], u + 1)
                                if u >= 4:
                                    dve.wait_ge(sems["ret_o"], u - 3)
                                sg["ret_p"].by(dve.tensor_tensor(st_b[u % 4][:, 0:w], ps[:, 4 + u % 2, 0:w],
                                                                 rtab[:, T_DECAY + h * S:T_DECAY + h * S + w], ALU.mult))
                        if i == GN - 1:
                            for j in range(2):
                                dve.wait_ge(sems["ret_o"], 2 * TB * (j + 1))
                                sg["gn_in"].by(dve.tensor_copy(gn[j][:], ps[:, 6 + j, :]))
                        if i == GN:
                            dve.wait_ge(sems["gn_in"], 2)
                            for j in range(2):
                                dve.wait_ge(sems["gn_mean"], j + 1)
                                sg["gn_c"].by(dve.tensor_tensor(gn[j][:], gn[j][:], ps[:, 4 + j, :], ALU.subtract))
                        if i == GN + 1:
                            for j in range(2):
                                dve.wait_ge(sems["gn_rstd"], j + 1)
                                link(dve, dve.scalar_tensor_tensor(out=gn[j][:], in0=gn[j][:], scalar=gains[:, 2, j:j + 1],
                                                                   in1=st_b[j][:], op0=ALU.mult, op1=ALU.mult))
                                sg["gn_out"].by(dve.tensor_tensor(gn[j][:], gn[j][:], gate[:, j, :], ALU.mult))
                        if i == GN + 2:
                            for j in range(2):
                                dve.wait_ge(sems["gn_out"], j + 1)
                                dve.wait_ge(sems["ret_hi"], j + 1)
                                sg["ret_lo"].by(dve.tensor_tensor(hid_lo[:, j, :], gn[j][:], hid_hi[:, j, :].bitcast(F32),
                                                                  ALU.subtract))

                    dsa.vector(dve, TB, retention)
                    for m in range(4):
                        add_out(G_MIX + 1, m)
                    dve.wait_ge(sems["bank_free"], BANKS + HALF * (G_MIX + 2))
                    for b in range(DB):
                        add_out(G_MIX + 2 + b // 4, b % 4)
                        if b >= 1:
                            stats_add(dve, 1, b - 1)
                    stats_add(dve, 1, DB - 1)
                    dve.wait_ge(sems["bank_free"], BANKS + HALF * G0)
                    norm_split_dve(dve, lambda k: gains[:, 1, k:k + 1], 1, 1)
                    dve.wait_ge(sems["h_lo_done"], 2 * DB)

                    def chunk(c, last):
                        for j in range(4):
                            for m in range(4):
                                bank = HALF * ((G0 + j) % 2) + m
                                if j < 2:
                                    n = 4 * j + m
                                    dve.wait_ge(sems["relu_ready"], 8 * c + (n + 1))
                                    dve.scalar_tensor_tensor(out=sq[m % 2][:], in0=ps[:, bank, :], scalar=0.0,
                                                             in1=tmp[m % 2][:], op0=ALU.max,
                                                             op1=ALU.mult).then_inc(sems["bank_free"], 1)
                                    dve.wait_ge(sems["bank_free"], 16 * c + (BANKS + HALF * (G0 + j) + m + 1))
                                    dve.wait_ge(sems["hid_hi_done"], 8 * c + (n + 1))
                                    dve.tensor_tensor(hid_lo[:, n, :], sq[m % 2][:], hid_hi[:, n, :].bitcast(F32),
                                                      ALU.subtract).then_inc(sems["hid_lo_done"], 1)
                                    dve.wait_ge(sems["hid_lo_done"], 8 * c + (n + 1))
                                else:
                                    b = 4 * (j - 2) + m
                                    dve.wait_ge(sems["bank_ready"], 16 * c + (HALF * (G0 + j) + m + 1))
                                    dve.tensor_tensor(x[:, b, :], x[:, b, :], ps[:, bank, :],
                                                      ALU.add).then_inc(sems["bank_free"], 1)
                                    if last and b >= 1:
                                        stats_add(dve, 2, b - 1)

                    with dve.Fori(0, CH - 1) as c:
                        chunk(c, False)
                    chunk(CH - 1, True)
                    stats_add(dve, 2, DB - 1)

        with nc.Fori(0, DEPTH) as L:
            first_layer(L)
            clear()

        def second_layer(layer):
            fresh()
            at[0] = region
            even = layer == 0
            acc = place(f"acc{layer}", [P, DB, S])
            st = Stream(there=0 if even else 2)
            kv = [KT, KT]
            if even:
                w_in = a["ev_w_in_2"][0]
                F = 512
                st.group(w_in, [(0, 512)], kv)
                st.group(w_in, [(F, 512)], kv)
                st.group(w_in, [(2 * F, 512)], kv)
                st.group(w_in, [(3 * F + FOX_H, 512)], kv)
                w_out = a["ev_w_out_2"][0]
                beside_groups = range(3, 6)
                for n in range(2):
                    st.group(w_out, [(512 * n, 512)], [KT], r0=512)
            else:
                w_in = a["od_w_in_2"][0]
                for c in (2, 3, 0, 1):
                    st.group(w_in, [(512 * c, 512)], kv)
                w_out = a["od_w_out_2"][0]
                beside_groups = range(2, 4)
            GM = len(st.groups)
            for n in range(2):
                st.group(w_out, [(512 * n, 512)], [KT] if even else kv)

            def half_of(g):
                return 1 if g in beside_groups else g % 2

            def before(g):
                return next((p for p in range(g - 1, -1, -1) if half_of(p) == half_of(g)), None)

            wg, wu, wd = (a[n][layer] for n in ("ffn_w_gate_2", "ffn_w_up_2", "ffn_w_down_2"))
            CH = D_FF2 // 512
            R0 = CH * 512

            def up_group(col, width):
                st.group_pairs(((wg, col, width), (wu, col, width)), kv)

            up_group(R0, D_FF2 - R0)
            st.group(wd, [(0, 512)], [(D_FF2 - R0) // P], r0=R0)
            st.group(wd, [(512, 512)], [(D_FF2 - R0) // P], r0=R0)
            G0, S0 = len(st.groups), len(st.slots)
            GU = GM + 2
            U0 = sum(len(t) - 1 for _, t in st.groups)
            land0 = list(st.need)
            SL, GC = 6, 4
            lens[:] = [DB] * (5 if even else 3)
            N0 = 1 if even else 0
            TOK = [(t, 0, 512, t, 0) for t in range(TB)]
            gb = lambda i: (lambda k: gains_2[:, layer, i, k:k + 1])
            xb = lambda k: x[:, k, :]
            ab = lambda k: acc[:, k, :]
            macc = place("macc", [P, DB, S], where=t_off["h_lo"]) if even else acc
            mb = lambda k: macc[:, k, :]
            SU = st.groups[GU][0]

            if even:
                fq, fk = place("fq", [P, 4, S]), place("fk", [P, 4, S])
                fv = place("fv", [P, TB, 512])
                lf, lc = place("lf", [FOX_H, S]), place("lc", [FOX_H, S])
                sel = place("sel_t", [FOX_H, FOX_H * P], where=t_off["acc0"])
                pw = place("pw", [P, 4, P], where=t_off["acc0"] + 4096)
                pooled = place("pooled", [P, 4, S], where=t_off["acc0"] + 4096 + 2048)
                ub = [place(f"ub{i}", [P, 16 + S]) for i in range(3)]
                t16 = place("t16", [P, 16])
                fox = Attention(FOX_H, fq, fk, fv, causal, 0, 0, 0, decay=(sel, lf))
                pool_pace = Pace(32, 0, 14)
                PM = 18
                out_a, out_b = Pace(16, 24, 8), Pace(16, 32, 8)
            else:
                xr, gt = place("xr", [P, DB, S]), place("gt", [P, DB, S])
                r8 = place("r8", [P, DB, S], where=t_off["acc1"])
                t8 = [place(f"t8_{b}", [P, S], where=t_off["hid_lo"] + 2048 * b if b < 4 else
                            t_off[("sq0", "sq1", "ssum", "p_more")[b - 4]]) for b in range(DB)]
                i_t = [place(f"i_t{i}", [P, S], where=t_off[n]) for i, n in enumerate(("pT_more", "rstd"))]
                wa = place("wa", [P, 8, 256], where=t_off["hid_hi"] + 4 * 2048)
                wx = place("wx", [P, 8, 256], where=t_off["hid_lo"] + 4 * 2048)
                lru = [(w, 2 * hd + e) for hd in range(4) for w in range(2) for e in range(2)]
                lru_pace = Pace(40, 0, len(lru))
                xp = [place(f"xp{i}", [P, 3 + S + 1]) for i in range(2)]
                sp8 = place("sp8", [P, 3, DB])

            with nc.Block() as block:
                @block.sync
                def _(sp):
                    if even:
                        load_slot(sp, 0, st.slots[0].pieces, None)
                        load_slot(sp, 1, st.slots[1].pieces, None)
                    if even:
                        sp.dma_start(sel[:], a["sel"]).then_inc(sems["consts"], 16)
                        sp.dma_start(pw[:], a["ev_pool_w_2"][0].rearrange("g d e -> d g e")).then_inc(sems["consts"], 16)
                    else:
                        for t, n in ((wa, "od_w_a_2"), (wx, "od_w_x_2")):
                            sp.dma_start(t[:], a[n][0].rearrange("h (b p) e -> p (h b) e", p=P)).then_inc(sems["consts"], 16)
                    for s in range(2, len(st.slots)):
                        load_slot(sp, s, st.slots[s].pieces, s - RING + 1)
                    with sp.Fori(0, CH) as c:
                        for j in range(SL):
                            s = SL * c + (S0 + j - RING + 1)
                            if j < 4:
                                rows = slice(512 * (j % 2), 512 * (j % 2) + 512)
                                col = bass.ds(512 * c + 256 * (j // 2), 256)
                                pieces = [(w[rows, col].rearrange("(k p) c -> p k c", p=P), 256 * q, 256)
                                          for q, w in enumerate((wg, wu))]
                            else:
                                src = wd[bass.ds(512 * c, 512), 512 * (j - 4):512 * (j - 4) + 512]
                                pieces = [(src.rearrange("(k p) c -> p k c", p=P), 0, 512)]
                            load_slot(sp, j, pieces, s)
                    if even:
                        for s in range(2):
                            sp.wait_ge(sems["lo_split"], S0 + SL * CH - 1 + s)
                            src = a["od_w_in_2"][0, 512 * s:512 * s + 512, D:D + 512]
                            sp.dma_start(raw[s][:], src.rearrange("(k p) c -> p k c", p=P)).then_inc(
                                sems["prefetched" if s else "prefetched0"], 16)
                        sp.wait_ge(sems["prefetched"], 16)
                    else:
                        for t in range(TB):
                            sp.wait_ge(sems[f"x_out{t}"], 2)
                            sp.dma_start(out[0, t * P:(t + 1) * P, :], xin[:, t, :]).then_inc(sems["stored"], 16)
                        sp.wait_ge(sems["stored"], 16 * TB)

                @block.gpsimd
                def _(pool):
                    stream_lo(pool, st, 0, SU + 1)
                    norm_post_pool(pool, 0)
                    stream_lo(pool, st, SU + 1, len(st.slots))
                    with pool.Fori(0, CH) as c:
                        for j in range(SL):
                            split_lo(pool, j, KT, 512, SL * c + (S0 + j + 1))
                    if even:
                        next_lo(pool, 512)
                    norm_post_pool(pool, 1)

                @block.tensor
                def _(pe):
                    def tiles_of(g, blocks, hi=h_hi, lo=h_lo, ready=None, k0=0):
                        first, tiles = st.groups[g]
                        return group_tiles(pe, g, first, tiles, blocks, hi, lo, half_of(g), k0, ready=ready,
                                           before=before(g))

                    def grp(*args, **kw):
                        for _ in tiles_of(*args, **kw):
                            pass

                    pe.sem_inc(sems["bank_free"], BANKS)
                    if even:
                        stats_pe(pe, 0, 0)
                        grp(0, FEAT, ready=("h_lo_done", 1))
                        pe.wait_ge(sems["bank_free"], BANKS + 1)
                        for k in range(DB):
                            for q, (w, h) in enumerate(((wf_hi, h_hi), (wf_hi, h_lo), (wf_lo, h_hi))):
                                mm = pe.matmul(ps[0:FOX_H, 0, :], w[:, k, :], h[:, k, :], start=k + q == 0,
                                               stop=k == DB - 1 and q == 2)
                        mm.then_inc(sems["f_mm"], 1)
                        grp(1, FEAT)
                        pe.wait_ge(sems["f_in"], 1)
                        grp(2, TOK)
                        pe.wait_ge(sems["bank_free"], BANKS + HALF * 3)
                        pe.wait_ge(sems["consts"], 32)
                        pe.wait_ge(sems["f_done"], 1)
                        pool_tiles = tiles_of(3, FEAT)
                        tiles_a = tiles_of(4, FEAT, hid_hi, hid_lo, k0=KT)
                        tiles_b = tiles_of(5, FEAT, hid_hi, hid_lo, k0=KT)

                        def pooling(i):
                            pool_pace.emit(i, pool_tiles)
                            g = i - PM
                            if 0 <= g < 4:
                                pe.wait_ge(sems["pool_in"], g + 1)
                                pe.matmul(ps[:, 4 + g, :], pw[:, g, :], pooled[:, g, :], start=True,
                                          stop=True).then_inc(sems["pool_mm"], 1)
                            if i == out_a.first:
                                pe.wait_ge(sems["pool_lo"], 4)
                            out_a.emit(i, tiles_a)
                            out_b.emit(i, tiles_b)

                        fox.tensor(pe, 0, pooling)
                        pe.wait_ge(sems["mix_lo"], TB)
                    else:
                        grp(0, FEAT, ready=("h_lo_done", 1))
                        grp(1, FEAT)
                        tiles = chain(tiles_of(2, FEAT), tiles_of(3, FEAT))
                        pe.wait_ge(sems["bank_free"], BANKS + HALF)
                        pe.wait_ge(sems["consts"], 32)
                        for u, (w, b) in enumerate(lru):
                            pe.wait_ge(sems["conv_done"], 2 * (b // 2) + 2)
                            if u >= 4:
                                pe.wait_ge(sems["lru_r"], u - 3)
                            for q in range(2):
                                mm = pe.matmul(ps[:, u % 4, :], (wa, wx)[w][:, 2 * (b // 2) + q, P * (b % 2):P * (b % 2) + P],
                                               xr[:, 2 * (b // 2) + q, :], start=q == 0, stop=q == 1)
                            mm.then_inc(sems["lru_mm"], 1)
                            lru_pace.emit(u, tiles)
                        for _ in tiles:
                            pass
                        pe.wait_ge(sems["lru_r"], len(lru))
                    grp(GM, FEAT, hid_hi, hid_lo, ready=None if even else ("mix_lo", 1))
                    grp(GM + 1, FEAT, hid_hi, hid_lo)
                    pe.wait_ge(sems["bank_free"], BANKS + HALF * (GU - 1))
                    stats_pe(pe, N0, HALF * (GU % 2))
                    pe.wait_ge(sems["rstd_ready"], N0 + 1)
                    stats_pe(pe, N0 + 1, HALF * (GU % 2))
                    grp(GU, FEAT, ready=("h_lo_done", DB + 1))
                    grp(GU + 1, FEAT, hid_hi, hid_lo, ready=("hid_lo_done", 1))
                    grp(GU + 2, FEAT, hid_hi, hid_lo)
                    with pe.Fori(0, CH) as c:
                        for j in range(GC):
                            ring_of[0] = (0, 0, 0, 1)[j]
                            group(pe, GC * c + (G0 + j), SL * c + (S0 + (0, 2, 4, 5)[j]), kv if j < 2 else [KT], FEAT,
                                  *((h_hi, h_lo) if j < 2 else (hid_hi, hid_lo)), (G0 + j) % 2,
                                  ready=("hid_lo_done", 4 * c + 3) if j == 2 else None)
                    pe.wait_ge(sems["bank_free"], BANKS + HALF * (G0 + GC * CH - 1))
                    stats_pe(pe, N0 + 2, HALF * (G0 % 2))
                    pe.wait_ge(sems["rstd_ready"], N0 + 3)
                    if even:
                        stats_pe(pe, N0 + 3, HALF * (G0 % 2))
                    else:
                        for k in range(DB):
                            pe.wait_ge(sems["xup"], DB + k + 1)
                            for t in range(TB):
                                mm = pe.transpose(ps[:, 2 * t + k // 4, (k % 4) * P:(k % 4 + 1) * P],
                                                  x[:, k, t * P:(t + 1) * P], ident)
                            if k % 4 == 3:
                                mm.then_inc(sems["x_T"], 1)

                @block.scalar
                def _(act):
                    stats_bank[0] = 0
                    if even:
                        stats_act(act, xb, 0, 1.0 / D, ready=("xup", 1), between=lambda: stream_hi(act, st, 0))
                    else:
                        stream_hi(act, st, 0)
                    norm_split_act(act, 0, after_first=lambda: stream_hi(act, st, 1))
                    if even:
                        for s in range(2, 4):
                            stream_hi(act, st, s)
                        act.wait_ge(sems["f_in"], 1)
                        alink(act, act.activation(lc[:], lf[:], ACT.Abs))
                        alink(act, act.activation(lc[:], lc[:], ACT.Exp, scale=-1.0))
                        sg["f_c"].by(act.activation(lc[:], lc[:], ACT.Ln, bias=1.0))
                        for s in range(4, 8):
                            stream_hi(act, st, s)

                        def pooling(i):
                            for s, step in ((8, pool_pace.step_of(16)), (9, pool_pace.step_of(32)),
                                            (10, out_a.step_of(16))):
                                if i == step:
                                    stream_hi(act, st, s)
                            g = i - PM
                            if 0 <= g < 4:
                                act.wait_ge(sems["pool_out"], g + 1)
                                sg["pool_hi"].by(act.activation(hid_hi[:, 4 + g, :], ub[g % 2][:, 16:], ACT.Copy))

                        fox.scalar(act, 0, pooling)
                        nxt = 11
                    else:
                        alink(act, act.activation(sp8[:, 0, :], par[:, 7, :], ACT.Abs))
                        alink(act, act.activation(sp8[:, 0, :], sp8[:, 0, :], ACT.Exp, scale=-1.0))
                        sg["f_c"].by(act.activation(sp8[:, 0, :], sp8[:, 0, :], ACT.Ln, bias=1.0))
                        for s in range(2, 6):
                            stream_hi(act, st, s)
                        act.wait_ge(sems["f_done"], 1)

                        def gates(u0, u1):
                            for u in range(u0, u1):
                                w, b = lru[u]
                                act.wait_ge(sems["lru_mm"], u + 1)
                                if w == 1 and b >= 2:
                                    act.wait_ge(sems["xi_done"], b - 1)
                                sg["lru_r"].by(act.activation(i_t[b % 2][:] if w else r8[:, b, :], ps[:, u % 4, :],
                                                              ACT.Sigmoid, bias=par[:, 5 + w, b:b + 1]))
                                for s, t in ((6, 16), (7, 32)):
                                    if lru_pace.step_of(t) == u:
                                        stream_hi(act, st, s)

                        def decay(b0):
                            for b in range(b0, b0 + 4):
                                sg["lru_t"].by(act.activation(t8[b][:], r8[:, b, :], ACT.Tanh, scale=sp8[:, 1, b:b + 1]))
                            act.wait_ge(sems["lru_t"], b0 + 4)
                            for b in range(b0, b0 + 4):
                                alink(act, act.activation(r8[:, b, :], r8[:, b, :], ACT.Exp, scale=sp8[:, 2, b:b + 1]))
                                if b >= 2:
                                    act.wait_ge(sems["lru_b"], b - 1)
                                else:
                                    act.wait_ge(sems["conv_done"], DB)
                                sg["lru_a"].by(act.activation(xp[b % 2][:, 0:S], r8[:, b, :], ACT.Square))

                        def roots(b0):
                            for b in range(b0, b0 + 4):
                                act.wait_ge(sems["lru_b"], b + 1)
                                sg["root_done"].by(act.activation(t8[b][:], t8[b][:], ACT.Sqrt))

                        def gelu(n):
                            act.wait_ge(sems["bank_free"], BANKS + HALF * (3 + n))
                            sg["gelu_done"].by(act.activation(gt[:, 4 * n:4 * n + 4, :], gt[:, 4 * n:4 * n + 4, :],
                                                              ACT.Gelu_apprx_tanh))

                        def mixed(b0):
                            for b in range(b0, b0 + 4):
                                act.wait_ge(sems["y_done"], b + 1)
                                sg["mix_hi"].by(act.activation(hid_hi[:, b, :], tmp[b % 2][:], ACT.Copy))

                        gates(0, 8)
                        act.wait_ge(sems["lru_r"], 8)
                        decay(0)
                        roots(0)
                        gates(8, 16)
                        act.wait_ge(sems["lru_r"], 16)
                        gelu(0)
                        decay(4)
                        stream_hi(act, st, 8)
                        mixed(0)
                        roots(4)
                        stream_hi(act, st, 9)
                        gelu(1)
                        mixed(4)
                        nxt = 10
                    for s in range(nxt, SU + 1):
                        stream_hi(act, st, s)
                    stats_bank[N0] = stats_bank[N0 + 1] = HALF * (GU % 2)
                    stats_act(act, mb, N0, 1.0 / D, ready=("m_done", 1))
                    stats_act(act, xb, N0 + 1, 1.0 / D, ready=("xup", DB * N0 + 1))
                    norm_split_act(act, 1, after_first=lambda: stream_hi(act, st, SU + 1))

                    def hi(c, j):
                        q, jj = divmod(j, SL)
                        cc = c + q
                        used = (("bank_ready", GC * HALF * cc + HALF * (G0 - 1)), ("bank_ready", GC * HALF * cc + HALF * G0),
                                ("slot_used", 2 * cc + (U0 + 1)), ("bank_ready", GC * HALF * cc + HALF * (G0 + 1)),
                                ("slot_used", 2 * cc + (U0 + 2)), ("bank_ready", GC * HALF * cc + HALF * (G0 + 2)))[jj]
                        split_hi(act, jj, KT, 512, 80 * cc + (land0[jj % 2] + (32, 32, 64, 64, 80, 80)[jj]), used)

                    def gated(g, n, ready, free):
                        act.wait_ge(sems["bank_free"], free)
                        for m in range(2):
                            act.wait_ge(sems["bank_ready"], ready + m + 1)
                            act.activation(tmp[m][:], ps[:, HALF * (g % 2) + m, :],
                                           ACT.Silu).then_inc(sems["relu_ready"], 1)
                        for m in range(2):
                            act.wait_ge(sems["v_ready"], n + m + 1)
                            act.activation(hid_hi[:, gated_at[0] + m, :], sq[m][:],
                                           ACT.Copy).then_inc(sems["hid_hi_done"], 1)

                    gated_at = [0]
                    gated(GU, 0, HALF * GU, BANKS + HALF * GU)
                    stream_hi(act, st, S0 - 2)
                    stream_hi(act, st, S0 - 1)
                    hi(0, 0)
                    hi(0, 1)

                    def chunk(c, last):
                        for j in range(2):
                            hi(c, 2 * j + 2)
                            gated_at[0] = 2 * j
                            gated(G0 + j, 4 * c + (2 + 2 * j), GC * HALF * c + HALF * (G0 + j),
                                  GC * HALF * c + (BANKS + HALF * (G0 + j)))
                            hi(c, 2 * j + 3)
                        if not last:
                            hi(c, 6)
                            hi(c, 7)

                    with act.Fori(0, CH - 1) as c:
                        chunk(c, False)
                    chunk(CH - 1, True)
                    stats_bank[N0 + 2] = stats_bank[N0 + 3] = HALF * (G0 % 2)
                    stats_act(act, ab, N0 + 2, 1.0 / D, ready=("bank_free", BANKS + HALF * (G0 + GC * CH - 2) + 1),
                              between=(lambda: next_hi(act, 512)) if even else None)
                    if even:
                        stats_act(act, xb, N0 + 3, 1.0 / D, ready=("xup", DB * (N0 + 1) + 1))
                    else:
                        for n in range(2):
                            act.wait_ge(sems["x_T"], n + 1)
                            for t in (1, 3):
                                act.activation(xin[:, t, 512 * n:512 * n + 512], ps[:, 2 * t + n, :],
                                               ACT.Copy).then_inc(sems[f"x_out{t}"], 1)

                @block.vector
                def _(dve):
                    if even:
                        for k in range(DB):
                            sg["xup"].by(dve.scalar_tensor_tensor(out=x[:, k, :], in0=x[:, k, :], scalar=gain_f[:, k:k + 1],
                                                                  in1=rstd[:], op0=ALU.mult, op1=ALU.mult))
                            if k >= 1:
                                stats_add(dve, 0, k - 1)
                        stats_add(dve, 0, DB - 1)
                        dve.wait_ge(sems["xup"], DB)
                    norm_split_dve(dve, gb(0), 0 if even else None, 0)

                    def evac(g, m, o):
                        dve.wait_ge(sems["bank_ready"], HALF * g + m + 1)
                        sg["bank_free"].by(dve.tensor_copy(o, ps[:, HALF * half_of(g) + m, :]))

                    if even:
                        for i in range(3):
                            link(dve, dve.memset(ub[i][:, 0:16], 0.0))
                        for m in range(4):
                            evac(0, m, fq[:, m, :])
                        dve.wait_ge(sems["f_mm"], 1)
                        sg["f_in"].by(dve.tensor_scalar(lf[:], ps[0:FOX_H, 0, :], bf[:], None, ALU.add))
                        for m in range(4):
                            evac(1, m, fk[:, m, :])
                        dve.wait_ge(sems["f_c"], 1)
                        link(dve, dve.scalar_tensor_tensor(out=lc[:], in0=lf[:], scalar=0.0, in1=lc[:], op0=ALU.min,
                                                           op1=ALU.subtract))
                        link(dve, dve.tensor_tensor_scan(lf[:], tab[0:FOX_H, T_ONES:T_ONES + 1].to_broadcast([FOX_H, S]),
                                                         lc[:], 0.0, ALU.mult, ALU.add))
                        sg["f_done"].by(dve.tensor_scalar(lf[:], lf[:], -1.0 / SCALE, None, ALU.mult))
                        for m in range(4):
                            evac(2, m, fv[:, m, :])

                        def pool_block(m):
                            w = POOL_W[m]
                            evac(3, m, ub[0][:, 16:])
                            dve.wait_ge(sems["bank_free"], sg["bank_free"].n + BANKS)
                            src, step, i = ub[0], 1, 1
                            while step < w:
                                link(dve, dve.tensor_tensor(ub[i][:, 16:], src[:, 16:], src[:, 16 - step:16 + S - step],
                                                            ALU.add))
                                src, step, i = ub[i], 2 * step, 3 - i
                            link(dve, dve.scalar_tensor_tensor(out=pooled[:, m, :], in0=src[:, 16:], scalar=1.0 / w,
                                                               in1=ub[0][:, 16:], op0=ALU.mult, op1=ALU.subtract))
                            link(dve, dve.tensor_tensor(t16[:], src[:, 16:32], tab[:, T_POOL + 16 * m:T_POOL + 16 * m + 16],
                                                        ALU.mult))
                            sg["pool_in"].by(dve.tensor_tensor(pooled[:, m, 0:16], t16[:], ub[0][:, 16:32], ALU.subtract))
                            dve.wait_ge(sems["pool_in"], m + 1)

                        def pooling(i):
                            for m in range(4):
                                if i == pool_pace.step_of(16 + 4 * (m + 1)) + 1:
                                    pool_block(m)
                            g = i - PM
                            if 1 <= g <= 4:
                                dve.wait_ge(sems["pool_hi"], g)
                                sg["pool_lo"].by(dve.tensor_tensor(hid_lo[:, 3 + g, :], ub[(g - 1) % 2][:, 16:],
                                                                   hid_hi[:, 3 + g, :].bitcast(F32), ALU.subtract))
                            if 0 <= g < 4:
                                dve.wait_ge(sems["pool_mm"], g + 1)
                                if g >= 2:
                                    dve.wait_ge(sems["pool_lo"], g - 1)
                                sg["pool_out"].by(dve.tensor_scalar(ub[g % 2][:, 16:], ps[:, 4 + g, :], psc[:, g:g + 1],
                                                                    None, ALU.mult))
                            for m in range(4):
                                if i == out_a.step_of(4 * (m + 1)) + 1:
                                    evac(4, m, macc[:, m, :])
                                if i == out_b.step_of(4 * (m + 1)) + 1:
                                    evac(5, m, macc[:, 4 + m, :])

                        fox.vector(dve, 0, pooling)
                        evac(5, 3, macc[:, 7, :])
                        dve.wait_ge(sems["bank_free"], BANKS + HALF * GM)
                    else:
                        for i in range(2):
                            link(dve, dve.memset(xp[i][:, 0:3], 0.0))
                        dve.wait_ge(sems["f_c"], 1)
                        link(dve, dve.tensor_scalar(sp8[:, 1, :], par[:, 7, :], -1.0, 0.0, ALU.mult, ALU.max))
                        link(dve, dve.tensor_tensor(sp8[:, 0, :], sp8[:, 0, :], sp8[:, 1, :], ALU.add))
                        link(dve, dve.tensor_scalar(sp8[:, 1, :], sp8[:, 0, :], LRU_C, None, ALU.mult))
                        sg["f_done"].by(dve.tensor_scalar(sp8[:, 2, :], sp8[:, 0, :], -LRU_C, None, ALU.mult))
                        for b in range(DB):
                            g, m = b // 4, b % 4
                            q = xp[b % 2]
                            dve.wait_ge(sems["bank_ready"], HALF * g + m + 1)
                            sg["bank_free"].by(dve.tensor_copy(q[:, 3:3 + S], ps[:, HALF * (g % 2) + m, :]))
                            dve.wait_ge(sems["bank_free"], sg["bank_free"].n + BANKS)
                            link(dve, dve.tensor_scalar(xr[:, b, :], q[:, 0:S], par[:, 0, b:b + 1], par[:, 4, b:b + 1],
                                                        ALU.mult, ALU.add))
                            for i in range(1, 4):
                                ins = dve.scalar_tensor_tensor(out=xr[:, b, :], in0=q[:, i:i + S],
                                                               scalar=par[:, i, b:b + 1], in1=xr[:, b, :],
                                                               op0=ALU.mult, op1=ALU.add)
                                if i < 3:
                                    link(dve, ins)
                                else:
                                    sg["conv_done"].by(ins)
                            dve.wait_ge(sems["conv_done"], b + 1)

                        def gated_input(b0):
                            for b in range(b0, b0 + 4):
                                dve.wait_ge(sems["lru_r"], lru.index((1, b)) + 1)
                                dve.wait_ge(sems["lru_mm"], 4 * (b // 2) + 4)
                                sg["xi_done"].by(dve.tensor_tensor(xr[:, b, :], xr[:, b, :], i_t[b % 2][:], ALU.mult))

                        def variance(b0):
                            for b in range(b0, b0 + 4):
                                dve.wait_ge(sems["lru_a"], b + 1)
                                sg["lru_b"].by(dve.scalar_tensor_tensor(out=t8[b][:], in0=xp[b % 2][:, 0:S], scalar=1.0,
                                                                        in1=t8[b][:], op0=ALU.add, op1=ALU.mult))

                        def recur(b0):
                            for b in range(b0, b0 + 4):
                                dve.wait_ge(sems["root_done"], b + 1)
                                link(dve, dve.tensor_tensor(t8[b][:], xr[:, b, :], t8[b][:], ALU.mult))
                                sg["dve_link"].by(dve.tensor_tensor_scan(xr[:, b, :], r8[:, b, :], t8[b][:], 0.0,
                                                                         ALU.mult, ALU.add))
                            dve.wait_ge(sems["dve_link"], sg["dve_link"].n)

                        def mixed(n):
                            dve.wait_ge(sems["gelu_done"], n + 1)
                            for b in range(4 * n, 4 * n + 5):
                                if b < 4 * n + 4:
                                    if b >= 2:
                                        dve.wait_ge(sems["mix_lo"], b - 1)
                                    sg["y_done"].by(dve.tensor_tensor(tmp[b % 2][:], xr[:, b, :], gt[:, b, :], ALU.mult))
                                if b > 4 * n:
                                    dve.wait_ge(sems["mix_hi"], b)
                                    sg["mix_lo"].by(dve.tensor_tensor(hid_lo[:, b - 1, :], tmp[(b - 1) % 2][:],
                                                                      hid_hi[:, b - 1, :].bitcast(F32), ALU.subtract))

                        gated_input(0)
                        variance(0)
                        for m in range(4):
                            evac(2, m, gt[:, m, :])
                        recur(0)
                        gated_input(4)
                        variance(4)
                        mixed(0)
                        recur(4)
                        for m in range(4):
                            evac(3, m, gt[:, 4 + m, :])
                        mixed(1)
                    for b in range(DB):
                        g, m = GM + b // 4, b % 4
                        dve.wait_ge(sems["bank_ready"], HALF * g + m + 1)
                        if even:
                            sg["m_done"].by(dve.tensor_tensor(macc[:, b, :], macc[:, b, :], ps[:, HALF * half_of(g) + m, :],
                                                              ALU.add))
                        else:
                            sg["m_done"].by(dve.tensor_copy(acc[:, b, :], ps[:, HALF * half_of(g) + m, :]))
                        if b >= 1:
                            stats_add(dve, N0, b - 1)
                        if m == 3:
                            dve.wait_ge(sems["m_done"], b + 1)
                            dve.sem_inc(sems["bank_free"], HALF)
                    stats_add(dve, N0, DB - 1)
                    norm_post(dve, mb, gb(1), N0, 0, n_next=N0 + 1, x0=DB * N0)
                    dve.wait_ge(sems["xup"], DB * (N0 + 1))
                    norm_split_dve(dve, gb(2), N0 + 1, 1)
                    dve.wait_ge(sems["h_lo_done"], 2 * DB)

                    def gated(g, n, at_block, ready):
                        for m in range(2):
                            dve.wait_ge(sems["relu_ready"], n + m + 1)
                            dve.wait_ge(sems["bank_ready"], ready + m + 3)
                            dve.tensor_tensor(sq[m][:], ps[:, HALF * (g % 2) + 2 + m, :], tmp[m][:],
                                              ALU.mult).then_inc(sems["v_ready"], 1)
                        dve.wait_ge(sems["v_ready"], n + 2)
                        dve.sem_inc(sems["bank_free"], HALF)
                        for m in range(2):
                            dve.wait_ge(sems["hid_hi_done"], n + m + 1)
                            dve.tensor_tensor(hid_lo[:, at_block + m, :], sq[m][:], hid_hi[:, at_block + m, :].bitcast(F32),
                                              ALU.subtract).then_inc(sems["hid_lo_done"], 1)
                        dve.wait_ge(sems["hid_lo_done"], n + 2)

                    gated(GU, 0, 0, HALF * GU)
                    for b in range(DB):
                        g, m = GU + 1 + b // 4, b % 4
                        dve.wait_ge(sems["bank_ready"], HALF * g + m + 1)
                        dve.tensor_copy(acc[:, b, :], ps[:, HALF * (g % 2) + m, :]).then_inc(sems["bank_free"], 1)

                    def chunk(c, last):
                        for j in range(2):
                            gated(G0 + j, 4 * c + (2 + 2 * j), 2 * j, GC * HALF * c + HALF * (G0 + j))
                        for b in range(DB):
                            j, m = 2 + b // 4, b % 4
                            dve.wait_ge(sems["bank_ready"], GC * HALF * c + (HALF * (G0 + j) + m + 1))
                            dve.tensor_tensor(acc[:, b, :], acc[:, b, :], ps[:, HALF * ((G0 + j) % 2) + m, :],
                                              ALU.add).then_inc(sems["bank_free"], 1)
                            if last and b >= 1:
                                stats_add(dve, N0 + 2, b - 1)

                    with dve.Fori(0, CH - 1) as c:
                        chunk(c, False)
                    chunk(CH - 1, True)
                    stats_add(dve, N0 + 2, DB - 1)
                    norm_post(dve, ab, gb(3), N0 + 2, 1, n_next=N0 + 3 if even else None, x0=DB * N0)
                    if not even:
                        for n in range(2):
                            dve.wait_ge(sems["x_T"], n + 1)
                            for t in (0, 2):
                                dve.tensor_copy(xin[:, t, 512 * n:512 * n + 512], ps[:, 2 * t + n, :]).then_inc(
                                    sems[f"x_out{t}"], 1)

        second_layer(0)
        clear()
        second_layer(1)


def kernel(**inputs):
    import concourse.bacc as bacc
    from concourse.bass_utils import run_bass_kernel_spmd

    nc = bacc.Bacc("TRN2", target_bir_lowering=False, num_devices=1)
    arrays, args = {}, {}
    tab, rtab, sel = shape_tables()
    for name, v in dict(inputs, tab=tab, rtab=rtab, sel=sel).items():
        v = np.ascontiguousarray(v)
        arrays[f"in_{name}"] = v
        args[name] = nc.dram_tensor(f"in_{name}", v.shape, mybir.dt.from_np(v.dtype), kind="ExternalInput").ap()
    out = nc.dram_tensor("out", (1, S, D), F32, kind="ExternalOutput").ap()
    build(nc, args, out)
    r = run_bass_kernel_spmd(nc, [arrays], core_ids=[0])
    return r.results[0]["out"]
```
